# Optimizing a Trainium2 kernel written in Bass

```python
import math
import jax
import jax.numpy as jnp
from jax import lax
import numpy as np

D_MODEL = 1024
BATCH = 1
SEQ = 256
DEPTH = 2

ATT_HEAD_DIM = D_MODEL // 16
FOX_HEADS = 4
MLSTM_HEADS = 4
MLSTM_HEAD_DIM = D_MODEL // 8
MOBA_HEADS = 4
FOX_W = FOX_HEADS * ATT_HEAD_DIM
MLSTM_W = MLSTM_HEADS * MLSTM_HEAD_DIM
MOBA_W = MOBA_HEADS * ATT_HEAD_DIM
MIX_W = FOX_W + MLSTM_W + MOBA_W
IN_SPLITS = [FOX_W, FOX_W, FOX_W, FOX_HEADS,
             MLSTM_W, MLSTM_W, MLSTM_W, MLSTM_HEADS, MLSTM_HEADS, MLSTM_W,
             MOBA_W, MOBA_W, MOBA_W]
IN_W = sum(IN_SPLITS)

ROPE_DIM = ATT_HEAD_DIM // 4
ROPE_THETA = 500000.0
Q_BLOCK = 128
MLSTM_CHUNK = 128
CONV_WIDTH = 4
MOBA_BLOCK = 256
MOBA_TOPK = 3

N_GROUPS = 4
EXPERTS_PER_GROUP = 8
N_EXPERTS = N_GROUPS * EXPERTS_PER_GROUP
EXPERT_TOPK = 2
D_EXPERT = 512
MOE_BLOCK = 128

ALPHA = (2 * DEPTH) ** 0.25
BETA = (8 * DEPTH) ** -0.25
EPS = 1e-5

kernel_name = 'hymba_fox_mlstm_moba_hmoe_deepnorm'

def layer_norm(x, g, b):
    xf = x.astype(jnp.float32)
    mu = jnp.mean(xf, -1, keepdims=True)
    var = jnp.mean(jnp.square(xf - mu), -1, keepdims=True)
    return ((xf - mu) * lax.rsqrt(var + EPS) * g + b).astype(x.dtype)

def headwise_rms(u, g, n_heads):
    B, S, W = u.shape
    uf = u.astype(jnp.float32).reshape(B, S, n_heads, W // n_heads)
    uf = uf * lax.rsqrt(jnp.mean(jnp.square(uf), -1, keepdims=True) + EPS)
    return (uf.reshape(B, S, W) * g).astype(u.dtype)

def partial_rope(u, positions):
    half = ROPE_DIM // 2
    inv = 1.0 / (ROPE_THETA ** (jnp.arange(0, ROPE_DIM, 2, dtype=jnp.float32) / ROPE_DIM))
    ang = positions.astype(jnp.float32)[..., None] * inv
    cos = jnp.cos(ang)[:, :, None, :]
    sin = jnp.sin(ang)[:, :, None, :]
    ur = u[..., :ROPE_DIM].astype(jnp.float32)
    u1, u2 = ur[..., :half], ur[..., half:]
    rot = jnp.concatenate([u1 * cos - u2 * sin, u1 * sin + u2 * cos], -1)
    return jnp.concatenate([rot.astype(u.dtype), u[..., ROPE_DIM:]], -1)

def causal_conv(u, w):
    C = u.shape[-1]
    return lax.conv_general_dilated(
        u, w[:, None, :].astype(u.dtype), window_strides=(1,),
        padding=[(CONV_WIDTH - 1, 0)], dimension_numbers=('NWC', 'WIO', 'NWC'),
        feature_group_count=C)

def fox_attention(q, k, v, log_f):
    B, S, H, D = q.shape
    qh = q.transpose(0, 2, 1, 3) * (D ** -0.5)
    kh = k.transpose(0, 2, 1, 3)
    vh = v.transpose(0, 2, 1, 3)
    cum = jnp.cumsum(log_f, axis=1).transpose(0, 2, 1)
    kpos = jnp.arange(S)

    def block(i):
        start = i * Q_BLOCK
        qb = lax.dynamic_slice_in_dim(qh, start, Q_BLOCK, axis=2)
        cb = lax.dynamic_slice_in_dim(cum, start, Q_BLOCK, axis=2)
        s = jnp.einsum('bhqd,bhkd->bhqk', qb, kh).astype(jnp.float32)
        s = s + cb[..., :, None] - cum[..., None, :]
        qpos = start + jnp.arange(Q_BLOCK)
        s = jnp.where(kpos[None, :] <= qpos[:, None], s, -jnp.inf)
        p = jax.nn.softmax(s, axis=-1)
        return jnp.einsum('bhqk,bhkd->bhqd', p.astype(vh.dtype), vh)

    out = lax.map(block, jnp.arange(S // Q_BLOCK))
    return out.transpose(1, 0, 3, 2, 4).reshape(B, S, H * D)

def mlstm(q, k, v, i_pre, f_pre):
    B, S, H, D = q.shape
    L = MLSTM_CHUNK
    NC = S // L
    to_chunks = lambda u: u.astype(jnp.float32).reshape(B, NC, L, H, D).transpose(1, 0, 3, 2, 4)
    gate_chunks = lambda g: g.reshape(B, NC, L, H).transpose(1, 0, 3, 2)
    qc, kc, vc = to_chunks(q), to_chunks(k) * (D ** -0.5), to_chunks(v)
    li = gate_chunks(i_pre)
    lf = gate_chunks(jax.nn.log_sigmoid(f_pre))
    tril = jnp.tril(jnp.ones((L, L), dtype=bool))

    def step(carry, inp):
        C, n, m = carry
        qt, kt, vt, it, ft = inp
        b = jnp.cumsum(ft, axis=-1)
        dmat = jnp.where(tril, b[..., :, None] - b[..., None, :] + it[..., None, :], -jnp.inf)
        inter = b + m[..., None]
        m_t = jnp.maximum(inter, jnp.max(dmat, -1))
        w_intra = jnp.exp(dmat - m_t[..., None])
        w_inter = jnp.exp(inter - m_t)
        a = jnp.einsum('bhtd,bhsd->bhts', qt, kt) * w_intra
        num = jnp.einsum('bhts,bhsd->bhtd', a, vt) + w_inter[..., None] * jnp.einsum('bhtd,bhde->bhte', qt, C)
        den = jnp.sum(a, -1) + w_inter * jnp.einsum('bhtd,bhd->bht', qt, n)
        h = num / jnp.maximum(jnp.abs(den), jnp.exp(-m_t))[..., None]
        b_last = b[..., -1]
        g = b_last[..., None] - b + it
        m_new = jnp.maximum(b_last + m, jnp.max(g, -1))
        decay = jnp.exp(b_last + m - m_new)
        ws = jnp.exp(g - m_new[..., None])
        C_new = decay[..., None, None] * C + jnp.einsum('bhs,bhsd,bhse->bhde', ws, kt, vt)
        n_new = decay[..., None] * n + jnp.einsum('bhs,bhsd->bhd', ws, kt)
        return (C_new, n_new, m_new), h

    init = (jnp.zeros((B, H, D, D), jnp.float32), jnp.zeros((B, H, D), jnp.float32),
            jnp.zeros((B, H), jnp.float32))
    _, hs = lax.scan(step, init, (qc, kc, vc, li, lf))
    return hs.transpose(1, 0, 3, 2, 4).reshape(B, S, H * D).astype(q.dtype)

def moba_attention(q, k, v):
    B, S, H, D = q.shape
    BS = MOBA_BLOCK
    NB = -(-S // BS)
    K_SEL = max(1, min(MOBA_TOPK, NB - 1))
    pad = NB * BS - S
    qh = q.transpose(0, 2, 1, 3) * (D ** -0.5)
    kh = jnp.pad(k.transpose(0, 2, 1, 3), ((0, 0), (0, 0), (0, pad), (0, 0)))
    vh = jnp.pad(v.transpose(0, 2, 1, 3), ((0, 0), (0, 0), (0, pad), (0, 0)))
    kb = kh.reshape(B, H, NB, BS, D)
    vb = vh.reshape(B, H, NB, BS, D)
    kmean = jnp.mean(kb, axis=3)
    bi = jnp.arange(B)[:, None, None, None]
    hi = jnp.arange(H)[None, :, None, None]

    def block(i):
        start = i * Q_BLOCK
        qb = lax.dynamic_slice_in_dim(qh, start, Q_BLOCK, axis=2)
        qpos = start + jnp.arange(Q_BLOCK)
        own = start // BS
        gate = jnp.einsum('bhqd,bhnd->bhqn', qb, kmean).astype(jnp.float32)
        gate = jnp.where(jnp.arange(NB) < own, gate, -jnp.inf)
        _, gidx = lax.top_k(gate, K_SEL)
        valid = jnp.arange(K_SEL) < own
        kg = kb[bi, hi, gidx]
        vg = vb[bi, hi, gidx]
        s_sel = jnp.einsum('bhqd,bhqnjd->bhqnj', qb, kg).astype(jnp.float32)
        s_sel = jnp.where(valid[:, None], s_sel, -jnp.inf)
        k_own = lax.dynamic_index_in_dim(kb, own, axis=2, keepdims=False)
        v_own = lax.dynamic_index_in_dim(vb, own, axis=2, keepdims=False)
        s_own = jnp.einsum('bhqd,bhjd->bhqj', qb, k_own).astype(jnp.float32)
        kpos = own * BS + jnp.arange(BS)
        s_own = jnp.where(kpos[None, :] <= qpos[:, None], s_own, -jnp.inf)
        s = jnp.concatenate([s_sel.reshape(B, H, Q_BLOCK, K_SEL * BS), s_own], -1)
        p = jax.nn.softmax(s, axis=-1).astype(vb.dtype)
        out = jnp.einsum('bhqj,bhqjd->bhqd', p[..., :K_SEL * BS],
                         vg.reshape(B, H, Q_BLOCK, K_SEL * BS, D))
        return out + jnp.einsum('bhqj,bhjd->bhqd', p[..., K_SEL * BS:], v_own)

    out = lax.map(block, jnp.arange(S // Q_BLOCK))
    return out.transpose(1, 0, 3, 2, 4).reshape(B, S, H * D)

def token_mixer(x, positions, w_in, b_fox_f, b_mlstm_i, b_mlstm_f, conv_w,
                g_fox, g_mlstm, g_moba, w_out):
    B, S, _ = x.shape
    z = jnp.einsum('bsd,dn->bsn', x, w_in)
    (fq, fk, fv, ff, mq, mk, mv, mi, mf, mo, bq, bk, bv) = jnp.split(
        z, np.cumsum(IN_SPLITS)[:-1].tolist(), axis=-1)
    heads = lambda u, h: u.reshape(B, S, h, -1)
    log_f = jax.nn.log_sigmoid(ff.astype(jnp.float32) + b_fox_f)
    y_fox = fox_attention(heads(fq, FOX_HEADS), heads(fk, FOX_HEADS), heads(fv, FOX_HEADS), log_f)
    qk = jax.nn.silu(causal_conv(jnp.concatenate([mq, mk], -1), conv_w))
    mq, mk = jnp.split(qk, 2, axis=-1)
    h = mlstm(heads(mq, MLSTM_HEADS), heads(mk, MLSTM_HEADS), heads(mv, MLSTM_HEADS),
              mi.astype(jnp.float32) + b_mlstm_i, mf.astype(jnp.float32) + b_mlstm_f)
    y_mlstm = jax.nn.sigmoid(mo) * h
    y_moba = moba_attention(partial_rope(heads(bq, MOBA_HEADS), positions),
                            partial_rope(heads(bk, MOBA_HEADS), positions),
                            heads(bv, MOBA_HEADS))
    y = jnp.concatenate([headwise_rms(y_fox, g_fox, FOX_HEADS),
                         headwise_rms(y_mlstm, g_mlstm, MLSTM_HEADS),
                         headwise_rms(y_moba, g_moba, MOBA_HEADS)], -1)
    return jnp.einsum('bsm,md->bsd', y, w_out)

def expert_ffn(xb, wg, wu, wd):
    return (jax.nn.silu(xb @ wg) * (xb @ wu)) @ wd

def hier_moe(x, w_grp, b_grp, w_exp_router, b_exp_router, w_gate, w_up, w_down):
    B, S, D = x.shape
    T = B * S
    h = x.reshape(T, D)
    grp_logits = (h @ w_grp).astype(jnp.float32) + b_grp
    g_sel = jnp.argmax(grp_logits, -1)
    p_grp = jnp.take_along_axis(jax.nn.softmax(grp_logits, -1), g_sel[:, None], 1)[:, 0]
    e_logits = jnp.einsum('td,dge->tge', h, w_exp_router).astype(jnp.float32) + b_exp_router
    e_logits = jnp.take_along_axis(e_logits, g_sel[:, None, None], 1)[:, 0]
    top_v, top_i = lax.top_k(e_logits, EXPERT_TOPK)
    gates = jax.nn.softmax(top_v, -1) * p_grp[:, None]
    expert_id = g_sel[:, None] * EXPERTS_PER_GROUP + top_i
    A = T * EXPERT_TOPK
    e_flat = expert_id.reshape(A).astype(jnp.int32)
    tok_flat = jnp.repeat(jnp.arange(T, dtype=jnp.int32), EXPERT_TOPK)
    w_flat = gates.reshape(A)
    order = jnp.argsort(e_flat)
    e_s, tok_s, w_s = e_flat[order], tok_flat[order], w_flat[order]
    counts = jnp.bincount(e_flat, length=N_EXPERTS)
    starts = jnp.cumsum(counts) - counts
    padded = ((counts + MOE_BLOCK - 1) // MOE_BLOCK) * MOE_BLOCK
    pends = jnp.cumsum(padded)
    pstarts = pends - padded
    dest = pstarts[e_s] + (jnp.arange(A, dtype=jnp.int32) - starts[e_s])
    P = A + N_EXPERTS * MOE_BLOCK
    NBLK = P // MOE_BLOCK
    buf = jnp.zeros((P, D), h.dtype).at[dest].set(h[tok_s])
    blk_e = jnp.minimum(jnp.searchsorted(pends, jnp.arange(NBLK) * MOE_BLOCK, side='right'),
                        N_EXPERTS - 1)
    ybuf = lax.map(lambda a: expert_ffn(a[0], w_gate[a[1]], w_up[a[1]], w_down[a[1]]),
                   (buf.reshape(NBLK, MOE_BLOCK, D), blk_e)).reshape(P, D)
    y_assign = (ybuf[dest] * w_s[:, None]).astype(h.dtype)
    y = jax.ops.segment_sum(y_assign, tok_s, num_segments=T)
    return y.reshape(B, S, D)

def setup_inputs(seed: int = 0) -> dict:
    key = jax.random.key(seed)
    ks = jax.random.split(key, 24)
    nrm = lambda k, shape, scale: jax.random.normal(k, shape, jnp.float32) * scale
    L, D = DEPTH, D_MODEL
    return {
        'x': nrm(ks[0], (BATCH, SEQ, D), 1.0),
        'positions': jnp.broadcast_to(jnp.arange(SEQ, dtype=jnp.int32)[None, :], (BATCH, SEQ)),
        'w_in': nrm(ks[1], (L, D, IN_W), D ** -0.5),
        'b_fox_f': 1.0 + nrm(ks[2], (L, FOX_HEADS), 0.1),
        'b_mlstm_i': nrm(ks[3], (L, MLSTM_HEADS), 0.1),
        'b_mlstm_f': 3.0 + nrm(ks[4], (L, MLSTM_HEADS), 0.5),
        'conv_w': nrm(ks[5], (L, CONV_WIDTH, 2 * MLSTM_W), CONV_WIDTH ** -0.5),
        'g_fox': 1.0 + nrm(ks[6], (L, FOX_W), 0.1),
        'g_mlstm': 1.0 + nrm(ks[7], (L, MLSTM_W), 0.1),
        'g_moba': 1.0 + nrm(ks[8], (L, MOBA_W), 0.1),
        'w_out': nrm(ks[9], (L, MIX_W, D), MIX_W ** -0.5 * BETA),
        'ln1_g': 1.0 + nrm(ks[10], (L, D), 0.1),
        'ln1_b': nrm(ks[11], (L, D), 0.02),
        'w_grp': nrm(ks[12], (L, D, N_GROUPS), D ** -0.5),
        'b_grp': nrm(ks[13], (L, N_GROUPS), 0.01),
        'w_exp_router': nrm(ks[14], (L, D, N_GROUPS, EXPERTS_PER_GROUP), D ** -0.5),
        'b_exp_router': nrm(ks[15], (L, N_GROUPS, EXPERTS_PER_GROUP), 0.01),
        'w_gate': nrm(ks[16], (L, N_EXPERTS, D, D_EXPERT), D ** -0.5),
        'w_up': nrm(ks[17], (L, N_EXPERTS, D, D_EXPERT), D ** -0.5),
        'w_down': nrm(ks[18], (L, N_EXPERTS, D_EXPERT, D), D_EXPERT ** -0.5 * BETA),
        'ln2_g': 1.0 + nrm(ks[19], (L, D), 0.1),
        'ln2_b': nrm(ks[20], (L, D), 0.02),
    }

def reference(x, positions, w_in, b_fox_f, b_mlstm_i, b_mlstm_f, conv_w, g_fox, g_mlstm,
              g_moba, w_out, ln1_g, ln1_b, w_grp, b_grp, w_exp_router, b_exp_router,
              w_gate, w_up, w_down, ln2_g, ln2_b):
    for l in range(DEPTH):
        mix = token_mixer(x, positions, w_in[l], b_fox_f[l], b_mlstm_i[l], b_mlstm_f[l],
                          conv_w[l], g_fox[l], g_mlstm[l], g_moba[l], w_out[l])
        x = layer_norm(ALPHA * x + mix, ln1_g[l], ln1_b[l])
        ffn = hier_moe(x, w_grp[l], b_grp[l], w_exp_router[l], b_exp_router[l],
                       w_gate[l], w_up[l], w_down[l])
        x = layer_norm(ALPHA * x + ffn, ln2_g[l], ln2_b[l])
    return x


_drawn_inputs = setup_inputs


def setup_inputs(seed=0):
    import zlib

    import numpy as np

    out = dict(_drawn_inputs(seed))
    spreads = {}
    factors = {'b_fox_f': 3.953, 'b_mlstm_i': 64.0, 'b_grp': 39.542, 'b_exp_router': 15.067}
    for name, (base, spread) in spreads.items():
        noise = np.random.default_rng([zlib.crc32(name.encode()), seed]).standard_normal(out[name].shape)
        drawn = base * np.exp(spread * noise) if base else spread * noise
        out[name] = jnp.asarray(drawn.astype(out[name].dtype))
    for name, factor in factors.items():
        out[name] = (out[name] * factor).astype(out[name].dtype)
    return out
```

```python
from contextlib import ExitStack
import math

import concourse.bass as bass
from concourse import mybir

ALU = mybir.AluOpType
ACT = mybir.ActivationFunctionType
F32 = mybir.dt.float32
BF16 = mybir.dt.bfloat16
I32 = mybir.dt.int32
AXX = mybir.AxisListType.X

P = 128
SEQ, D, DEPTH = 256, 1024, 2
TT = SEQ // P
KT = D // P
FH, FD = 4, 64
MH, MD = 4, 128
CONV = 4
ROPE_HALF = 8
NG, EG, NE, DE = 4, 8, 32, 512
FT = DE // P
SLOTS = 64
EXTRA = 8
ALPHA = (2 * DEPTH) ** 0.25
EPS = 1e-5
BIG = 1e30
CH = 512
NCHUNK = 10
HEADS = 2 * FH + MH
SLOT_OF = [6, 7, 0, 1, 2, 3, 4, 5, 6, 7]
COLS = [[(0, 512)], [(512, 772), (2308, 2316)], [(772, 1284)], [(1284, 1796)], [(1796, 2308)],
        [(2316, 2828)], [(2828, 3340)], [(3340, 3596)]]
DVE_READ = [1, 2, 3, 4, 5, 5, 6, 7]
ACT_READ = [1, 2, 2, 2, 3, 4, 5, 6]
PAR_DMAS = 11


class Steps:

    def __init__(self, eng, sem, base):
        self.eng, self.sem, self.base, self.n = eng, sem, base, 0

    def __call__(self, ins):
        self.n += 1
        ins.then_inc(self.sem, 1)
        self.eng.wait_ge(self.sem, self.base + self.n)


def kind(j):
    return "fox" if j < FH else "mlstm" if j < FH + MH else "moba"


def width(j):
    return MD if kind(j) == "mlstm" else FD


def column(j):
    if kind(j) == "fox":
        return j * FD
    if kind(j) == "mlstm":
        return FH * FD + (j - FH) * MD
    return FH * FD + MH * MD + (j - FH - MH) * FD


def soft_up_to(j):
    return sum(kind(i) != "mlstm" for i in range(j + 1))


def mlstm_up_to(j):
    return sum(kind(i) == "mlstm" for i in range(j + 1))


SOFT, MLS = soft_up_to(HEADS - 1), mlstm_up_to(HEADS - 1)
DVE_LAYER_STEPS = 93
DVE_PAIR_STEPS = 4
ACT_LAYER_STEPS = 1
POOL_LAYER_STEPS = 2


def build(nc, A, out):
    ctx = ExitStack()
    with ctx:
        def sb(name, shape, dt=F32):
            return ctx.enter_context(nc.sbuf_tensor(name, shape, dt))

        def sem(name):
            return ctx.enter_context(nc.semaphore(name))

        ring = sb("ring", [P, 8, KT * CH])
        x = sb("xres", [P, TT, D])
        bufa = sb("bufa", [P, 2048])
        bufb = sb("bufb", [P, 2048])
        bufc = sb("bufc", [P, 2048])
        bufd = sb("bufd", [P, 1024])
        bufe = sb("bufe", [P, 1024])
        lnp = sb("lnp", [P, 2, D])
        qf = sb("qf", [P, FH, SEQ])
        kf = sb("kf", [P, FH // 2, SEQ])
        qb = sb("qb", [P, FH, SEQ])
        kb = sb("kb", [P, FH // 2, SEQ])
        Pm = sb("Pm", [P, 2, 3 * P])
        Wm = sb("Wm", [P, 3 * P])
        catT = sb("catT", [P, SEQ])
        gpad = sb("gpad", [P, TT, P])
        ident = sb("ident", [P, P])
        identb = sb("identb", [P, P], BF16)
        maskb = sb("maskb", [P, P], BF16)
        tri_incl = sb("tri_incl", [P, P])
        tri_strict = sb("tri_strict", [P, P])
        ones = sb("ones", [P, P])
        zerob = sb("zerob", [P, P], BF16)
        iota_f = sb("iota_f", [P, P])
        desc = sb("desc", [P, NE])
        base_e = sb("base_e", [P, NE])
        tri65 = sb("tri65", [NE, 2 * NE + 1])
        iot8 = sb("iot8", [1, EXTRA * NE])
        pcol_i = sb("pcol_i", [P, 1], I32)
        pcol = sb("pcol", [P, 1])
        ones_c = sb("ones_c", [P, 1])
        pos_i = sb("pos_i", [P, TT], I32)
        pos_f = sb("pos_f", [P, TT])
        inv = sb("inv", [P, ROPE_HALF])
        ang = sb("ang", [P, TT, ROPE_HALF])
        kk = sb("kk", [P, TT, ROPE_HALF])
        ang_s = sb("ang_s", [P, TT, ROPE_HALF])
        ang_c = sb("ang_c", [P, TT, ROPE_HALF])
        cos = sb("cos", [P, TT, ROPE_HALF])
        sin = sb("sin", [P, TT, ROPE_HALF])
        cwr = sb("cwr", [CONV * 8, P])
        cw = sb("cw", [P, CONV * 8])
        bias12 = sb("bias12", [P, 12])
        rb36 = sb("rb36", [P, 36])
        gcol = sb("gcol", [P, KT])
        wr4 = sb("wr4", [P, KT, NG])
        wr32 = sb("wr32", [P, KT, NE])
        z12 = sb("z12", [P, TT, 12])
        az = sb("az", [P, TT, 8])
        mn = sb("mn", [P, TT, 8])
        ls = sb("ls", [P, TT, 8])
        bcum = sb("bcum", [P, TT, 4])
        nmx = sb("nmx", [P, 4, 2])
        stat = sb("stat", [P, 4, 2])
        rinv = sb("rinv", [P, 4, 2])
        em = sb("em", [P, 4, 2])
        mhalf = sb("mhalf", [P, HEADS])
        ms = sb("ms", [P, TT, HEADS])
        bns = sb("bns", [P, TT, 2, 6])
        mv = sb("mv", [P, TT, 2])
        rstd = sb("rstd", [P, TT])
        nmr = sb("nmr", [P, TT])
        lg = sb("lg", [P, TT, 36])
        r1 = sb("r1", [P, TT, 1])
        g4 = sb("g4", [P, TT, NG])
        e4 = sb("e4", [P, TT, NG])
        d4 = sb("d4", [P, TT, NG])
        s4 = sb("s4", [P, TT, 1])
        gmx = sb("gmx", [P, TT, 1])
        v12 = sb("v12", [P, 2, TT, 1])
        emk = sb("emk", [P, TT, NE])
        eq = sb("eq", [P, TT, NE])
        oh = sb("oh", [P, 2, TT, NE])
        mall = sb("mall", [P, TT, NE])
        dd = sb("dd", [P, TT, 1])
        ex = sb("ex", [P, TT, 1])
        wgt = sb("wgt", [P, 2, TT, 1])
        dst = sb("dst", [P, 2, TT, 1])
        novt = sb("novt", [NE, P])
        starts = sb("starts", [P, 2 * NE + 1])
        delta = sb("delta", [P, NE])
        dall = sb("dall", [P, TT, NE])
        dcur = sb("dcur", [P, 2, TT, 1])
        pcur = sb("pcur", [P, 1])
        tabf = sb("tabf", [1, 48])
        tabx = sb("tabx", [1, 4])
        tabi = sb("tabi", [1, 48], I32)
        total = sb("total", [1, 1])

        xT = bufa[:, :].rearrange("p (k t) -> p k t", k=KT)
        y = bufa[:, :].rearrange("p (t n) -> p t n", t=TT)
        v = bufb[:, :].rearrange("p (t n) -> p t n", t=TT)
        yT = bufb[:, :].rearrange("p (k t) -> p k t", k=KT)
        drow = bufb[:, 0:512].rearrange("p (k t) -> p k t", k=2)
        wrow = bufb[:, 512:1024].rearrange("p (k t) -> p k t", k=2)
        sil = bufb[:, 1024:1536]
        hid = bufb[:, 1536:2048]
        qkm = bufc[:, :].rearrange("p (c t) -> p c t", c=8)
        sq = bufc[:, :].rearrange("p (t n) -> p t n", t=TT)
        xg = bufc[:, 0:1024].rearrange("p (k s) -> p k s", k=KT)
        ym = bufc[:, 1024:2048]
        sg = bufd[:, :].rearrange("p (t n) -> p t n", t=TT)
        hT = bufd[:, 0:512].rearrange("p (k s) -> p k s", k=FT)
        oneh = bufd[:, 512:768].rearrange("p (t s) -> p t s", t=TT)
        wt = bufd[:, 768:1024]
        bqk = bufe[:, :].rearrange("p (t n) -> p t n", t=TT)
        PT = bufe[:, 0:768].rearrange("p (b n) -> p b n", b=2)
        rt = Pm[:, :, :].rearrange("p b n -> p (b n)")[:, 0:8 * 64].rearrange("p (i t h d) -> p i t h d", i=4, t=TT, h=8)
        cmp8 = Wm[0:1, 0:EXTRA * NE].rearrange("p (b e) -> p b e", b=EXTRA)
        iota_i = bufc[:, 0:P].bitcast(I32)
        desc_i = bufc[:, P:P + NE].bitcast(I32)
        iot8_i = bufc[0:1, 512:512 + EXTRA * NE].bitcast(I32)
        w2 = Pm[:, 0, 0:SEQ]

        ps = [ctx.enter_context(nc.psum_tensor(f"ps{i}", [P, 512], F32)) for i in range(8)]

        x_in, pos_in = sem("x_in"), sem("pos_in")
        chunk_in = [sem(f"chunk_in{c}") for c in range(NCHUNK)]
        gate_in, up_in, down_in = sem("gate_in"), sem("up_in"), sem("down_in")
        par_issued = sem("par_issued")
        par_in, ln_in = sem("par_in"), sem("ln_in")
        consts_ready = sem("consts_ready")
        dve_consts = sem("dve_consts")
        angles = sem("angles")
        trig = sem("trig")
        dve_step, act_step, pool_step = sem("dve_step"), sem("act_step"), sem("pool_step")
        dve_pair = sem("dve_pair")
        dve_setup = sem("dve_setup")
        pool_setup = sem("pool_setup")
        tr_bank = sem("tr_bank")
        tr_dve, tr_act = sem("tr_dve"), sem("tr_act")
        proj = sem("proj")
        read_dve, read_act = sem("read_dve"), sem("read_act")
        cw_tr, cw_ready = sem("cw_tr"), sem("cw_ready")
        az_ready, ln_ready, ls_ready = sem("az_ready"), sem("ln_ready"), sem("ls_ready")
        cum_done, gpad_ready, cat_tr, cat_ready = sem("cum_done"), sem("gpad_ready"), sem("cat_tr"), sem("cat_ready")
        silu_done, kscaled = sem("silu_done"), sem("kscaled")
        roped, rope_tr, qb_ready, kb_ready = sem("roped"), sem("rope_tr"), sem("qb_ready"), sem("kb_ready")
        scored, maxed = sem("scored"), sem("maxed")
        exp_done, wexp_done, prod_done = sem("exp_done"), sem("wexp_done"), sem("prod_done")
        p_tr, pt_ready, pv_done, o_read = sem("p_tr"), sem("pt_ready"), sem("pv_done"), sem("o_read")
        y_gated, squared, y_ready = sem("y_gated"), sem("squared"), sem("y_ready")
        var_ready, rstd_ready = sem("var_ready"), sem("rstd_ready")
        stats_ready, normed, scaled, x_done = sem("stats_ready"), sem("normed"), sem("scaled"), sem("x_done")
        logits, gdiff, gexp, vdiff, vexp = sem("logits"), sem("gdiff"), sem("gexp"), sem("vdiff"), sem("vexp")
        masks_ready, ranks, novt_ready, starts_ps = sem("masks_ready"), sem("ranks"), sem("novt_ready"), sem("starts_ps")
        dst_ready, rows_ps, rows_dve, rows_act = sem("dst_ready"), sem("rows_ps"), sem("rows_dve"), sem("rows_act")
        table_ready = sem("table_ready")
        oneh_ready, gathered, xg_dve, xg_act = sem("oneh_ready"), sem("gathered"), sem("xg_dve"), sem("xg_act")
        gate_used, up_used, down_used = sem("gate_used"), sem("up_used"), sem("down_used")
        combined, silued, h_ready, h_tr, hT_ready = sem("combined"), sem("silued"), sem("h_ready"), sem("h_tr"), sem("hT_ready")
        wt_ready, y_dve, y_act = sem("wt_ready"), sem("y_dve"), sem("y_act")
        acc_done = sem("acc_done")
        out_sem = sem("out_sem")
        dve_held, act_held, pe_held, pool_held = sem("dve_held"), sem("act_held"), sem("pe_held"), sem("pool_held")

        block = ctx.enter_context(nc.Block())

        def bc(ap, shape):
            return ap.to_broadcast(shape)

        def slot(s, n=CH):
            return ring[:, s, 0:KT * n].rearrange("p (k n) -> p k n", k=KT)

        @block.sync
        def _(sp):
            with nc.allow_non_contiguous_dma(reason="256 positions"):
                sp.dma_start(pos_i[:, :], A["positions"][0].rearrange("(t p) -> p t", p=P)).then_inc(pos_in, 16)
            sp.dma_start(x[:, :, :], A["x"][0].rearrange("(t p) d -> p t d", p=P)).then_inc(x_in, 16)

            def load_chunk(l, c):
                s = slot(SLOT_OF[c])
                if c >= 8:
                    src = A["w_out"][l].rearrange("(p k) n -> p k n", k=KT)[:, :, (c - 8) * CH:(c - 7) * CH]
                    sp.dma_start(s[:, :, :], src).then_inc(chunk_in[c], 16)
                    return
                at = 0
                for a, b in COLS[c]:
                    src = A["w_in"][l].rearrange("(p k) n -> p k n", k=KT)[:, :, a:b]
                    sp.dma_start(s[:, :, at:at + b - a], src).then_inc(chunk_in[c], 16)
                    at += b - a

            def load_pair(l, part, e):
                w, first, arrived = {"gate": ("w_gate", 0, gate_in), "up": ("w_up", 2, up_in),
                                     "down": ("w_down", 4, down_in)}[part]
                for q in range(2):
                    src = A[w][l].rearrange("e (p k) n -> e p (k n)", p=P)[bass.ds(e[q], 1)] if not isinstance(e[q], int) \
                        else A[w][l].rearrange("e (p k) n -> e p (k n)", p=P)[e[q]:e[q] + 1]
                    sp.dma_start(ring[:, first + q, :], src.rearrange("a p n -> (a p) n")).then_inc(arrived, 16)

            load_chunk(0, 0)
            sp.wait_ge(par_issued, 1)
            load_chunk(0, 1)
            done = 0
            for l in range(DEPTH):
                for c in range(2, 8):
                    if l > 0:
                        sp.wait_ge((gate_used, up_used, down_used)[SLOT_OF[c] // 2], done)
                    load_chunk(l, c)
                for c in (8, 9):
                    sp.wait_ge(proj, NCHUNK * l + c - 7)
                    load_chunk(l, c)
                for i, part in enumerate(("gate", "up", "down")):
                    sp.wait_ge(proj, NCHUNK * l + 2 * i + 4)
                    load_pair(l, part, (0, 1))
                if l + 1 < DEPTH:
                    for c in (0, 1):
                        sp.wait_ge(proj, NCHUNK * l + 9 + c)
                        load_chunk(l + 1, c)
                sp.wait_ge(table_ready, l + 1)
                pairs = sp.value_load(tabi[0:1, 40:41], min_val=NE // 2, max_val=(NE + EXTRA) // 2)
                with sp.Fori(1, pairs) as i:
                    e = [sp.value_load(tabi[0:1, bass.ds(2 * i + q, 1)], min_val=0, max_val=NE - 1) for q in range(2)]
                    for part, used in (("gate", gate_used), ("up", up_used), ("down", down_used)):
                        sp.wait_ge(used, done + i)
                        load_pair(l, part, e)
                done = sp.snap(done + pairs)
            for tt in range(TT):
                sp.wait_ge(x_done, 4 * DEPTH + tt)
                sp.dma_start(out[0].rearrange("(t p) d -> t p d", p=P)[tt], x[:, tt, :]).then_inc(out_sem, 16)
            sp.wait_ge(out_sem, 16 * TT)

        @block.gpsimd
        def _(pool):
            st = Steps(pool, pool_setup, 0)
            g = nc.gpsimd
            g.memset(ident[:, :], 0.0)
            g.memset(tri_incl[:, :], 1.0)
            g.memset(tri_strict[:, :], 1.0)
            g.memset(ones[:, :], 1.0)
            g.memset(ones_c[:, :], 1.0)
            g.memset(maskb[:, :], 0.0)
            g.memset(zerob[:, :], 0.0)
            g.memset(tri65[:, :], 1.0)
            g.memset(qf[:, :, :], 0.0)
            g.memset(qb[:, :, :], 0.0)
            g.memset(gpad[:, :, :], 0.0)
            g.memset(total[:, :], 0.0)
            for j in range(ROPE_HALF):
                g.memset(inv[:, j:j + 1], 500000.0 ** (-j / ROPE_HALF))
            for j in range(4):
                g.memset(tabx[:, j:j + 1], 2.0 * j)
            g.iota(iota_i[:, :], pattern=[[1, P]], base=0, channel_multiplier=0)
            g.iota(desc_i[:, :], pattern=[[-1, NE]], base=NE, channel_multiplier=0)
            g.iota(iot8_i[:, :], pattern=[[1, EXTRA], [0, NE]], base=0, channel_multiplier=0)
            st(g.iota(pcol_i[:, :], pattern=[[0, 1]], base=0, channel_multiplier=1))
            g.tensor_copy(iota_f[:, :], iota_i[:, :])
            g.tensor_copy(desc[:, :], desc_i[:, :])
            g.tensor_copy(iot8[:, :], iot8_i[:, :])
            g.tensor_copy(pcol[:, :], pcol_i[:, :])
            g.affine_select(out=ident[:, :], in_=ident[:, :], compare_op=ALU.not_equal, fill=1.0,
                            base=0, pattern=[[-1, P]], channel_multiplier=1)
            g.affine_select(out=tri_incl[:, :], in_=tri_incl[:, :], compare_op=ALU.is_ge, fill=0.0,
                            base=0, pattern=[[1, P]], channel_multiplier=-1)
            g.affine_select(out=tri_strict[:, :], in_=tri_strict[:, :], compare_op=ALU.is_gt, fill=0.0,
                            base=0, pattern=[[1, P]], channel_multiplier=-1)
            g.affine_select(out=maskb[:, :], in_=maskb[:, :], compare_op=ALU.is_ge, fill=-BIG,
                            base=0, pattern=[[-1, P]], channel_multiplier=1)
            g.affine_select(out=tri65[:, 0:NE], in_=tri65[:, 0:NE], compare_op=ALU.is_gt, fill=0.0,
                            base=0, pattern=[[1, NE]], channel_multiplier=-1)
            st(g.affine_select(out=tri65[:, NE:2 * NE], in_=tri65[:, NE:2 * NE], compare_op=ALU.is_ge, fill=0.0,
                               base=0, pattern=[[1, NE]], channel_multiplier=-1))
            g.tensor_copy(identb[:, :], ident[:, :]).then_inc(consts_ready, 1)
            g.memset(mhalf[:, :], -0.5).then_inc(x_done, 1)
            pool.wait_ge(trig, 2)
            with pool.Fori(0, DEPTH) as l:
                st = Steps(pool, pool_step, l * POOL_LAYER_STEPS)
                pool.wait_ge(silu_done, 2 * l + 2)
                pool.sem_inc(pool_held, 1)
                g.tensor_scalar(qkm[:, MH:2 * MH, :], qkm[:, MH:2 * MH, :], float(MD) ** -0.5, None, ALU.mult).then_inc(kscaled, 1)
                pool.wait_ge(read_dve, 7 * l + DVE_READ[6])
                pool.wait_ge(read_act, 6 * l + ACT_READ[6])
                for tt in range(TT):
                    u = bqk[:, tt, :].rearrange("p (h d) -> p h d", d=FD)
                    u1, u2 = u[:, :, 0:ROPE_HALF], u[:, :, ROPE_HALF:2 * ROPE_HALF]
                    c = bc(cos[:, tt:tt + 1, :], [P, 8, ROPE_HALF])
                    s = bc(sin[:, tt:tt + 1, :], [P, 8, ROPE_HALF])
                    g.tensor_tensor(rt[:, 0, tt], u1, c, ALU.mult)
                    g.tensor_tensor(rt[:, 1, tt], u2, s, ALU.mult)
                    g.tensor_tensor(rt[:, 2, tt], u1, s, ALU.mult)
                    st(g.tensor_tensor(rt[:, 3, tt], u2, c, ALU.mult))
                    g.tensor_tensor(u1, rt[:, 0, tt], rt[:, 1, tt], ALU.subtract)
                    g.tensor_tensor(u2, rt[:, 2, tt], rt[:, 3, tt], ALU.add).then_inc(roped, 1)
                pool.wait_ge(o_read, HEADS * l + FH + MH)
                ym_ = y[:, :, FH * FD:FH * FD + MH * MD]
                g.tensor_tensor(ym_, ym_, sg[:, :, :], ALU.mult).then_inc(y_gated, 1)

                def powers(n, of, to):
                    pool.wait_ge(var_ready, 6 * l + n + 1)
                    g.tensor_tensor(to, of, mhalf[:, 0:of.shape[1]], ALU.pow).then_inc(rstd_ready, 1)

                for tt in range(TT):
                    powers(tt, ms[:, tt, :], ms[:, tt, :])
                for q in range(2):
                    for tt in range(TT):
                        powers(2 + 2 * q + tt, mv[:, tt, 1:2], rstd[:, tt:tt + 1])
                    for tt in range(TT):
                        pool.wait_ge(scaled, 4 * l + 2 * q + tt + 1)
                        g.tensor_tensor(x[:, tt, :], x[:, tt, :], lnp[:, 1, :], ALU.add).then_inc(x_done, 1)
                assert st.n == POOL_LAYER_STEPS, st.n

        @block.scalar
        def _(act):
            a = nc.scalar

            def evac_tr(n, dest):
                for b in (1, 3):
                    act.wait_ge(tr_bank, n + b + 1)
                    a.activation(dest[:, 2 * b:2 * b + 2, :].rearrange("p k t -> p (k t)"), ps[4 + b][:, :],
                                 ACT.Copy).then_inc(tr_act, 1)

            act.wait_ge(angles, 1)
            a.activation(sin[:, :, :], ang_s[:, :, :], ACT.Sin).then_inc(trig, 1)
            a.activation(cos[:, :, :], ang_c[:, :, :], ACT.Sin).then_inc(trig, 1)
            with act.Fori(0, DEPTH) as l:
                st = Steps(act, act_step, l * ACT_LAYER_STEPS)

                act.wait_ge(x_done, 4 * l + 1)
                with nc.allow_non_contiguous_dma(reason="small parameters"):
                    act.dma_start(cwr[:, :], A["conv_w"][bass.ds(l, 1)].rearrange("a j (c p) -> (a j c) p", p=P)).then_inc(par_in, 16)
                    for i, n in enumerate(("b_fox_f", "b_mlstm_i", "b_mlstm_f")):
                        act.dma_start(bias12[:, 4 * i:4 * i + 4], A[n][bass.ds(l, 1)].to_broadcast([P, 4])).then_inc(par_in, 16)
                    for n, lo, hi in (("g_fox", 0, 32), ("g_mlstm", 32, 96), ("g_moba", 96, 128)):
                        act.dma_start(gcol[lo:hi, :], A[n][bass.ds(l, 1)].rearrange("a (p k) -> (a p) k", k=KT)).then_inc(par_in, 16)
                    act.dma_start(wr4[:, :, :], A["w_grp"][bass.ds(l, 1)].rearrange("a (p k) g -> (a p) k g", k=KT)).then_inc(par_in, 16)
                    act.dma_start(wr32[:, :, :], A["w_exp_router"][bass.ds(l, 1)].rearrange("a (p k) g e -> (a p) k (g e)", k=KT)).then_inc(par_in, 16)
                    act.dma_start(rb36[:, 0:NG], A["b_grp"][bass.ds(l, 1)].to_broadcast([P, NG])).then_inc(par_in, 16)
                    act.dma_start(rb36[:, NG:36], A["b_exp_router"][bass.ds(l, 1)].rearrange("a g e -> a (g e)").to_broadcast([P, NE])).then_inc(par_in, 16)
                    act.dma_start(lnp[:, 0, :], A["ln1_g"][bass.ds(l, 1)].to_broadcast([P, D])).then_inc(ln_in, 16)
                    act.dma_start(lnp[:, 1, :], A["ln1_b"][bass.ds(l, 1)].to_broadcast([P, D])).then_inc(ln_in, 16)

                act.sem_inc(par_issued, 1)
                evac_tr(12 * l, xT)

                def chunk(c):
                    act.wait_ge(proj, NCHUNK * l + c + 1)

                chunk(0)
                a.activation(kf[:, :, :].rearrange("p c t -> p (c t)"), ps[1][:, :], ACT.Copy).then_inc(read_act, 1)
                chunk(1)
                a.activation(v[:, 1, 0:256], ps[3][:, 0:256], ACT.Copy)
                a.activation(z12[:, 1, :], ps[3][:, 256:268], ACT.Copy).then_inc(read_act, 1)
                act.wait_ge(az_ready, l + 1)
                st(a.activation(ls[:, :, :], az[:, :, :], ACT.Exp))
                a.activation(az[:, :, :], ls[:, :, :], ACT.Ln, bias=1.0).then_inc(ln_ready, 1)
                for q in range(2):
                    act.wait_ge(read_dve, 7 * l + q + 3)
                    u = qkm[:, 4 * q:4 * q + 4, :]
                    a.activation(u, u, ACT.Silu).then_inc(silu_done, 1)
                chunk(4)
                a.activation(v[:, 1, 256:768], ps[1][:, :], ACT.Copy).then_inc(read_act, 1)
                chunk(5)
                a.activation(sg[:, 0, :], ps[2][:, :], ACT.Sigmoid)
                a.activation(sg[:, 1, :], ps[3][:, :], ACT.Sigmoid).then_inc(read_act, 1)
                chunk(6)
                a.activation(bqk[:, 1, :], ps[1][:, :], ACT.Copy).then_inc(read_act, 1)
                chunk(7)
                a.activation(v[:, 1, 768:1024], ps[3][:, 0:256], ACT.Copy).then_inc(read_act, 1)
                act.wait_ge(rope_tr, 2 * l + 2)
                a.activation(kb[:, :, :].rearrange("p c t -> p (c t)"), ps[5][:, :], ACT.Copy).then_inc(kb_ready, 1)

                for it in range(HEADS + 1):
                    if it < HEADS:
                        j = it
                        act.wait_ge(maxed, HEADS * l + j + 1)
                        b = j % 2
                        if kind(j) == "mlstm":
                            m = mlstm_up_to(j)
                            if m > 1:
                                act.wait_ge(prod_done, MLS * l + m - 1)
                            a.activation(Wm[:, 0:P], ps[2 + b][:, 0:P], ACT.Exp, bias=nmx[:, j % 4, 0:1])
                            a.activation(em[:, j % 4, :], em[:, j % 4, :], ACT.Exp)
                            a.activation(Wm[:, P:3 * P], ps[2 + b][:, P:3 * P], ACT.Exp, bias=nmx[:, j % 4, 1:2]).then_inc(wexp_done, 1)
                        else:
                            if j >= 2:
                                act.wait_ge(p_tr, HEADS * l + j - 1)
                            if j >= 4:
                                act.wait_ge(o_read, HEADS * l + j - 3)
                            a.activation(Pm[:, b, 0:P], ps[b][:, 0:P], ACT.Exp, bias=nmx[:, j % 4, 0:1],
                                         accum_out=stat[:, j % 4, 0:1])
                            a.activation(Pm[:, b, P:3 * P], ps[b][:, P:3 * P], ACT.Exp, bias=nmx[:, j % 4, 1:2],
                                         accum_out=stat[:, j % 4, 1:2]).then_inc(exp_done, 1)
                    if it >= 1:
                        j = it - 1
                        act.wait_ge(p_tr, HEADS * l + j + 1)
                        if j >= 2:
                            act.wait_ge(pv_done, HEADS * l + j - 1)
                        a.activation(PT[:, j % 2, :], ps[4 + j % 2][:, 0:3 * P], ACT.Copy).then_inc(pt_ready, 1)

                act.wait_ge(o_read, HEADS * (l + 1))
                act.wait_ge(y_gated, l + 1)
                act.wait_ge(kscaled, l + 1)
                for tt in range(TT):
                    a.activation(sq[:, tt, :], y[:, tt, :], ACT.Square).then_inc(squared, 1)
                for b in (1, 3):
                    act.wait_ge(tr_bank, 4 + 12 * l + b + 1)
                    a.activation(yT[:, 2 * b, :], ps[4 + b][:, 0:SEQ], ACT.Copy, scale=gcol[:, 2 * b:2 * b + 1])
                    a.activation(yT[:, 2 * b + 1, :], ps[4 + b][:, SEQ:2 * SEQ], ACT.Copy,
                                 scale=gcol[:, 2 * b + 1:2 * b + 2]).then_inc(tr_act, 1)

                def normalise(q):
                    for tt in range(TT):
                        act.wait_ge(stats_ready, 4 * l + 2 * q + tt + 1)
                        a.activation(x[:, tt, :], x[:, tt, :], ACT.Identity, bias=nmr[:, tt:tt + 1],
                                     scale=rstd[:, tt:tt + 1]).then_inc(normed, 1)

                normalise(0)
                act.wait_ge(x_done, 4 * l + 3)
                act.dma_start(lnp[:, 0, :], A["ln2_g"][bass.ds(l, 1)].to_broadcast([P, D])).then_inc(ln_in, 16)
                act.dma_start(lnp[:, 1, :], A["ln2_b"][bass.ds(l, 1)].to_broadcast([P, D])).then_inc(ln_in, 16)
                evac_tr(8 + 12 * l, xT)
                act.wait_ge(gdiff, l + 1)
                a.activation(e4[:, :, :], d4[:, :, :], ACT.Exp).then_inc(gexp, 1)
                act.wait_ge(vdiff, l + 1)
                a.activation(ex[:, :, :], dd[:, :, :], ACT.Exp).then_inc(vexp, 1)
                act.wait_ge(rows_ps, 2 * l + 2)
                a.activation(wrow.rearrange("p k t -> p (k t)"), ps[3][:, :], ACT.Copy).then_inc(rows_act, 1)

                act.wait_ge(table_ready, l + 1)
                act.sem_inc(act_held, 1)
                pairs = act.value_load(tabi[0:1, 40:41], min_val=NE // 2, max_val=(NE + EXTRA) // 2)
                done = act.value_load(tabi[0:1, 41:42], min_val=0, max_val=DEPTH * (NE + EXTRA) // 2)
                act.wait_ge(gathered, 2 * (done + l) + 2)
                a.activation(xg[:, 4:8, :].rearrange("p k s -> p (k s)"), ps[7][:, :], ACT.Copy).then_inc(xg_act, 1)
                with act.Fori(0, pairs) as i:
                    n = act.snap(done + i)
                    act.wait_ge(gate_used, n + 1)
                    a.activation(sil, ps[4][:, :], ACT.Silu).then_inc(silued, 1)
                    act.wait_ge(gathered, 2 * (n + l) + 4)
                    a.activation(xg[:, 4:8, :].rearrange("p k s -> p (k s)"), ps[7][:, :], ACT.Copy).then_inc(xg_act, 1)
                    act.wait_ge(down_used, n + 1)
                    a.activation(ym[:, CH:2 * CH], ps[7][:, :], ACT.Copy).then_inc(y_act, 1)
                normalise(1)
                assert st.n == ACT_LAYER_STEPS, st.n

        @block.vector
        def _(dve):
            d = nc.vector
            st = Steps(dve, dve_setup, 0)
            dve.wait_ge(pos_in, 16)
            dve.wait_ge(consts_ready, 1)
            d.tensor_scalar(base_e[:, :], iota_f[:, 0:NE], float(SLOTS), None, ALU.mult)
            st(d.tensor_copy(pos_f[:, :], pos_i[:, :]))
            st(d.tensor_tensor(ang[:, :, :], bc(pos_f[:, :].unsqueeze(2), [P, TT, ROPE_HALF]),
                               bc(inv[:, :].unsqueeze(1), [P, TT, ROPE_HALF]), ALU.mult))
            magic = 1.5 * 2.0 ** 23
            c1 = 6.28125
            c2 = float(int((2 * math.pi - c1) * 2 ** 20)) / 2 ** 20
            c3 = 2 * math.pi - c1 - c2
            st(d.tensor_scalar(kk[:, :, :], ang[:, :, :], 1 / (2 * math.pi), None, ALU.mult))
            st(d.tensor_scalar(kk[:, :, :], kk[:, :, :], magic, None, ALU.add))
            st(d.tensor_scalar(kk[:, :, :], kk[:, :, :], magic, None, ALU.subtract))
            for c in (c1, c2, c3):
                st(d.scalar_tensor_tensor(ang[:, :, :], kk[:, :, :], -c, ang[:, :, :], ALU.mult, ALU.add))
            pi = 3.1415925
            d.tensor_scalar(ang_s[:, :, :], ang[:, :, :], pi, -pi, ALU.min, ALU.max)
            st(d.tensor_scalar(ang_c[:, :, :], ang[:, :, :], math.pi / 2, None, ALU.add))
            st(d.tensor_scalar(kk[:, :, :], ang_c[:, :, :], math.pi, -2 * math.pi, ALU.is_gt, ALU.mult))
            st(d.tensor_tensor(ang_c[:, :, :], ang_c[:, :, :], kk[:, :, :], ALU.add))
            d.tensor_scalar(ang_c[:, :, :], ang_c[:, :, :], pi, -pi, ALU.min, ALU.max).then_inc(angles, 1)

            def evac_tr(n, dest):
                for b in (0, 2):
                    dve.wait_ge(tr_bank, n + b + 1)
                    d.tensor_copy(dest[:, 2 * b:2 * b + 2, :].rearrange("p k t -> p (k t)"), ps[4 + b][:, :]).then_inc(tr_dve, 1)

            with dve.Fori(0, DEPTH) as l:
                st = Steps(dve, dve_step, l * DVE_LAYER_STEPS)
                evac_tr(12 * l, xT)

                def chunk(c):
                    dve.wait_ge(proj, NCHUNK * l + c + 1)

                chunk(0)
                u = ps[0][:, :].rearrange("p (c t) -> p c t", c=2)
                d.tensor_scalar(qf[0:64, 0:FH:2, :], u[0:64], FD ** -0.5, None, ALU.mult)
                d.tensor_scalar(qf[64:128, 1:FH:2, :], u[64:128], FD ** -0.5, None, ALU.mult).then_inc(read_dve, 1)
                chunk(1)
                d.tensor_copy(v[:, 0, 0:256], ps[2][:, 0:256])
                d.tensor_copy(z12[:, 0, :], ps[2][:, 256:268]).then_inc(read_dve, 1)
                dve.wait_ge(read_dve, 7 * l + 2)
                dve.wait_ge(read_act, 6 * l + 2)
                dve.wait_ge(par_in, 16 * PAR_DMAS * (l + 1))
                st(d.tensor_tensor(z12[:, :, :], z12[:, :, :], bc(bias12[:, :].unsqueeze(1), [P, TT, 12]), ALU.add))
                for h, c in ((0, 0), (4, 8)):
                    d.tensor_scalar(mn[:, :, h:h + 4], z12[:, :, c:c + 4], 0.0, None, ALU.min)
                    last = d.tensor_scalar(az[:, :, h:h + 4], z12[:, :, c:c + 4], 0.0, None, ALU.max)
                st(last)
                d.tensor_tensor(az[:, :, :], mn[:, :, :], az[:, :, :], ALU.subtract).then_inc(az_ready, 1)
                dve.wait_ge(cw_tr, l + 1)
                d.tensor_copy(cw[:, :], ps[7][:, 384:384 + CONV * 8]).then_inc(cw_ready, 1)
                dve.wait_ge(cw_ready, l + 1)
                dve.wait_ge(ln_ready, l + 1)
                d.tensor_tensor(ls[:, :, :], mn[:, :, :], az[:, :, :], ALU.subtract).then_inc(ls_ready, 1)

                def conv(q):
                    chunk(2 + q)
                    for j in range(CONV - 1, -1, -1):
                        back = CONV - 1 - j
                        for c in range(MH):
                            u = ps[2 * q + c // 2][:, (c % 2) * SEQ:(c % 2 + 1) * SEQ]
                            w = cw[:, j * 8 + 4 * q + c:j * 8 + 4 * q + c + 1]
                            o = qkm[:, 4 * q + c, :]
                            if back == 0:
                                last = d.tensor_scalar(o, u, w, None, ALU.mult)
                            else:
                                last = d.scalar_tensor_tensor(o[:, back:], u[:, 0:SEQ - back], w, o[:, back:],
                                                              ALU.mult, ALU.add)
                        if j:
                            st(last)
                    last.then_inc(read_dve, 1)

                conv(0)
                dve.wait_ge(cum_done, l + 1)
                u = ps[7][:, 0:TT * 8].rearrange("p (t g) -> p t g", t=TT)
                d.tensor_scalar(gpad[:, :, 0:4], u[:, :, 0:4], -1.0, None, ALU.mult)
                d.tensor_copy(bcum[:, :, :], u[:, :, 4:8])
                d.tensor_tensor(gpad[:, :, 4:8], z12[:, :, 4:8], u[:, :, 4:8], ALU.subtract).then_inc(gpad_ready, 1)
                conv(1)
                dve.wait_ge(cat_tr, l + 1)
                d.tensor_copy(catT[:, :], ps[7][:, 0:SEQ]).then_inc(cat_ready, 1)
                chunk(4)
                d.tensor_copy(v[:, 0, 256:768], ps[0][:, :]).then_inc(read_dve, 1)
                chunk(6)
                d.tensor_copy(bqk[:, 0, :], ps[0][:, :]).then_inc(read_dve, 1)
                chunk(7)
                d.tensor_copy(v[:, 0, 768:1024], ps[2][:, 0:256]).then_inc(read_dve, 1)
                dve.wait_ge(rope_tr, 2 * l + 1)
                u = ps[4][:, :].rearrange("p (c t) -> p c t", c=2)
                d.tensor_scalar(qb[0:64, 0:FH:2, :], u[0:64], FD ** -0.5, None, ALU.mult)
                d.tensor_scalar(qb[64:128, 1:FH:2, :], u[64:128], FD ** -0.5, None, ALU.mult).then_inc(qb_ready, 1)

                for it in range(HEADS + 2):
                    if it < HEADS:
                        j, b = it, it % 2
                        dve.wait_ge(scored, HEADS * l + j + 1)
                        s = ps[(2 if kind(j) == "mlstm" else 0) + b]
                        d.tensor_reduce(nmx[:, j % 4, 0:1], s[:, 0:P], AXX, ALU.max, negate=True)
                        last = d.tensor_reduce(nmx[:, j % 4, 1:2], s[:, P:3 * P], AXX, ALU.max, negate=True)
                        if kind(j) != "mlstm":
                            last.then_inc(maxed, 1)
                        else:
                            st(last)
                            st(d.tensor_scalar(nmx[:, j % 4, :], nmx[:, j % 4, :], 0.0, None, ALU.min))
                            d.tensor_tensor(em[:, j % 4, :], nmx[:, j % 4, :], bcum[:, :, j - FH], ALU.subtract).then_inc(maxed, 1)
                            dve.wait_ge(wexp_done, MLS * l + mlstm_up_to(j))
                            dve.wait_ge(p_tr, HEADS * l + j - 1)
                            d.scalar_tensor_tensor(Pm[:, b, 0:P], ps[b][:, 0:P], 1.0, Wm[:, 0:P], ALU.mult, ALU.mult,
                                                   accum_out=stat[:, j % 4, 0:1])
                            d.scalar_tensor_tensor(Pm[:, b, P:3 * P], ps[b][:, P:3 * P], 1.0, Wm[:, P:3 * P], ALU.mult,
                                                   ALU.mult, accum_out=stat[:, j % 4, 1:2]).then_inc(prod_done, 1)
                    if it >= 2:
                        j, b = it - 2, it % 2
                        if kind(j) == "mlstm":
                            dve.wait_ge(prod_done, MLS * l + mlstm_up_to(j))
                            st(d.scalar_tensor_tensor(rinv[:, j % 4, :], stat[:, j % 4, :], -1.0, stat[:, j % 4, :], ALU.mult, ALU.max))
                            st(d.tensor_tensor(rinv[:, j % 4, :], rinv[:, j % 4, :], em[:, j % 4, :], ALU.max))
                            st(d.reciprocal(rinv[:, j % 4, :], rinv[:, j % 4, :]))
                        else:
                            dve.wait_ge(exp_done, SOFT * l + soft_up_to(j))
                            st(d.reciprocal(rinv[:, j % 4, :], stat[:, j % 4, :]))
                        dve.wait_ge(pv_done, HEADS * l + j + 1)
                        w, c = width(j), column(j)
                        for tt in range(TT):
                            last = d.tensor_scalar(y[:, tt, c:c + w], ps[6 + b][:, tt * w:(tt + 1) * w],
                                                   rinv[:, j % 4, tt:tt + 1], None, ALU.mult)
                        last.then_inc(o_read, 1)

                lo, mi, hi = FH * FD, FH * FD + MH * MD, D
                groups = ((0, lo, FD, 0), (lo, mi, MD, FH), (mi, hi, FD, FH + MH))
                for tt in range(TT):
                    dve.wait_ge(squared, 2 * l + tt + 1)
                    for a0, a1, w, h0 in groups:
                        last = d.tensor_reduce(ms[:, tt, h0:h0 + 4], sq[:, tt, a0:a1].rearrange("p (h w) -> p h w", w=w), AXX, ALU.add)
                    st(last)
                    for a0, a1, w, h0 in groups:
                        last = d.tensor_scalar(ms[:, tt, h0:h0 + 4], ms[:, tt, h0:h0 + 4], 1.0 / w, EPS, ALU.mult, ALU.add)
                    last.then_inc(var_ready, 1)
                for tt in range(TT):
                    dve.wait_ge(rstd_ready, 6 * l + tt + 1)
                    for a0, a1, w, h0 in groups:
                        u = y[:, tt, a0:a1].rearrange("p (h w) -> p h w", w=w)
                        last = d.tensor_tensor(u, u, bc(ms[:, tt, h0:h0 + 4].unsqueeze(2), [P, 4, w]), ALU.mult)
                    last.then_inc(y_ready, 1)
                for b in (0, 2):
                    dve.wait_ge(tr_bank, 4 + 12 * l + b + 1)
                    d.tensor_scalar(yT[:, 2 * b, :], ps[4 + b][:, 0:SEQ], gcol[:, 2 * b:2 * b + 1], None, ALU.mult)
                    d.tensor_scalar(yT[:, 2 * b + 1, :], ps[4 + b][:, SEQ:2 * SEQ], gcol[:, 2 * b + 1:2 * b + 2],
                                    None, ALU.mult).then_inc(tr_dve, 1)

                def layer_norm(q, ready):
                    for tt in range(TT):
                        for half in range(2):
                            ready(tt, half)
                            u = x[:, tt, half * CH:(half + 1) * CH]
                            bank = 2 * half + tt
                            last = d.scalar_tensor_tensor(u, u, ALPHA, ps[bank][:, :], ALU.mult, ALU.add)
                        st(last)
                        for half in range(2):
                            last = d.bn_stats(bns[:, tt, half, :], x[:, tt, half * CH:(half + 1) * CH])
                        st(last)
                        dve.sem_inc(dve_held, 1)
                        st(d.bn_aggr(mv[:, tt, :], bns[:, tt, :, :].rearrange("p a b -> p (a b)")))
                        d.tensor_scalar(mv[:, tt, 1:2], mv[:, tt, 1:2], EPS, None, ALU.add).then_inc(var_ready, 1)
                        dve.wait_ge(rstd_ready, 6 * l + 2 * q + tt + 3)
                        d.scalar_tensor_tensor(nmr[:, tt:tt + 1], mv[:, tt, 0:1], -1.0, rstd[:, tt:tt + 1],
                                               ALU.mult, ALU.mult).then_inc(stats_ready, 1)
                    for tt in range(TT):
                        dve.wait_ge(normed, 4 * l + 2 * q + tt + 1)
                        if tt == 0:
                            dve.wait_ge(ln_in, 64 * l + 32 * q + 32)
                        d.tensor_tensor(x[:, tt, :], x[:, tt, :], lnp[:, 0, :], ALU.mult).then_inc(scaled, 1)

                layer_norm(0, lambda tt, half: dve.wait_ge(proj, NCHUNK * l + 9 + half))
                evac_tr(8 + 12 * l, xT)

                dve.wait_ge(logits, l + 1)
                st(d.tensor_tensor(lg[:, :, :], ps[0][:, 0:128].rearrange("p (t n) -> p t n", t=TT)[:, :, 0:36],
                                   bc(rb36[:, :].unsqueeze(1), [P, TT, 36]), ALU.add))
                st(d.tensor_reduce(gmx[:, :, :], lg[:, :, 0:NG], AXX, ALU.max))
                d.tensor_tensor(d4[:, :, :], lg[:, :, 0:NG], bc(gmx[:, :, :], [P, TT, NG]), ALU.subtract).then_inc(gdiff, 1)
                st(d.tensor_tensor(g4[:, :, :], lg[:, :, 0:NG], bc(gmx[:, :, :], [P, TT, NG]), ALU.is_equal))
                st(d.tensor_tensor(g4[:, :, :], g4[:, :, :], bc(desc[:, 0:NG].unsqueeze(1), [P, TT, NG]), ALU.mult))
                st(d.tensor_reduce(r1[:, :, :], g4[:, :, :], AXX, ALU.max))
                st(d.tensor_tensor(g4[:, :, :], g4[:, :, :], bc(r1[:, :, :], [P, TT, NG]), ALU.is_equal))
                st(d.tensor_scalar(g4[:, :, :], g4[:, :, :], -1.0, BIG, ALU.add, ALU.mult))
                for tt in range(TT):
                    last = d.tensor_tensor(emk[:, tt, :].rearrange("p (g e) -> p g e", g=NG),
                                           lg[:, tt, NG:36].rearrange("p (g e) -> p g e", g=NG),
                                           bc(g4[:, tt, :].unsqueeze(2), [P, NG, EG]), ALU.add)
                st(last)
                for k in range(2):
                    st(d.tensor_reduce(v12[:, k], emk[:, :, :], AXX, ALU.max))
                    st(d.tensor_tensor(eq[:, :, :], emk[:, :, :], bc(v12[:, k], [P, TT, NE]), ALU.is_equal))
                    st(d.tensor_tensor(eq[:, :, :], eq[:, :, :], bc(desc[:, :].unsqueeze(1), [P, TT, NE]), ALU.mult))
                    st(d.tensor_reduce(r1[:, :, :], eq[:, :, :], AXX, ALU.max))
                    st(d.tensor_tensor(oh[:, k], bc(desc[:, :].unsqueeze(1), [P, TT, NE]), bc(r1[:, :, :], [P, TT, NE]), ALU.is_equal))
                    if k == 0:
                        st(d.scalar_tensor_tensor(emk[:, :, :], oh[:, 0], -3 * BIG, emk[:, :, :], ALU.mult, ALU.add))
                d.tensor_tensor(mall[:, :, :], oh[:, 0], oh[:, 1], ALU.add).then_inc(masks_ready, 1)
                d.tensor_tensor(dd[:, :, :], v12[:, 1], v12[:, 0], ALU.subtract).then_inc(vdiff, 1)
                dve.wait_ge(gexp, l + 1)
                st(d.tensor_reduce(s4[:, :, :], e4[:, :, :], AXX, ALU.add))
                dve.wait_ge(vexp, l + 1)
                st(d.tensor_scalar(r1[:, :, :], ex[:, :, :], 1.0, None, ALU.add))
                st(d.tensor_tensor(s4[:, :, :], s4[:, :, :], r1[:, :, :], ALU.mult))
                st(d.reciprocal(wgt[:, 0], s4[:, :, :]))
                d.tensor_tensor(wgt[:, 1], wgt[:, 0], ex[:, :, :], ALU.mult)
                dve.wait_ge(ranks, l + 1)
                cnt = ps[1][0:NE, 128:256]
                st(d.tensor_scalar(novt[:, :], cnt, float(SLOTS), None, ALU.is_gt))
                st(d.scalar_tensor_tensor(novt[:, :], cnt, 2.0 * SLOTS, novt[:, :], ALU.is_gt, ALU.add))
                d.scalar_tensor_tensor(novt[:, :], cnt, 3.0 * SLOTS, novt[:, :], ALU.is_gt, ALU.add).then_inc(novt_ready, 1)
                dve.wait_ge(starts_ps, l + 1)
                st(d.tensor_copy(starts[:, :], ps[2][:, 0:2 * NE + 1]))
                st(d.tensor_scalar(delta[:, :], starts[:, 0:NE], float(NE - 1), float(SLOTS), ALU.add, ALU.mult))
                st(d.tensor_tensor(delta[:, :], delta[:, :], base_e[:, :], ALU.subtract))
                rank = ps[1][:, 0:TT * NE].rearrange("p (t e) -> p t e", t=TT)
                st(d.scalar_tensor_tensor(dall[:, :, :], rank, float(SLOTS), bc(delta[:, :].unsqueeze(1), [P, TT, NE]),
                                          ALU.is_ge, ALU.mult))
                st(d.tensor_tensor(dall[:, :, :], dall[:, :, :], bc(base_e[:, :].unsqueeze(1), [P, TT, NE]), ALU.add))
                st(d.tensor_tensor(dall[:, :, :], dall[:, :, :], rank, ALU.add))
                st(d.tensor_tensor(eq[:, :, :], oh[:, 0], dall[:, :, :], ALU.mult))
                st(d.tensor_reduce(dst[:, 0], eq[:, :, :], AXX, ALU.add))
                st(d.tensor_tensor(eq[:, :, :], oh[:, 1], dall[:, :, :], ALU.mult))
                d.tensor_reduce(dst[:, 1], eq[:, :, :], AXX, ALU.add).then_inc(dst_ready, 1)
                dve.wait_ge(dst_ready, l + 1)
                st(d.tensor_tensor(cmp8[:, :, :], bc(starts[0:1, NE:2 * NE].unsqueeze(1), [1, EXTRA, NE]),
                                   iot8[:, :].rearrange("p (b e) -> p b e", b=EXTRA), ALU.is_le))
                st(d.tensor_reduce(tabf[:, NE:NE + EXTRA], cmp8[:, :, :], AXX, ALU.add))
                st(d.tensor_scalar(tabf[:, NE:NE + EXTRA], tabf[:, NE:NE + EXTRA], float(NE - 1), None, ALU.min))
                d.tensor_copy(tabf[:, 0:NE], iota_f[0:1, 0:NE])
                d.tensor_copy(tabf[:, 41:42], total[:, :])
                st(d.tensor_scalar(cmp8[:, 0, 0:4], tabx[:, :], starts[0:1, 2 * NE:2 * NE + 1], None, ALU.is_lt))
                st(d.tensor_reduce(tabf[:, 40:41], cmp8[:, 0, 0:4], AXX, ALU.add))
                st(d.tensor_scalar(tabf[:, 40:41], tabf[:, 40:41], float(NE // 2), None, ALU.add))
                d.tensor_tensor(total[:, :], total[:, :], tabf[:, 40:41], ALU.add)
                d.tensor_copy(tabi[:, 0:42], tabf[:, 0:42]).then_inc(table_ready, 1)
                d.tensor_copy(dcur[:, :, :, :], dst[:, :, :, :])
                st(d.tensor_copy(pcur[:, :], pcol[:, :]))
                dve.wait_ge(rows_ps, 2 * l + 1)
                d.tensor_copy(drow.rearrange("p k t -> p (k t)"), ps[2][:, :]).then_inc(rows_dve, 1)

                dve.wait_ge(table_ready, l + 1)
                dve.sem_inc(dve_held, 1)
                pairs = dve.value_load(tabi[0:1, 40:41], min_val=NE // 2, max_val=(NE + EXTRA) // 2)
                done = dve.value_load(tabi[0:1, 41:42], min_val=0, max_val=DEPTH * (NE + EXTRA) // 2)

                def one_hots(steps, made):
                    for tt in range(TT):
                        last = d.tensor_scalar(oneh[:, tt, :], iota_f[:, :], dcur[:, 0, tt, :], None, ALU.is_equal)
                    steps(last)
                    for tt in range(TT):
                        last = d.scalar_tensor_tensor(oneh[:, tt, :], iota_f[:, :], dcur[:, 1, tt, :], oneh[:, tt, :],
                                                      ALU.is_equal, ALU.add)
                    last.then_inc(oneh_ready, 1)
                    dve.wait_ge(oneh_ready, made)
                    steps(d.tensor_scalar(dcur[:, :, :, :], dcur[:, :, :, :], float(2 * SLOTS), None, ALU.subtract))

                def rows_in():
                    d.tensor_copy(xg[:, 0:4, :].rearrange("p k s -> p (k s)"), ps[6][:, :]).then_inc(xg_dve, 1)

                one_hots(st, done + l + 1)
                d.memset(wt, 0.0).then_inc(wt_ready, 1)
                d.memset(ym[:, 0:CH], 0.0).then_inc(y_dve, 1)
                d.memset(ym[:, CH:2 * CH], 0.0).then_inc(y_act, 1)
                dve.wait_ge(gathered, 2 * (done + l) + 1)
                rows_in()
                dve.wait_ge(rows_act, l + 1)
                dve.sem_inc(dve_held, 1)
                with dve.Fori(0, pairs) as i:
                    n = dve.snap(done + i)
                    sp_ = Steps(dve, dve_pair, n * DVE_PAIR_STEPS)
                    dve.wait_ge(gathered, 2 * (n + l) + 2)
                    one_hots(sp_, n + l + 2)
                    dve.wait_ge(combined, n + l + 1)
                    d.scalar_tensor_tensor(wt, drow[:, 0, :], pcur[:, :], wrow[:, 0, :], ALU.is_equal, ALU.mult)
                    sp_(d.scalar_tensor_tensor(w2, drow[:, 1, :], pcur[:, :], wrow[:, 1, :], ALU.is_equal, ALU.mult))
                    d.tensor_tensor(wt, wt, w2, ALU.add).then_inc(wt_ready, 1)
                    sp_(d.tensor_scalar(pcur[:, :], pcur[:, :], float(2 * SLOTS), None, ALU.add))
                    dve.wait_ge(up_used, n + 1)
                    dve.wait_ge(silued, n + 1)
                    d.tensor_tensor(hid, sil, ps[5][:, :], ALU.mult).then_inc(h_ready, 1)
                    dve.wait_ge(gathered, 2 * (n + l) + 3)
                    rows_in()
                    dve.wait_ge(h_tr, n + 1)
                    d.tensor_copy(hT.rearrange("p k s -> p (k s)"), ps[4][:, :]).then_inc(hT_ready, 1)
                    dve.wait_ge(down_used, n + 1)
                    d.tensor_copy(ym[:, 0:CH], ps[6][:, :]).then_inc(y_dve, 1)
                    assert sp_.n == DVE_PAIR_STEPS, sp_.n
                layer_norm(1, lambda tt, half: dve.wait_ge(acc_done, l + 1))
                assert st.n == DVE_LAYER_STEPS, st.n

        @block.tensor
        def _(pe):
            t = nc.tensor

            def transpose_rows(src, n):
                for b in range(4):
                    for k in (2 * b, 2 * b + 1):
                        for tt in range(TT):
                            last = t.transpose(ps[4 + b][:, (k % 2) * SEQ + tt * P:(k % 2) * SEQ + (tt + 1) * P],
                                               src[:, tt, k:D:KT], ident[:, :])
                    last.then_inc(tr_bank, 1)

            pe.wait_ge(consts_ready, 1)
            pe.wait_ge(x_in, 16)
            with pe.Fori(0, DEPTH) as l:
                def project(c):
                    pe.wait_ge(chunk_in[c], 16 * (l + 1) * (len(COLS[c]) if c < 8 else 1))
                    if 2 <= c < 8:
                        pe.wait_ge(read_dve, 7 * l + DVE_READ[c - 2])
                        pe.wait_ge(read_act, 6 * l + ACT_READ[c - 2])
                    w = slot(SLOT_OF[c])
                    b0 = 2 * (c % 2)
                    if c in (0, 2, 3):
                        for j in range(4):
                            for k in range(KT):
                                last = t.matmul(ps[b0 + j // 2][:, (j % 2) * SEQ:(j % 2 + 1) * SEQ],
                                                w[:, k, j * P:(j + 1) * P], xT[:, k, :], start=(k == 0), stop=(k == KT - 1))
                    else:
                        n = sum(b - a for a, b in COLS[c]) if c < 8 else CH
                        src = xT if c < 8 else yT
                        for tt in range(TT):
                            for k in range(KT):
                                last = t.matmul(ps[b0 + tt][:, 0:n], src[:, k, tt * P:(tt + 1) * P], w[:, k, 0:n],
                                                start=(k == 0), stop=(k == KT - 1))
                    last.then_inc(proj, 1)

                pe.wait_ge(x_done, 4 * l + 1)
                transpose_rows(x, 12 * l)
                pe.wait_ge(tr_dve, 6 * l + 2)
                pe.wait_ge(tr_act, 6 * l + 2)
                project(0)
                pe.wait_ge(par_in, 16 * PAR_DMAS * (l + 1))
                t.matmul(ps[7][:, 384:384 + CONV * 8], cwr[:, :], ident[0:CONV * 8, 0:CONV * 8],
                         start=True, stop=True).then_inc(cw_tr, 1)
                project(1)
                project(2)
                pe.wait_ge(ls_ready, l + 1)
                pe.wait_ge(cw_ready, l + 1)
                t.matmul(ps[7][:, 0:8], tri_incl[:, :], ls[:, 0, :], start=True, stop=True)
                t.matmul(ps[7][:, 8:16], tri_incl[:, :], ls[:, 1, :], start=True, stop=False)
                t.matmul(ps[7][:, 8:16], ones[:, :], ls[:, 0, :], start=False, stop=True).then_inc(cum_done, 1)
                project(3)
                pe.wait_ge(gpad_ready, l + 1)
                for tt in range(TT):
                    last = t.transpose(ps[7][:, tt * P:(tt + 1) * P], gpad[:, tt, :], ident[:, :])
                last.then_inc(cat_tr, 1)
                for c in (4, 5, 6, 7):
                    project(c)
                pe.wait_ge(roped, 2 * l + 2)
                for bank in (4, 5):
                    for c in range(2):
                        for tt in range(TT):
                            o = (2 * (bank - 4) + c) * P
                            last = t.transpose(ps[bank][:, c * SEQ + tt * P:c * SEQ + (tt + 1) * P], bqk[:, tt, o:o + P], ident[:, :])
                    last.then_inc(rope_tr, 1)

                pe.wait_ge(read_dve, 7 * l + DVE_READ[7])
                pe.wait_ge(read_act, 6 * l + ACT_READ[7])
                pe.wait_ge(cat_ready, l + 1)
                pe.wait_ge(kscaled, l + 1)
                pe.wait_ge(qb_ready, l + 1)
                pe.wait_ge(kb_ready, l + 1)

                def masked(dest, mm):
                    for tt in range(TT):
                        o = dest[:, 0:P] if tt == 0 else dest[:, P:3 * P]
                        mm(tt, o, (tt + 1) * P)
                        last = t.matmul(dest[:, 2 * tt * P:(2 * tt + 1) * P], identb[:, :], maskb[:, :], start=False, stop=True)
                    return last

                def scores(j):
                    b, h = j % 2, j % FH
                    q, k = {"fox": (qf[:, h], kf[:, h // 2]), "mlstm": (qkm[:, h], qkm[:, MH + h]),
                            "moba": (qb[:, h], kb[:, h // 2])}[kind(j)]
                    row = h if kind(j) == "fox" else 4 + h
                    if j >= 2:
                        if kind(j - 2) == "mlstm":
                            pe.wait_ge(prod_done, MLS * l + mlstm_up_to(j - 2))
                        else:
                            pe.wait_ge(exp_done, SOFT * l + soft_up_to(j - 2))

                    def qk(tt, o, n, stop=False):
                        t.matmul(o, q[:, tt * P:(tt + 1) * P], k[:, 0:n], start=True, stop=stop)

                    def cum(tt, o, n, start=False):
                        t.matmul(o, bc(ident[:, row:row + 1], [P, P]), catT[:, 0:n], start=start, stop=False)

                    if kind(j) == "fox":
                        last = masked(ps[b], lambda tt, o, n: (qk(tt, o, n), cum(tt, o, n)))
                    elif kind(j) == "moba":
                        last = masked(ps[b], qk)
                    else:
                        for tt in range(TT):
                            qk(tt, ps[b][:, 0:P] if tt == 0 else ps[b][:, P:3 * P], (tt + 1) * P, True)
                        last = masked(ps[2 + b], lambda tt, o, n: cum(tt, o, n, True))
                    last.then_inc(scored, 1)

                for it in range(HEADS + 2):
                    if it < HEADS:
                        scores(it)
                    if 1 <= it <= HEADS:
                        j, b = it - 1, (it - 1) % 2
                        if kind(j) == "mlstm":
                            pe.wait_ge(prod_done, MLS * l + mlstm_up_to(j))
                        else:
                            pe.wait_ge(exp_done, SOFT * l + soft_up_to(j))
                        if j >= 2:
                            pe.wait_ge(pt_ready, HEADS * l + j - 1)
                        for q in range(3):
                            last = t.transpose(ps[4 + b][:, q * P:(q + 1) * P], Pm[:, b, q * P:(q + 1) * P], ident[:, :])
                        last.then_inc(p_tr, 1)
                    if it >= 2:
                        j, b = it - 2, it % 2
                        w, c = width(j), column(j)
                        pe.wait_ge(pt_ready, HEADS * l + j + 1)
                        if j >= 2:
                            pe.wait_ge(o_read, HEADS * l + j - 1)
                        t.matmul(ps[6 + b][:, 0:w], PT[:, b, 0:P], v[:, 0, c:c + w], start=True, stop=True)
                        t.matmul(ps[6 + b][:, w:2 * w], PT[:, b, P:2 * P], v[:, 0, c:c + w], start=True, stop=False)
                        t.matmul(ps[6 + b][:, w:2 * w], PT[:, b, 2 * P:3 * P], v[:, 1, c:c + w], start=False,
                                 stop=True).then_inc(pv_done, 1)

                pe.wait_ge(y_ready, 2 * l + 2)
                transpose_rows(y, 4 + 12 * l)
                pe.wait_ge(tr_dve, 6 * l + 4)
                pe.wait_ge(tr_act, 6 * l + 4)
                project(8)
                project(9)
                pe.wait_ge(x_done, 4 * l + 3)
                transpose_rows(x, 8 + 12 * l)
                pe.wait_ge(tr_dve, 6 * l + 6)
                pe.wait_ge(tr_act, 6 * l + 6)
                for tt in range(TT):
                    for w, o, n in ((wr4, 0, NG), (wr32, NG, NE)):
                        for k in range(KT):
                            last = t.matmul(ps[0][:, tt * 64 + o:tt * 64 + o + n], xT[:, k, tt * P:(tt + 1) * P], w[:, k, :],
                                            start=(k == 0), stop=(k == KT - 1))
                last.then_inc(logits, 1)
                pe.wait_ge(masks_ready, l + 1)
                t.matmul(ps[1][:, 0:NE], tri_strict[:, :], mall[:, 0, :], start=True, stop=True)
                t.matmul(ps[1][:, NE:2 * NE], tri_strict[:, :], mall[:, 1, :], start=True, stop=False)
                t.matmul(ps[1][:, NE:2 * NE], ones[:, :], mall[:, 0, :], start=False, stop=True)
                t.matmul(ps[1][0:NE, 128:256], mall[:, 0, :], ones[:, :], start=True, stop=False)
                t.matmul(ps[1][0:NE, 128:256], mall[:, 1, :], ones[:, :], start=False, stop=True).then_inc(ranks, 1)
                pe.wait_ge(novt_ready, l + 1)
                t.matmul(ps[2][:, 0:2 * NE + 1], novt[:, :], tri65[:, :], start=True, stop=True).then_inc(starts_ps, 1)
                pe.wait_ge(dst_ready, l + 1)
                for bank, col in ((2, dst), (3, wgt)):
                    for k in range(2):
                        for tt in range(TT):
                            last = t.matmul(ps[bank][:, k * SEQ + tt * P:k * SEQ + (tt + 1) * P], bc(col[:, k, tt, :], [P, P]),
                                            ident[:, :], start=True, stop=True)
                    last.then_inc(rows_ps, 1)

                pe.wait_ge(table_ready, l + 1)
                pe.sem_inc(pe_held, 1)
                pairs = pe.value_load(tabi[0:1, 40:41], min_val=NE // 2, max_val=(NE + EXTRA) // 2)
                done = pe.value_load(tabi[0:1, 41:42], min_val=0, max_val=DEPTH * (NE + EXTRA) // 2)
                pe.wait_ge(rows_dve, l + 1)
                pe.wait_ge(rows_act, l + 1)
                for b in range(4):
                    t.matmul(ps[b][:, :], zerob[:, :], bc(zerob[:, 0:1], [P, CH]), start=True, stop=False)

                def gather():
                    for k in range(KT):
                        for tt in range(TT):
                            last = t.matmul(ps[6 + k // 4][:, (k % 4) * P:(k % 4 + 1) * P], x[:, tt, k:D:KT], oneh[:, tt, :],
                                            start=(tt == 0), stop=(tt == TT - 1))
                        if k % 4 == 3:
                            last.then_inc(gathered, 1)

                def combine():
                    for tt in range(TT):
                        for half in range(2):
                            last = t.matmul(ps[2 * half + tt][:, :], wt[:, tt * P:(tt + 1) * P], ym[:, half * CH:(half + 1) * CH],
                                            start=False, stop=False)
                    last.then_inc(combined, 1)

                pe.wait_ge(oneh_ready, done + l + 1)
                gather()
                with pe.Fori(0, pairs) as i:
                    n = pe.snap(done + i)
                    nl = pe.snap(n + l)
                    pe.wait_ge(xg_dve, nl + 1)
                    pe.wait_ge(xg_act, nl + 1)
                    pe.wait_ge(gate_in, n * 32 + 32)
                    for k in range(KT):
                        for q in range(2):
                            last = t.matmul(ps[4][64 * q:64 * q + 64, :], xg[:, k, 64 * q:64 * q + 64], slot(q)[:, k, :],
                                            start=(k == 0), stop=(k == KT - 1))
                    last.then_inc(gate_used, 1)
                    pe.wait_ge(y_dve, nl + 1)
                    pe.wait_ge(y_act, nl + 1)
                    pe.wait_ge(wt_ready, nl + 1)
                    combine()
                    pe.wait_ge(up_in, n * 32 + 32)
                    for k in range(KT):
                        for q in range(2):
                            last = t.matmul(ps[5][64 * q:64 * q + 64, :], xg[:, k, 64 * q:64 * q + 64], slot(2 + q)[:, k, :],
                                            start=(k == 0), stop=(k == KT - 1))
                    last.then_inc(up_used, 1)
                    pe.wait_ge(oneh_ready, nl + 2)
                    gather()
                    pe.wait_ge(h_ready, n + 1)
                    for f in range(FT):
                        last = t.transpose(ps[4][:, f * P:(f + 1) * P], hid[:, f:DE:FT], ident[:, :])
                    last.then_inc(h_tr, 1)
                    pe.wait_ge(hT_ready, n + 1)
                    pe.wait_ge(xg_dve, nl + 2)
                    pe.wait_ge(xg_act, nl + 2)
                    pe.wait_ge(down_in, n * 32 + 32)
                    for f in range(FT):
                        for half in range(2):
                            for q in range(2):
                                w = ring[:, 4 + q, :].rearrange("p (f n) -> p f n", f=FT)
                                last = t.matmul(ps[6 + half][64 * q:64 * q + 64, :], hT[:, f, 64 * q:64 * q + 64],
                                                w[:, f, half * CH:(half + 1) * CH], start=(f == 0), stop=(f == FT - 1))
                    last.then_inc(down_used, 1)
                end = pe.snap(done + pairs)
                pe.wait_ge(y_dve, end + l + 1)
                pe.wait_ge(y_act, end + l + 1)
                pe.wait_ge(wt_ready, end + l + 1)
                combine()
                for b in range(4):
                    last = t.matmul(ps[b][:, :], zerob[:, :], bc(zerob[:, 0:1], [P, CH]), start=False, stop=True)
                last.then_inc(acc_done, 1)


_INS = ['x', 'positions', 'w_in', 'b_fox_f', 'b_mlstm_i', 'b_mlstm_f', 'conv_w', 'g_fox', 'g_mlstm', 'g_moba',
        'w_out', 'ln1_g', 'ln1_b', 'w_grp', 'b_grp', 'w_exp_router', 'b_exp_router', 'w_gate', 'w_up', 'w_down',
        'ln2_g', 'ln2_b']


def kernel(**inputs):
    import numpy as _np
    import concourse.bacc as _bacc
    from concourse import mybir as _mybir
    from concourse.bass_utils import run_bass_kernel_spmd as _run

    nc = _bacc.Bacc("TRN2", target_bir_lowering=False, num_devices=1)
    arrays, args = {}, {}
    for name in _INS:
        a = _np.ascontiguousarray(inputs[name])
        arrays[f"in_{name}_dram"] = a
        args[name] = nc.dram_tensor(f"in_{name}_dram", a.shape, _mybir.dt.from_np(a.dtype), kind="ExternalInput").ap()
    out = nc.dram_tensor("out_0_dram", (1, SEQ, D), _mybir.dt.float32, kind="ExternalOutput").ap()
    build(nc, args, out)
    r = _run(nc, [arrays], core_ids=[0])
    return r.results[0]["out_0_dram"]
```

```python
from contextlib import ExitStack
import math

import concourse.bass as bass
from concourse import mybir

ALU = mybir.AluOpType
ACT = mybir.ActivationFunctionType
F32 = mybir.dt.float32
BF16 = mybir.dt.bfloat16
I32 = mybir.dt.int32
AXX = mybir.AxisListType.X

P = 128
SEQ, D, DEPTH = 256, 1024, 2
TT = SEQ // P
KT = D // P
FH, FD = 4, 64
MH, MD = 4, 128
CONV = 4
ROPE_HALF = 8
NG, EG, NE, DE = 4, 8, 32, 512
FT = DE // P
SLOTS = 64
EXTRA = 8
ALPHA = (2 * DEPTH) ** 0.25
EPS = 1e-5
BIG = 1e30
CH = 512
NCHUNK = 10
HEADS = 2 * FH + MH
SLOT_OF = [6, 7, 0, 1, 2, 3, 4, 5, 6, 7]
COLS = [[(0, 512)], [(512, 772), (2308, 2316)], [(2828, 3340)], [(3340, 3596)], [(772, 1284)],
        [(1284, 1796)], [(1796, 2308)], [(2316, 2828)]]
DVE_READ = [1, 2, 3, 4, 5, 6, 7, 7]
ACT_READ = [1, 2, 3, 4, 4, 4, 5, 6]
PAR_DMAS = 11


class Steps:

    def __init__(self, eng, sem, base):
        self.eng, self.sem, self.base, self.n = eng, sem, base, 0

    def __call__(self, ins):
        self.n += 1
        ins.then_inc(self.sem, 1)
        self.eng.wait_ge(self.sem, self.base + self.n)


def kind(j):
    return "fox" if j < FH else "moba" if j < 2 * FH else "mlstm"


def width(j):
    return MD if kind(j) == "mlstm" else FD


def column(j):
    if kind(j) == "fox":
        return j * FD
    if kind(j) == "mlstm":
        return FH * FD + (j - 2 * FH) * MD
    return FH * FD + MH * MD + (j - FH) * FD


def soft_up_to(j):
    return min(j + 1, 2 * FH)


def mlstm_up_to(j):
    return max(j + 1 - 2 * FH, 0)


def mixer_order():
    between = {(2, 1): ["cum"], (2, 3): ["cat"], (3, 1): [0], (3, 3): [1], (4, 0): [2], (4, 1): ["ropeq", 3],
               (4, 2): ["ropek"], (4, 3): [4], (5, 0): [5], (5, 1): [6], (5, 2): [7], (6, 2): [8], (6, 3): [9],
               (7, 0): [10], (7, 1): [11], (7, 2): [12], (7, 3): [13]}
    for c in range(8):
        for part in range(4):
            yield "proj", c, part
            for e in between.get((c, part), ()):
                yield ("att", e, 0) if isinstance(e, int) else (e, 0, 0)


SOFT, MLS = soft_up_to(HEADS - 1), mlstm_up_to(HEADS - 1)
DVE_LAYER_STEPS = 95
DVE_PAIR_STEPS = 4
ACT_LAYER_STEPS = 1
POOL_LAYER_STEPS = 2


def build(nc, A, out):
    ctx = ExitStack()
    with ctx:
        def sb(name, shape, dt=F32):
            return ctx.enter_context(nc.sbuf_tensor(name, shape, dt))

        def sem(name):
            return ctx.enter_context(nc.semaphore(name))

        ring = sb("ring", [P, 8, KT * CH])
        x = sb("xres", [P, TT, D])
        bufa = sb("bufa", [P, 2048])
        bufb = sb("bufb", [P, 2048])
        bufc = sb("bufc", [P, 2048])
        bufd = sb("bufd", [P, 1024])
        bufe = sb("bufe", [P, 1024])
        lnp = sb("lnp", [P, 2, D])
        qf = sb("qf", [P, FH, SEQ])
        kf = sb("kf", [P, FH // 2, SEQ])
        qb = sb("qb", [P, FH, SEQ])
        kb = sb("kb", [P, FH // 2, SEQ])
        Pm = sb("Pm", [P, 2, 3 * P])
        Wm = sb("Wm", [P, 3 * P])
        catT = sb("catT", [P, SEQ])
        gpad = sb("gpad", [P, TT, P])
        ident = sb("ident", [P, P])
        identb = sb("identb", [P, P], BF16)
        maskb = sb("maskb", [P, P], BF16)
        tri_incl = sb("tri_incl", [P, P])
        tri_strict = sb("tri_strict", [P, P])
        ones = sb("ones", [P, P])
        zerob = sb("zerob", [P, P], BF16)
        iota_f = sb("iota_f", [P, P])
        desc = sb("desc", [P, NE])
        base_e = sb("base_e", [P, NE])
        tri65 = sb("tri65", [NE, 2 * NE + 1])
        iot8 = sb("iot8", [1, EXTRA * NE])
        pcol_i = sb("pcol_i", [P, 1], I32)
        pcol = sb("pcol", [P, 1])
        ones_c = sb("ones_c", [P, 1])
        pos_i = sb("pos_i", [P, TT], I32)
        pos_f = sb("pos_f", [P, TT])
        inv = sb("inv", [P, ROPE_HALF])
        ang = sb("ang", [P, TT, ROPE_HALF])
        kk = sb("kk", [P, TT, ROPE_HALF])
        ang_s = sb("ang_s", [P, TT, ROPE_HALF])
        ang_c = sb("ang_c", [P, TT, ROPE_HALF])
        cos = sb("cos", [P, TT, ROPE_HALF])
        sin = sb("sin", [P, TT, ROPE_HALF])
        cwr = sb("cwr", [CONV * 8, P])
        cw = sb("cw", [P, CONV * 8])
        bias12 = sb("bias12", [P, 12])
        rb36 = sb("rb36", [P, 36])
        gcol = sb("gcol", [P, KT])
        wr = sb("wr", [P, KT, NG + NE])
        lgT = Wm[0:NG + NE, 0:SEQ]
        junk = sb("junk", [P, 4, TT, FD])
        junk_m = bufc[:, 0:1024].rearrange("p (t n) -> p t n", t=TT)
        z12 = sb("z12", [P, TT, 12])
        az = sb("az", [P, TT, 8])
        mn = sb("mn", [P, TT, 8])
        ls = sb("ls", [P, TT, 8])
        bcum = sb("bcum", [P, TT, 4])
        nmx = sb("nmx", [P, 4, 2])
        stat = sb("stat", [P, 4, 2])
        rinv = sb("rinv", [P, 4, 2])
        em = sb("em", [P, 4, 2])
        mhalf = sb("mhalf", [P, TT])
        ms = sb("ms", [P, TT, HEADS])
        bns = sb("bns", [P, TT, 2, 6])
        mv = sb("mv", [P, TT, 2])
        rstd = sb("rstd", [P, TT])
        nmr = sb("nmr", [P, TT])
        lg = sb("lg", [P, TT, 36])
        r1 = sb("r1", [P, TT, 1])
        g4 = sb("g4", [P, TT, NG])
        e4 = sb("e4", [P, TT, NG])
        d4 = sb("d4", [P, TT, NG])
        s4 = sb("s4", [P, TT, 1])
        gmx = sb("gmx", [P, TT, 1])
        v12 = sb("v12", [P, 2, TT, 1])
        emk = sb("emk", [P, TT, NE])
        eq = sb("eq", [P, TT, NE])
        oh = sb("oh", [P, 2, TT, NE])
        mall = sb("mall", [P, TT, NE])
        dd = sb("dd", [P, TT, 1])
        ex = sb("ex", [P, TT, 1])
        wgt = sb("wgt", [P, 2, TT, 1])
        dst = sb("dst", [P, 2, TT, 1])
        novt = Wm[0:NE, 2 * P:3 * P]
        starts = sb("starts", [P, 2 * NE + 1])
        delta = sb("delta", [P, NE])
        dall = sb("dall", [P, TT, NE])
        dcur = sb("dcur", [P, 2, TT, 1])
        pcur = sb("pcur", [P, 1])
        tabf = sb("tabf", [1, 48])
        tabx = sb("tabx", [1, 4])
        tabi = sb("tabi", [1, 48], I32)
        total = sb("total", [1, 1])

        xT = bufa[:, :].rearrange("p (k t) -> p k t", k=KT)
        y = lnp[:, :, :]
        v = bufb[:, :].rearrange("p (t n) -> p t n", t=TT)
        yT = bufb[:, :].rearrange("p (k t) -> p k t", k=KT)
        drow = bufb[:, 0:512].rearrange("p (k t) -> p k t", k=2)
        wrow = bufb[:, 512:1024].rearrange("p (k t) -> p k t", k=2)
        sil = bufb[:, 1024:1536]
        hid = bufb[:, 1536:2048]
        qkm = bufc[:, :].rearrange("p (c t) -> p c t", c=8)
        xg = bufc[:, 0:1024].rearrange("p (k s) -> p k s", k=KT)
        ym = bufc[:, 1024:2048]
        sg = bufd[:, :].rearrange("p (t n) -> p t n", t=TT)
        hT = bufd[:, 0:512].rearrange("p (k s) -> p k s", k=FT)
        oneh = bufd[:, 512:768].rearrange("p (t s) -> p t s", t=TT)
        wt = bufd[:, 768:1024]
        bqk = bufd[:, :].rearrange("p (t n) -> p t n", t=TT)
        PT = bufe[:, 0:768].rearrange("p (b n) -> p b n", b=2)
        rt = bufe[:, 768:1024].rearrange("p (i h d) -> p i h d", i=4, h=8)
        cmp8 = Wm[0:1, 0:EXTRA * NE].rearrange("p (b e) -> p b e", b=EXTRA)
        iota_i = bufc[:, 0:P].bitcast(I32)
        desc_i = bufc[:, P:P + NE].bitcast(I32)
        iot8_i = bufc[0:1, 512:512 + EXTRA * NE].bitcast(I32)
        w2 = Pm[:, 0, 0:SEQ]

        ps = [ctx.enter_context(nc.psum_tensor(f"ps{i}", [P, 512], F32)) for i in range(8)]

        x_in, pos_in = sem("x_in"), sem("pos_in")
        chunk_in = [sem(f"chunk_in{c}") for c in range(NCHUNK)]
        gate_in, up_in, down_in = sem("gate_in"), sem("up_in"), sem("down_in")
        par_issued = sem("par_issued")
        par_in, ln_in = sem("par_in"), sem("ln_in")
        consts_ready = sem("consts_ready")
        dve_consts = sem("dve_consts")
        angles = sem("angles")
        trig = sem("trig")
        dve_step, act_step, pool_step = sem("dve_step"), sem("act_step"), sem("pool_step")
        dve_pair = sem("dve_pair")
        dve_setup = sem("dve_setup")
        pool_setup = sem("pool_setup")
        tr_bank = sem("tr_bank")
        tr_dve, tr_act = sem("tr_dve"), sem("tr_act")
        mix_half = sem("mix_half")
        proj = sem("proj")
        read_dve, read_act = sem("read_dve"), sem("read_act")
        cw_tr, cw_ready = sem("cw_tr"), sem("cw_ready")
        az_ready, ln_ready, ls_ready = sem("az_ready"), sem("ln_ready"), sem("ls_ready")
        cum_done, gpad_ready, cat_tr, cat_ready = sem("cum_done"), sem("gpad_ready"), sem("cat_tr"), sem("cat_ready")
        silu_done, kscaled = sem("silu_done"), sem("kscaled")
        roped, rope_tr, qb_ready, kb_ready = sem("roped"), sem("rope_tr"), sem("qb_ready"), sem("kb_ready")
        scored, maxed = sem("scored"), sem("maxed")
        exp_done, wexp_done, prod_done = sem("exp_done"), sem("wexp_done"), sem("prod_done")
        p_tr, pt_ready, pv_done, o_read = sem("p_tr"), sem("pt_ready"), sem("pv_done"), sem("o_read")
        y_gated, squared, y_ready = sem("y_gated"), sem("squared"), sem("y_ready")
        var_ready, rstd_ready = sem("var_ready"), sem("rstd_ready")
        stats_ready, normed, scaled, x_done = sem("stats_ready"), sem("normed"), sem("scaled"), sem("x_done")
        logits, lgT_ready, logits_tr = sem("logits"), sem("lgT_ready"), sem("logits_tr")
        gdiff, gexp, vdiff, vexp = sem("gdiff"), sem("gexp"), sem("vdiff"), sem("vexp")
        masks_ready, ranks, novt_ready, starts_ps = sem("masks_ready"), sem("ranks"), sem("novt_ready"), sem("starts_ps")
        dst_ready, rows_ps, rows_dve, rows_act = sem("dst_ready"), sem("rows_ps"), sem("rows_dve"), sem("rows_act")
        table_ready = sem("table_ready")
        oneh_ready, gathered, xg_dve, xg_act = sem("oneh_ready"), sem("gathered"), sem("xg_dve"), sem("xg_act")
        gate_used, up_used, down_used = sem("gate_used"), sem("up_used"), sem("down_used")
        combined, silued, h_ready, h_tr, hT_ready = sem("combined"), sem("silued"), sem("h_ready"), sem("h_tr"), sem("hT_ready")
        wt_ready, y_dve, y_act = sem("wt_ready"), sem("y_dve"), sem("y_act")
        acc_done = sem("acc_done")
        out_sem = sem("out_sem")
        dve_held, act_held, pe_held, pool_held = sem("dve_held"), sem("act_held"), sem("pe_held"), sem("pool_held")

        block = ctx.enter_context(nc.Block())

        def bc(ap, shape):
            return ap.to_broadcast(shape)

        def slot(s, n=CH):
            return ring[:, s, 0:KT * n].rearrange("p (k n) -> p k n", k=KT)

        @block.sync
        def _(sp):
            with nc.allow_non_contiguous_dma(reason="256 positions"):
                sp.dma_start(pos_i[:, :], A["positions"][0].rearrange("(t p) -> p t", p=P)).then_inc(pos_in, 16)
            sp.dma_start(x[:, :, :], A["x"][0].rearrange("(t p) d -> p t d", p=P)).then_inc(x_in, 16)

            def load_chunk(l, c):
                s = slot(SLOT_OF[c])
                if c >= 8:
                    src = A["w_out"][l].rearrange("(p k) n -> p k n", k=KT)[:, :, (c - 8) * CH:(c - 7) * CH]
                    sp.dma_start(s[:, :, :], src).then_inc(chunk_in[c], 16)
                    return
                at = 0
                for a, b in COLS[c]:
                    src = A["w_in"][l].rearrange("(p k) n -> p k n", k=KT)[:, :, a:b]
                    sp.dma_start(s[:, :, at:at + b - a], src).then_inc(chunk_in[c], 16)
                    at += b - a

            def load_pair(l, part, e):
                w, first, arrived = {"gate": ("w_gate", 0, gate_in), "up": ("w_up", 2, up_in),
                                     "down": ("w_down", 4, down_in)}[part]
                for q in range(2):
                    src = A[w][l].rearrange("e (p k) n -> e p (k n)", p=P)[bass.ds(e[q], 1)] if not isinstance(e[q], int) \
                        else A[w][l].rearrange("e (p k) n -> e p (k n)", p=P)[e[q]:e[q] + 1]
                    sp.dma_start(ring[:, first + q, :], src.rearrange("a p n -> (a p) n")).then_inc(arrived, 16)

            load_chunk(0, 0)
            sp.wait_ge(par_issued, 1)
            load_chunk(0, 1)
            done = 0
            for l in range(DEPTH):
                for c in range(2, 8):
                    if l > 0:
                        sp.wait_ge((gate_used, up_used, down_used)[SLOT_OF[c] // 2], done)
                    load_chunk(l, c)
                for c in (8, 9):
                    sp.wait_ge(proj, NCHUNK * l + c - 7)
                    load_chunk(l, c)
                for i, part in enumerate(("gate", "up", "down")):
                    sp.wait_ge(proj, NCHUNK * l + 2 * i + 4)
                    load_pair(l, part, (0, 1))
                if l + 1 < DEPTH:
                    for c in (0, 1):
                        sp.wait_ge(proj, NCHUNK * l + 9 + c)
                        load_chunk(l + 1, c)
                sp.wait_ge(table_ready, l + 1)
                pairs = sp.value_load(tabi[0:1, 40:41], min_val=NE // 2, max_val=(NE + EXTRA) // 2)
                with sp.Fori(1, pairs) as i:
                    e = [sp.value_load(tabi[0:1, bass.ds(2 * i + q, 1)], min_val=0, max_val=NE - 1) for q in range(2)]
                    for part, used in (("gate", gate_used), ("up", up_used), ("down", down_used)):
                        sp.wait_ge(used, done + i)
                        load_pair(l, part, e)
                done = sp.snap(done + pairs)
            for tt in range(TT):
                sp.wait_ge(x_done, 4 * DEPTH + 1 + tt)
                sp.dma_start(out[0].rearrange("(t p) d -> t p d", p=P)[tt], x[:, tt, :]).then_inc(out_sem, 16)
            sp.wait_ge(out_sem, 16 * TT)

        @block.gpsimd
        def _(pool):
            st = Steps(pool, pool_setup, 0)
            g = nc.gpsimd
            g.memset(ident[:, :], 0.0)
            g.memset(tri_incl[:, :], 1.0)
            g.memset(tri_strict[:, :], 1.0)
            g.memset(ones[:, :], 1.0)
            g.memset(maskb[:, :], 0.0)
            g.memset(zerob[:, :], 0.0)
            g.memset(tri65[:, :], 1.0)
            g.memset(qf[:, :, :], 0.0)
            g.memset(qb[:, :, :], 0.0)
            g.memset(gpad[:, :, :], 0.0)
            g.memset(total[:, :], 0.0)
            for j in range(ROPE_HALF):
                g.memset(inv[:, j:j + 1], 500000.0 ** (-j / ROPE_HALF))
            for j in range(4):
                g.memset(tabx[:, j:j + 1], 2.0 * j)
            g.iota(iota_i[:, :], pattern=[[1, P]], base=0, channel_multiplier=0)
            g.iota(desc_i[:, :], pattern=[[-1, NE]], base=NE, channel_multiplier=0)
            g.iota(iot8_i[:, :], pattern=[[1, EXTRA], [0, NE]], base=0, channel_multiplier=0)
            st(g.iota(pcol_i[:, :], pattern=[[0, 1]], base=0, channel_multiplier=1))
            g.tensor_copy(iota_f[:, :], iota_i[:, :])
            g.tensor_copy(desc[:, :], desc_i[:, :])
            g.tensor_copy(iot8[:, :], iot8_i[:, :])
            g.tensor_copy(pcol[:, :], pcol_i[:, :])
            g.affine_select(out=ident[:, :], in_=ident[:, :], compare_op=ALU.not_equal, fill=1.0,
                            base=0, pattern=[[-1, P]], channel_multiplier=1)
            g.affine_select(out=tri_incl[:, :], in_=tri_incl[:, :], compare_op=ALU.is_ge, fill=0.0,
                            base=0, pattern=[[1, P]], channel_multiplier=-1)
            g.affine_select(out=tri_strict[:, :], in_=tri_strict[:, :], compare_op=ALU.is_gt, fill=0.0,
                            base=0, pattern=[[1, P]], channel_multiplier=-1)
            g.affine_select(out=maskb[:, :], in_=maskb[:, :], compare_op=ALU.is_ge, fill=-BIG,
                            base=0, pattern=[[-1, P]], channel_multiplier=1)
            g.affine_select(out=tri65[:, 0:NE], in_=tri65[:, 0:NE], compare_op=ALU.is_gt, fill=0.0,
                            base=0, pattern=[[1, NE]], channel_multiplier=-1)
            st(g.affine_select(out=tri65[:, NE:2 * NE], in_=tri65[:, NE:2 * NE], compare_op=ALU.is_ge, fill=0.0,
                               base=0, pattern=[[1, NE]], channel_multiplier=-1))
            g.tensor_copy(identb[:, :], ident[:, :]).then_inc(consts_ready, 1)
            g.memset(mhalf[:, :], -0.5).then_inc(x_done, 1)
            g.memset(ones_c[:, :], 1.0).then_inc(x_done, 1)
            pool.wait_ge(trig, 2)
            with pool.Fori(0, DEPTH) as l:
                st = Steps(pool, pool_step, l * POOL_LAYER_STEPS)
                pool.wait_ge(read_dve, 7 * l + DVE_READ[2])
                pool.wait_ge(read_act, 6 * l + ACT_READ[2])
                for tt in range(TT):
                    u = bqk[:, tt, :].rearrange("p (h d) -> p h d", d=FD)
                    u1, u2 = u[:, :, 0:ROPE_HALF], u[:, :, ROPE_HALF:2 * ROPE_HALF]
                    c = bc(cos[:, tt:tt + 1, :], [P, 8, ROPE_HALF])
                    s = bc(sin[:, tt:tt + 1, :], [P, 8, ROPE_HALF])
                    g.tensor_tensor(rt[:, 0], u1, c, ALU.mult)
                    g.tensor_tensor(rt[:, 1], u2, s, ALU.mult)
                    g.tensor_tensor(rt[:, 2], u1, s, ALU.mult)
                    st(g.tensor_tensor(rt[:, 3], u2, c, ALU.mult))
                    g.tensor_tensor(u1, rt[:, 0], rt[:, 1], ALU.subtract)
                    g.tensor_tensor(u2, rt[:, 2], rt[:, 3], ALU.add).then_inc(roped, 1)
                    pool.wait_ge(roped, 2 * l + tt + 1)
                pool.wait_ge(silu_done, 2 * l + 2)
                pool.sem_inc(pool_held, 1)
                g.tensor_scalar(qkm[:, MH:2 * MH, :], qkm[:, MH:2 * MH, :], float(MD) ** -0.5, None, ALU.mult).then_inc(kscaled, 1)

                def powers(n, of, to):
                    pool.wait_ge(var_ready, 6 * l + n + 1)
                    g.tensor_tensor(to, of, bc(mhalf[:, 0:1], of.shape) if len(of.shape) == 2 else
                                    bc(mhalf[:, :].unsqueeze(2), of.shape), ALU.pow).then_inc(rstd_ready, 1)

                powers(0, ms[:, :, 0:2 * FH], ms[:, :, 0:2 * FH])
                powers(1, ms[:, :, 2 * FH:HEADS], ms[:, :, 2 * FH:HEADS])
                for q in range(2):
                    for tt in range(TT):
                        powers(2 + 2 * q + tt, mv[:, tt, 1:2], rstd[:, tt:tt + 1])
                    for tt in range(TT):
                        pool.wait_ge(scaled, 4 * l + 2 * q + tt + 1)
                        g.tensor_tensor(x[:, tt, :], x[:, tt, :], lnp[:, 1, :], ALU.add).then_inc(x_done, 1)
                assert st.n == POOL_LAYER_STEPS, st.n

        @block.scalar
        def _(act):
            a = nc.scalar

            def evac_tr(n, dest):
                for b in (1, 3):
                    act.wait_ge(tr_bank, n + b + 1)
                    a.activation(dest[:, 2 * b:2 * b + 2, :].rearrange("p k t -> p (k t)"), ps[4 + b][:, :],
                                 ACT.Copy).then_inc(tr_act, 1)

            act.wait_ge(angles, 1)
            a.activation(sin[:, :, :], ang_s[:, :, :], ACT.Sin).then_inc(trig, 1)
            a.activation(cos[:, :, :], ang_c[:, :, :], ACT.Sin).then_inc(trig, 1)
            with act.Fori(0, DEPTH) as l:
                st = Steps(act, act_step, l * ACT_LAYER_STEPS)

                act.wait_ge(x_done, 4 * l + 2)
                with nc.allow_non_contiguous_dma(reason="small parameters"):
                    act.dma_start(cwr[:, :], A["conv_w"][bass.ds(l, 1)].rearrange("a j (c p) -> (a j c) p", p=P)).then_inc(par_in, 16)
                    for i, n in enumerate(("b_fox_f", "b_mlstm_i", "b_mlstm_f")):
                        act.dma_start(bias12[:, 4 * i:4 * i + 4], A[n][bass.ds(l, 1)].to_broadcast([P, 4])).then_inc(par_in, 16)
                    for n, lo, hi in (("g_fox", 0, 32), ("g_mlstm", 32, 96), ("g_moba", 96, 128)):
                        act.dma_start(gcol[lo:hi, :], A[n][bass.ds(l, 1)].rearrange("a (p k) -> (a p) k", k=KT)).then_inc(par_in, 16)
                    act.dma_start(wr[:, :, 0:NG], A["w_grp"][bass.ds(l, 1)].rearrange("a (p k) g -> (a p) k g", k=KT)).then_inc(par_in, 16)
                    act.dma_start(wr[:, :, NG:NG + NE], A["w_exp_router"][bass.ds(l, 1)].rearrange("a (p k) g e -> (a p) k (g e)", k=KT)).then_inc(par_in, 16)
                    act.dma_start(rb36[:, 0:NG], A["b_grp"][bass.ds(l, 1)].to_broadcast([P, NG])).then_inc(par_in, 16)
                    act.dma_start(rb36[:, NG:36], A["b_exp_router"][bass.ds(l, 1)].rearrange("a g e -> a (g e)").to_broadcast([P, NE])).then_inc(par_in, 16)

                act.sem_inc(par_issued, 1)
                evac_tr(12 * l, xT)

                def chunk(c):
                    act.wait_ge(proj, NCHUNK * l + c + 1)

                def finished(c):
                    chunk(c)
                    if c == 0:
                        a.activation(kf[:, :, :].rearrange("p c t -> p (c t)"), ps[1][:, :], ACT.Copy).then_inc(read_act, 1)
                    elif c == 1:
                        a.activation(v[:, 1, 0:256], ps[3][:, 0:256], ACT.Copy)
                        a.activation(z12[:, 1, :], ps[3][:, 256:268], ACT.Copy).then_inc(read_act, 1)
                        act.wait_ge(az_ready, l + 1)
                        st(a.activation(ls[:, :, :], az[:, :, :], ACT.Exp))
                        a.activation(az[:, :, :], ls[:, :, :], ACT.Ln, bias=1.0).then_inc(ln_ready, 1)
                    elif c == 2:
                        a.activation(bqk[:, 1, :], ps[1][:, :], ACT.Copy).then_inc(read_act, 1)
                    elif c == 3:
                        a.activation(v[:, 1, 768:1024], ps[3][:, 0:256], ACT.Copy).then_inc(read_act, 1)
                    elif c in (4, 5):
                        act.wait_ge(read_dve, 7 * l + DVE_READ[c])
                        u = qkm[:, MH * (c - 4):MH * (c - 3), :]
                        a.activation(u, u, ACT.Silu).then_inc(silu_done, 1)
                    elif c == 6:
                        a.activation(v[:, 1, 256:768], ps[1][:, :], ACT.Copy).then_inc(read_act, 1)
                    else:
                        a.activation(sg[:, 0, :], ps[2][:, :], ACT.Sigmoid)
                        a.activation(sg[:, 1, :], ps[3][:, :], ACT.Sigmoid).then_inc(read_act, 1)

                def attend(it):
                    if it < HEADS:
                        j, b = it, it % 2
                        act.wait_ge(maxed, HEADS * l + j + 1)
                        if kind(j) == "mlstm":
                            if mlstm_up_to(j) > 1:
                                act.wait_ge(prod_done, MLS * l + mlstm_up_to(j) - 1)
                            a.activation(Wm[:, 0:P], ps[7][:, 0:P], ACT.Exp, bias=nmx[:, j % 4, 0:1])
                            a.activation(em[:, j % 4, :], em[:, j % 4, :], ACT.Exp)
                            a.activation(Wm[:, P:3 * P], ps[7][:, P:3 * P], ACT.Exp, bias=nmx[:, j % 4, 1:2]).then_inc(wexp_done, 1)
                        else:
                            if j >= 2:
                                act.wait_ge(p_tr, HEADS * l + j - 1)
                            if j >= 4:
                                act.wait_ge(o_read, HEADS * l + j - 3)
                            a.activation(Pm[:, b, 0:P], ps[4][:, 0:P], ACT.Exp, bias=nmx[:, j % 4, 0:1],
                                         accum_out=stat[:, j % 4, 0:1])
                            a.activation(Pm[:, b, P:3 * P], ps[4][:, P:3 * P], ACT.Exp, bias=nmx[:, j % 4, 1:2],
                                         accum_out=stat[:, j % 4, 1:2]).then_inc(exp_done, 1)
                    if 1 <= it <= HEADS:
                        j = it - 1
                        act.wait_ge(p_tr, HEADS * l + j + 1)
                        if j >= 2:
                            act.wait_ge(pv_done, HEADS * l + j - 1)
                        a.activation(PT[:, j % 2, :], ps[5][:, 0:3 * P], ACT.Copy).then_inc(pt_ready, 1)
                    if it >= 3 and kind(it - 3) != "mlstm":
                        j = it - 3
                        act.wait_ge(o_read, HEADS * l + j + 1)
                        for tt in range(TT):
                            last = a.activation(junk[:, j % 4, tt, :], y[:, tt, column(j):column(j) + FD], ACT.Square,
                                                accum_out=ms[:, tt, j:j + 1])
                        last.then_inc(squared, 1)

                for what, n, part in mixer_order():
                    if what == "proj" and part == 3:
                        finished(n)
                    elif what == "att":
                        attend(n)
                    elif what == "ropek":
                        act.wait_ge(rope_tr, 2 * l + 2)
                        a.activation(kb[:, :, :].rearrange("p c t -> p (c t)"), ps[7][:, :], ACT.Copy).then_inc(kb_ready, 1)

                for tt in range(TT):
                    act.wait_ge(y_gated, 2 * l + tt + 1)
                    for j in range(2 * FH, HEADS):
                        last = a.activation(junk_m[:, tt, (j - 2 * FH) * MD:(j - 2 * FH + 1) * MD], y[:, tt, column(j):column(j) + MD], ACT.Square,
                                            accum_out=ms[:, tt, j:j + 1])
                last.then_inc(squared, 1)
                for b in (1, 3):
                    act.wait_ge(tr_bank, 4 + 12 * l + b + 1)
                    a.activation(yT[:, 2 * b, :], ps[4 + b][:, 0:SEQ], ACT.Copy, scale=gcol[:, 2 * b:2 * b + 1])
                    a.activation(yT[:, 2 * b + 1, :], ps[4 + b][:, SEQ:2 * SEQ], ACT.Copy,
                                 scale=gcol[:, 2 * b + 1:2 * b + 2]).then_inc(tr_act, 1)
                act.wait_ge(tr_bank, 4 + 12 * l + 4)
                act.dma_start(lnp[:, 0, :], A["ln1_g"][bass.ds(l, 1)].to_broadcast([P, D])).then_inc(ln_in, 16)
                act.dma_start(lnp[:, 1, :], A["ln1_b"][bass.ds(l, 1)].to_broadcast([P, D])).then_inc(ln_in, 16)

                def normalise(q):
                    for tt in range(TT):
                        act.wait_ge(stats_ready, 4 * l + 2 * q + tt + 1)
                        a.activation(x[:, tt, :], x[:, tt, :], ACT.Identity, bias=nmr[:, tt:tt + 1],
                                     scale=rstd[:, tt:tt + 1]).then_inc(normed, 1)

                normalise(0)
                act.wait_ge(x_done, 4 * l + 4)
                act.dma_start(lnp[:, 0, :], A["ln2_g"][bass.ds(l, 1)].to_broadcast([P, D])).then_inc(ln_in, 16)
                act.dma_start(lnp[:, 1, :], A["ln2_b"][bass.ds(l, 1)].to_broadcast([P, D])).then_inc(ln_in, 16)
                evac_tr(8 + 12 * l, xT)
                act.wait_ge(gdiff, l + 1)
                a.activation(e4[:, :, :], d4[:, :, :], ACT.Exp).then_inc(gexp, 1)
                act.wait_ge(vdiff, l + 1)
                a.activation(ex[:, :, :], dd[:, :, :], ACT.Exp).then_inc(vexp, 1)
                act.wait_ge(rows_ps, 2 * l + 2)
                a.activation(wrow.rearrange("p k t -> p (k t)"), ps[3][:, :], ACT.Copy).then_inc(rows_act, 1)

                act.wait_ge(table_ready, l + 1)
                act.sem_inc(act_held, 1)
                pairs = act.value_load(tabi[0:1, 40:41], min_val=NE // 2, max_val=(NE + EXTRA) // 2)
                done = act.value_load(tabi[0:1, 41:42], min_val=0, max_val=DEPTH * (NE + EXTRA) // 2)
                act.wait_ge(gathered, 2 * (done + l) + 2)
                a.activation(xg[:, 4:8, :].rearrange("p k s -> p (k s)"), ps[7][:, :], ACT.Copy).then_inc(xg_act, 1)
                with act.Fori(0, pairs) as i:
                    n = act.snap(done + i)
                    act.wait_ge(gate_used, n + 1)
                    a.activation(sil, ps[4][:, :], ACT.Silu).then_inc(silued, 1)
                    act.wait_ge(gathered, 2 * (n + l) + 4)
                    a.activation(xg[:, 4:8, :].rearrange("p k s -> p (k s)"), ps[7][:, :], ACT.Copy).then_inc(xg_act, 1)
                    act.wait_ge(down_used, n + 1)
                    a.activation(ym[:, CH:2 * CH], ps[7][:, :], ACT.Copy).then_inc(y_act, 1)
                normalise(1)
                assert st.n == ACT_LAYER_STEPS, st.n

        @block.vector
        def _(dve):
            d = nc.vector
            st = Steps(dve, dve_setup, 0)
            dve.wait_ge(pos_in, 16)
            dve.wait_ge(consts_ready, 1)
            d.tensor_scalar(base_e[:, :], iota_f[:, 0:NE], float(SLOTS), None, ALU.mult)
            st(d.tensor_copy(pos_f[:, :], pos_i[:, :]))
            st(d.tensor_tensor(ang[:, :, :], bc(pos_f[:, :].unsqueeze(2), [P, TT, ROPE_HALF]),
                               bc(inv[:, :].unsqueeze(1), [P, TT, ROPE_HALF]), ALU.mult))
            magic = 1.5 * 2.0 ** 23
            c1 = 6.28125
            c2 = float(int((2 * math.pi - c1) * 2 ** 20)) / 2 ** 20
            c3 = 2 * math.pi - c1 - c2
            st(d.tensor_scalar(kk[:, :, :], ang[:, :, :], 1 / (2 * math.pi), None, ALU.mult))
            st(d.tensor_scalar(kk[:, :, :], kk[:, :, :], magic, None, ALU.add))
            st(d.tensor_scalar(kk[:, :, :], kk[:, :, :], magic, None, ALU.subtract))
            for c in (c1, c2, c3):
                st(d.scalar_tensor_tensor(ang[:, :, :], kk[:, :, :], -c, ang[:, :, :], ALU.mult, ALU.add))
            pi = 3.1415925
            d.tensor_scalar(ang_s[:, :, :], ang[:, :, :], pi, -pi, ALU.min, ALU.max)
            st(d.tensor_scalar(ang_c[:, :, :], ang[:, :, :], math.pi / 2, None, ALU.add))
            st(d.tensor_scalar(kk[:, :, :], ang_c[:, :, :], math.pi, -2 * math.pi, ALU.is_gt, ALU.mult))
            st(d.tensor_tensor(ang_c[:, :, :], ang_c[:, :, :], kk[:, :, :], ALU.add))
            d.tensor_scalar(ang_c[:, :, :], ang_c[:, :, :], pi, -pi, ALU.min, ALU.max).then_inc(angles, 1)

            def evac_tr(n, dest):
                for b in (0, 2):
                    dve.wait_ge(tr_bank, n + b + 1)
                    d.tensor_copy(dest[:, 2 * b:2 * b + 2, :].rearrange("p k t -> p (k t)"), ps[4 + b][:, :]).then_inc(tr_dve, 1)

            with dve.Fori(0, DEPTH) as l:
                st = Steps(dve, dve_step, l * DVE_LAYER_STEPS)
                evac_tr(12 * l, xT)

                def chunk(c):
                    dve.wait_ge(proj, NCHUNK * l + c + 1)

                def conv(q):
                    for j in range(CONV - 1, -1, -1):
                        back = CONV - 1 - j
                        for c in range(MH):
                            u = ps[2 * q + c // 2][:, (c % 2) * SEQ:(c % 2 + 1) * SEQ]
                            w = cw[:, j * 8 + 4 * q + c:j * 8 + 4 * q + c + 1]
                            o = qkm[:, 4 * q + c, :]
                            if back == 0:
                                last = d.tensor_scalar(o, u, w, None, ALU.mult)
                            else:
                                last = d.scalar_tensor_tensor(o[:, back:], u[:, 0:SEQ - back], w, o[:, back:],
                                                              ALU.mult, ALU.add)
                        if j:
                            st(last)
                    last.then_inc(read_dve, 1)

                def finished(c):
                    if c < 7:
                        chunk(c)
                    if c == 0:
                        u = ps[0][:, :].rearrange("p (c t) -> p c t", c=2)
                        d.tensor_scalar(qf[0:64, 0:FH:2, :], u[0:64], FD ** -0.5, None, ALU.mult)
                        d.tensor_scalar(qf[64:128, 1:FH:2, :], u[64:128], FD ** -0.5, None, ALU.mult).then_inc(read_dve, 1)
                    elif c == 1:
                        d.tensor_copy(v[:, 0, 0:256], ps[2][:, 0:256])
                        d.tensor_copy(z12[:, 0, :], ps[2][:, 256:268]).then_inc(read_dve, 1)
                        gates()
                    elif c == 2:
                        d.tensor_copy(bqk[:, 0, :], ps[0][:, :]).then_inc(read_dve, 1)
                    elif c == 3:
                        d.tensor_copy(v[:, 0, 768:1024], ps[2][:, 0:256]).then_inc(read_dve, 1)
                    elif c in (4, 5):
                        conv(c - 4)
                    elif c == 6:
                        d.tensor_copy(v[:, 0, 256:768], ps[0][:, :]).then_inc(read_dve, 1)

                def gates():
                    dve.wait_ge(read_dve, 7 * l + 2)
                    dve.wait_ge(read_act, 6 * l + 2)
                    dve.wait_ge(par_in, 16 * PAR_DMAS * (l + 1))
                    st(d.tensor_tensor(z12[:, :, :], z12[:, :, :], bc(bias12[:, :].unsqueeze(1), [P, TT, 12]), ALU.add))
                    for h, c in ((0, 0), (4, 8)):
                        d.tensor_scalar(mn[:, :, h:h + 4], z12[:, :, c:c + 4], 0.0, None, ALU.min)
                        last = d.tensor_scalar(az[:, :, h:h + 4], z12[:, :, c:c + 4], 0.0, None, ALU.max)
                    st(last)
                    d.tensor_tensor(az[:, :, :], mn[:, :, :], az[:, :, :], ALU.subtract).then_inc(az_ready, 1)
                    dve.wait_ge(cw_tr, l + 1)
                    d.tensor_copy(cw[:, :], ps[7][:, 384:384 + CONV * 8]).then_inc(cw_ready, 1)
                    dve.wait_ge(cw_ready, l + 1)
                    dve.wait_ge(ln_ready, l + 1)
                    d.tensor_tensor(ls[:, :, :], mn[:, :, :], az[:, :, :], ALU.subtract).then_inc(ls_ready, 1)

                def attend(it):
                    if it < HEADS:
                        j, b = it, it % 2
                        dve.wait_ge(scored, HEADS * l + j + 1)
                        s = ps[7 if kind(j) == "mlstm" else 4]
                        d.tensor_reduce(nmx[:, j % 4, 0:1], s[:, 0:P], AXX, ALU.max, negate=True)
                        last = d.tensor_reduce(nmx[:, j % 4, 1:2], s[:, P:3 * P], AXX, ALU.max, negate=True)
                        if kind(j) != "mlstm":
                            last.then_inc(maxed, 1)
                        else:
                            st(last)
                            st(d.tensor_scalar(nmx[:, j % 4, :], nmx[:, j % 4, :], 0.0, None, ALU.min))
                            d.tensor_tensor(em[:, j % 4, :], nmx[:, j % 4, :], bcum[:, :, j - 2 * FH], ALU.subtract).then_inc(maxed, 1)
                            dve.wait_ge(wexp_done, MLS * l + mlstm_up_to(j))
                            dve.wait_ge(p_tr, HEADS * l + j - 1)
                            d.scalar_tensor_tensor(Pm[:, b, 0:P], ps[4][:, 0:P], 1.0, Wm[:, 0:P], ALU.mult, ALU.mult,
                                                   accum_out=stat[:, j % 4, 0:1])
                            d.scalar_tensor_tensor(Pm[:, b, P:3 * P], ps[4][:, P:3 * P], 1.0, Wm[:, P:3 * P], ALU.mult,
                                                   ALU.mult, accum_out=stat[:, j % 4, 1:2]).then_inc(prod_done, 1)
                    if it >= 2:
                        j = it - 2
                        if kind(j) == "mlstm":
                            dve.wait_ge(prod_done, MLS * l + mlstm_up_to(j))
                            st(d.scalar_tensor_tensor(rinv[:, j % 4, :], stat[:, j % 4, :], -1.0, stat[:, j % 4, :], ALU.mult, ALU.max))
                            st(d.tensor_tensor(rinv[:, j % 4, :], rinv[:, j % 4, :], em[:, j % 4, :], ALU.max))
                            st(d.reciprocal(rinv[:, j % 4, :], rinv[:, j % 4, :]))
                        else:
                            dve.wait_ge(exp_done, SOFT * l + soft_up_to(j))
                            st(d.reciprocal(rinv[:, j % 4, :], stat[:, j % 4, :]))
                        dve.wait_ge(pv_done, HEADS * l + j + 1)
                        w, c = width(j), column(j)
                        for tt in range(TT):
                            last = d.tensor_scalar(y[:, tt, c:c + w], ps[6][:, tt * w:(tt + 1) * w],
                                                   rinv[:, j % 4, tt:tt + 1], None, ALU.mult)
                        last.then_inc(o_read, 1)

                lo, mi, hi = FH * FD, FH * FD + MH * MD, D

                def mean_squares(h0, h1, w):
                    last = d.tensor_scalar(ms[:, :, h0:h1], ms[:, :, h0:h1], 1.0 / w, EPS, ALU.mult, ALU.add)
                    last.then_inc(var_ready, 1)

                def scale_heads(tt, a0, a1, w, h0):
                    u = y[:, tt, a0:a1].rearrange("p (h w) -> p h w", w=w)
                    return d.tensor_tensor(u, u, bc(ms[:, tt, h0:h0 + 4].unsqueeze(2), [P, 4, w]), ALU.mult)

                for what, n, part in mixer_order():
                    if what == "proj" and part == 3:
                        finished(n)
                    elif what == "att":
                        attend(n)
                        if n == 11:
                            dve.wait_ge(squared, 9 * l + 8)
                            mean_squares(0, 2 * FH, FD)
                        elif n == 12:
                            dve.wait_ge(rstd_ready, 6 * l + 1)
                            for tt in range(TT):
                                scale_heads(tt, 0, lo, FD, 0)
                                scale_heads(tt, mi, hi, FD, FH)
                    elif what == "cum":
                        dve.wait_ge(cum_done, l + 1)
                        u = ps[7][:, 0:TT * 8].rearrange("p (t g) -> p t g", t=TT)
                        d.tensor_scalar(gpad[:, :, 0:4], u[:, :, 0:4], -1.0, None, ALU.mult)
                        d.tensor_copy(bcum[:, :, :], u[:, :, 4:8])
                        d.tensor_tensor(gpad[:, :, 4:8], z12[:, :, 4:8], u[:, :, 4:8], ALU.subtract).then_inc(gpad_ready, 1)
                    elif what == "cat":
                        dve.wait_ge(cat_tr, l + 1)
                        d.tensor_copy(catT[:, :], ps[7][:, 0:SEQ]).then_inc(cat_ready, 1)
                    elif what == "ropeq":
                        dve.wait_ge(rope_tr, 2 * l + 1)
                        u = ps[7][:, :].rearrange("p (c t) -> p c t", c=2)
                        d.tensor_scalar(qb[0:64, 0:FH:2, :], u[0:64], FD ** -0.5, None, ALU.mult)
                        d.tensor_scalar(qb[64:128, 1:FH:2, :], u[64:128], FD ** -0.5, None, ALU.mult).then_inc(qb_ready, 1)

                dve.wait_ge(read_act, 6 * l + ACT_READ[7])
                dve.wait_ge(o_read, HEADS * (l + 1))
                for tt in range(TT):
                    d.tensor_tensor(y[:, tt, lo:mi], y[:, tt, lo:mi], sg[:, tt, :], ALU.mult).then_inc(y_gated, 1)
                dve.wait_ge(squared, 9 * l + 9)
                mean_squares(2 * FH, HEADS, MD)
                dve.wait_ge(rstd_ready, 6 * l + 2)
                for tt in range(TT):
                    scale_heads(tt, lo, mi, MD, 2 * FH).then_inc(y_ready, 1)
                for b in (0, 2):
                    dve.wait_ge(tr_bank, 4 + 12 * l + b + 1)
                    d.tensor_scalar(yT[:, 2 * b, :], ps[4 + b][:, 0:SEQ], gcol[:, 2 * b:2 * b + 1], None, ALU.mult)
                    d.tensor_scalar(yT[:, 2 * b + 1, :], ps[4 + b][:, SEQ:2 * SEQ], gcol[:, 2 * b + 1:2 * b + 2],
                                    None, ALU.mult).then_inc(tr_dve, 1)

                def layer_norm(q, ready):
                    for half, tt in ((0, 0), (0, 1), (1, 0), (1, 1)):
                        ready(tt, half)
                        u = x[:, tt, half * CH:(half + 1) * CH]
                        st(d.scalar_tensor_tensor(u, u, ALPHA, ps[2 * half + tt][:, :], ALU.mult, ALU.add))
                        last = d.bn_stats(bns[:, tt, half, :], u)
                        if half == 1:
                            st(last)
                            dve.sem_inc(dve_held, 1)
                            st(d.bn_aggr(mv[:, tt, :], bns[:, tt, :, :].rearrange("p a b -> p (a b)")))
                            d.tensor_scalar(mv[:, tt, 1:2], mv[:, tt, 1:2], EPS, None, ALU.add).then_inc(var_ready, 1)
                            dve.wait_ge(rstd_ready, 6 * l + 2 * q + tt + 3)
                            d.scalar_tensor_tensor(nmr[:, tt:tt + 1], mv[:, tt, 0:1], -1.0, rstd[:, tt:tt + 1],
                                                   ALU.mult, ALU.mult).then_inc(stats_ready, 1)
                    for tt in range(TT):
                        dve.wait_ge(normed, 4 * l + 2 * q + tt + 1)
                        if tt == 0:
                            dve.wait_ge(ln_in, 64 * l + 32 * q + 32)
                        d.tensor_tensor(x[:, tt, :], x[:, tt, :], lnp[:, 0, :], ALU.mult).then_inc(scaled, 1)

                def mixed(tt, half):
                    if tt == 0:
                        dve.wait_ge(mix_half, 2 * l + half + 1)
                    else:
                        dve.wait_ge(proj, NCHUNK * l + 9 + half)

                layer_norm(0, mixed)
                evac_tr(8 + 12 * l, xT)

                dve.wait_ge(logits, l + 1)
                d.tensor_copy(lgT, ps[0][0:NG + NE, 0:SEQ]).then_inc(lgT_ready, 1)
                dve.wait_ge(logits_tr, l + 1)
                st(d.tensor_tensor(lg[:, :, :], ps[1][:, 0:128].rearrange("p (t n) -> p t n", t=TT)[:, :, 0:36],
                                   bc(rb36[:, :].unsqueeze(1), [P, TT, 36]), ALU.add))
                st(d.tensor_reduce(gmx[:, :, :], lg[:, :, 0:NG], AXX, ALU.max))
                d.tensor_tensor(d4[:, :, :], lg[:, :, 0:NG], bc(gmx[:, :, :], [P, TT, NG]), ALU.subtract).then_inc(gdiff, 1)
                st(d.tensor_tensor(g4[:, :, :], lg[:, :, 0:NG], bc(gmx[:, :, :], [P, TT, NG]), ALU.is_equal))
                st(d.tensor_tensor(g4[:, :, :], g4[:, :, :], bc(desc[:, 0:NG].unsqueeze(1), [P, TT, NG]), ALU.mult))
                st(d.tensor_reduce(r1[:, :, :], g4[:, :, :], AXX, ALU.max))
                st(d.tensor_tensor(g4[:, :, :], g4[:, :, :], bc(r1[:, :, :], [P, TT, NG]), ALU.is_equal))
                st(d.tensor_scalar(g4[:, :, :], g4[:, :, :], -1.0, BIG, ALU.add, ALU.mult))
                for tt in range(TT):
                    last = d.tensor_tensor(emk[:, tt, :].rearrange("p (g e) -> p g e", g=NG),
                                           lg[:, tt, NG:36].rearrange("p (g e) -> p g e", g=NG),
                                           bc(g4[:, tt, :].unsqueeze(2), [P, NG, EG]), ALU.add)
                st(last)
                for k in range(2):
                    st(d.tensor_reduce(v12[:, k], emk[:, :, :], AXX, ALU.max))
                    st(d.tensor_tensor(eq[:, :, :], emk[:, :, :], bc(v12[:, k], [P, TT, NE]), ALU.is_equal))
                    st(d.tensor_tensor(eq[:, :, :], eq[:, :, :], bc(desc[:, :].unsqueeze(1), [P, TT, NE]), ALU.mult))
                    st(d.tensor_reduce(r1[:, :, :], eq[:, :, :], AXX, ALU.max))
                    st(d.tensor_tensor(oh[:, k], bc(desc[:, :].unsqueeze(1), [P, TT, NE]), bc(r1[:, :, :], [P, TT, NE]), ALU.is_equal))
                    if k == 0:
                        st(d.scalar_tensor_tensor(emk[:, :, :], oh[:, 0], -3 * BIG, emk[:, :, :], ALU.mult, ALU.add))
                d.tensor_tensor(mall[:, :, :], oh[:, 0], oh[:, 1], ALU.add).then_inc(masks_ready, 1)
                d.tensor_tensor(dd[:, :, :], v12[:, 1], v12[:, 0], ALU.subtract).then_inc(vdiff, 1)
                dve.wait_ge(gexp, l + 1)
                st(d.tensor_reduce(s4[:, :, :], e4[:, :, :], AXX, ALU.add))
                dve.wait_ge(vexp, l + 1)
                st(d.tensor_scalar(r1[:, :, :], ex[:, :, :], 1.0, None, ALU.add))
                st(d.tensor_tensor(s4[:, :, :], s4[:, :, :], r1[:, :, :], ALU.mult))
                st(d.reciprocal(wgt[:, 0], s4[:, :, :]))
                d.tensor_tensor(wgt[:, 1], wgt[:, 0], ex[:, :, :], ALU.mult)
                dve.wait_ge(ranks, l + 1)
                cnt = ps[1][0:NE, 128:256]
                st(d.tensor_scalar(novt[:, :], cnt, float(SLOTS), None, ALU.is_gt))
                st(d.scalar_tensor_tensor(novt[:, :], cnt, 2.0 * SLOTS, novt[:, :], ALU.is_gt, ALU.add))
                d.scalar_tensor_tensor(novt[:, :], cnt, 3.0 * SLOTS, novt[:, :], ALU.is_gt, ALU.add).then_inc(novt_ready, 1)
                dve.wait_ge(starts_ps, l + 1)
                st(d.tensor_copy(starts[:, :], ps[2][:, 0:2 * NE + 1]))
                st(d.tensor_scalar(delta[:, :], starts[:, 0:NE], float(NE - 1), float(SLOTS), ALU.add, ALU.mult))
                st(d.tensor_tensor(delta[:, :], delta[:, :], base_e[:, :], ALU.subtract))
                rank = ps[1][:, 0:TT * NE].rearrange("p (t e) -> p t e", t=TT)
                st(d.scalar_tensor_tensor(dall[:, :, :], rank, float(SLOTS), bc(delta[:, :].unsqueeze(1), [P, TT, NE]),
                                          ALU.is_ge, ALU.mult))
                st(d.tensor_tensor(dall[:, :, :], dall[:, :, :], bc(base_e[:, :].unsqueeze(1), [P, TT, NE]), ALU.add))
                st(d.tensor_tensor(dall[:, :, :], dall[:, :, :], rank, ALU.add))
                st(d.tensor_tensor(eq[:, :, :], oh[:, 0], dall[:, :, :], ALU.mult))
                st(d.tensor_reduce(dst[:, 0], eq[:, :, :], AXX, ALU.add))
                st(d.tensor_tensor(eq[:, :, :], oh[:, 1], dall[:, :, :], ALU.mult))
                d.tensor_reduce(dst[:, 1], eq[:, :, :], AXX, ALU.add).then_inc(dst_ready, 1)
                dve.wait_ge(dst_ready, l + 1)
                st(d.tensor_tensor(cmp8[:, :, :], bc(starts[0:1, NE:2 * NE].unsqueeze(1), [1, EXTRA, NE]),
                                   iot8[:, :].rearrange("p (b e) -> p b e", b=EXTRA), ALU.is_le))
                st(d.tensor_reduce(tabf[:, NE:NE + EXTRA], cmp8[:, :, :], AXX, ALU.add))
                st(d.tensor_scalar(tabf[:, NE:NE + EXTRA], tabf[:, NE:NE + EXTRA], float(NE - 1), None, ALU.min))
                d.tensor_copy(tabf[:, 0:NE], iota_f[0:1, 0:NE])
                d.tensor_copy(tabf[:, 41:42], total[:, :])
                st(d.tensor_scalar(cmp8[:, 0, 0:4], tabx[:, :], starts[0:1, 2 * NE:2 * NE + 1], None, ALU.is_lt))
                st(d.tensor_reduce(tabf[:, 40:41], cmp8[:, 0, 0:4], AXX, ALU.add))
                st(d.tensor_scalar(tabf[:, 40:41], tabf[:, 40:41], float(NE // 2), None, ALU.add))
                d.tensor_tensor(total[:, :], total[:, :], tabf[:, 40:41], ALU.add)
                d.tensor_copy(tabi[:, 0:42], tabf[:, 0:42]).then_inc(table_ready, 1)
                d.tensor_copy(dcur[:, :, :, :], dst[:, :, :, :])
                st(d.tensor_copy(pcur[:, :], pcol[:, :]))
                dve.wait_ge(rows_ps, 2 * l + 1)
                d.tensor_copy(drow.rearrange("p k t -> p (k t)"), ps[2][:, :]).then_inc(rows_dve, 1)

                dve.wait_ge(table_ready, l + 1)
                dve.sem_inc(dve_held, 1)
                pairs = dve.value_load(tabi[0:1, 40:41], min_val=NE // 2, max_val=(NE + EXTRA) // 2)
                done = dve.value_load(tabi[0:1, 41:42], min_val=0, max_val=DEPTH * (NE + EXTRA) // 2)

                def one_hots(steps, made):
                    for tt in range(TT):
                        last = d.tensor_scalar(oneh[:, tt, :], iota_f[:, :], dcur[:, 0, tt, :], None, ALU.is_equal)
                    steps(last)
                    for tt in range(TT):
                        last = d.scalar_tensor_tensor(oneh[:, tt, :], iota_f[:, :], dcur[:, 1, tt, :], oneh[:, tt, :],
                                                      ALU.is_equal, ALU.add)
                    last.then_inc(oneh_ready, 1)
                    dve.wait_ge(oneh_ready, made)
                    steps(d.tensor_scalar(dcur[:, :, :, :], dcur[:, :, :, :], float(2 * SLOTS), None, ALU.subtract))

                def rows_in():
                    d.tensor_copy(xg[:, 0:4, :].rearrange("p k s -> p (k s)"), ps[6][:, :]).then_inc(xg_dve, 1)

                one_hots(st, done + l + 1)
                d.memset(wt, 0.0).then_inc(wt_ready, 1)
                d.memset(ym[:, 0:CH], 0.0).then_inc(y_dve, 1)
                d.memset(ym[:, CH:2 * CH], 0.0).then_inc(y_act, 1)
                dve.wait_ge(gathered, 2 * (done + l) + 1)
                rows_in()
                dve.wait_ge(rows_act, l + 1)
                dve.sem_inc(dve_held, 1)
                with dve.Fori(0, pairs) as i:
                    n = dve.snap(done + i)
                    sp_ = Steps(dve, dve_pair, n * DVE_PAIR_STEPS)
                    dve.wait_ge(gathered, 2 * (n + l) + 2)
                    one_hots(sp_, n + l + 2)
                    dve.wait_ge(combined, n + 1)
                    d.scalar_tensor_tensor(wt, drow[:, 0, :], pcur[:, :], wrow[:, 0, :], ALU.is_equal, ALU.mult)
                    sp_(d.scalar_tensor_tensor(w2, drow[:, 1, :], pcur[:, :], wrow[:, 1, :], ALU.is_equal, ALU.mult))
                    d.tensor_tensor(wt, wt, w2, ALU.add).then_inc(wt_ready, 1)
                    sp_(d.tensor_scalar(pcur[:, :], pcur[:, :], float(2 * SLOTS), None, ALU.add))
                    dve.wait_ge(up_used, n + 1)
                    dve.wait_ge(silued, n + 1)
                    d.tensor_tensor(hid, sil, ps[5][:, :], ALU.mult).then_inc(h_ready, 1)
                    dve.wait_ge(gathered, 2 * (n + l) + 3)
                    rows_in()
                    dve.wait_ge(h_tr, n + 1)
                    d.tensor_copy(hT.rearrange("p k s -> p (k s)"), ps[4][:, :]).then_inc(hT_ready, 1)
                    dve.wait_ge(down_used, n + 1)
                    d.tensor_copy(ym[:, 0:CH], ps[6][:, :]).then_inc(y_dve, 1)
                    assert sp_.n == DVE_PAIR_STEPS, sp_.n
                layer_norm(1, lambda tt, half: dve.wait_ge(acc_done, 2 * l + tt + 1))
                assert st.n == DVE_LAYER_STEPS, st.n

        @block.tensor
        def _(pe):
            t = nc.tensor

            def transpose_rows(src, ready, n):
                for tt in range(TT):
                    pe.wait_ge(ready, n + tt)
                    for k in range(KT):
                        last = t.transpose(ps[4 + k // 2][:, (k % 2) * SEQ + tt * P:(k % 2) * SEQ + (tt + 1) * P],
                                           src[:, tt, k:D:KT], ident[:, :])
                        if tt == TT - 1 and k % 2:
                            last.then_inc(tr_bank, 1)

            pe.wait_ge(consts_ready, 1)
            pe.wait_ge(x_in, 16)
            with pe.Fori(0, DEPTH) as l:
                def project(c, part):
                    if part == 0:
                        pe.wait_ge(chunk_in[c], 16 * (l + 1) * (len(COLS[c]) if c < 8 else 1))
                        if 2 <= c < 8:
                            pe.wait_ge(read_dve, 7 * l + DVE_READ[c - 2])
                            pe.wait_ge(read_act, 6 * l + ACT_READ[c - 2])
                    w = slot(SLOT_OF[c])
                    b0 = 2 * (c % 2)
                    if c in (0, 4, 5):
                        j = part
                        for k in range(KT):
                            last = t.matmul(ps[b0 + j // 2][:, (j % 2) * SEQ:(j % 2 + 1) * SEQ],
                                            w[:, k, j * P:(j + 1) * P], xT[:, k, :], start=(k == 0), stop=(k == KT - 1))
                    else:
                        n = sum(b - a for a, b in COLS[c]) if c < 8 else CH
                        src = xT if c < 8 else yT
                        tt = part // 2
                        for k in range((part % 2) * KT // 2, (part % 2 + 1) * KT // 2):
                            last = t.matmul(ps[b0 + tt][:, 0:n], src[:, k, tt * P:(tt + 1) * P], w[:, k, 0:n],
                                            start=(k == 0), stop=(k == KT - 1))
                    if part == 3:
                        last.then_inc(proj, 1)
                    elif part == 1 and c >= 8:
                        last.then_inc(mix_half, 1)

                transpose_rows(x, x_done, 4 * l + 1)
                pe.wait_ge(tr_dve, 6 * l + 2)
                pe.wait_ge(tr_act, 6 * l + 2)
                def masked(dest, mm):
                    for tt in range(TT):
                        o = dest[:, 0:P] if tt == 0 else dest[:, P:3 * P]
                        mm(tt, o, (tt + 1) * P)
                        last = t.matmul(dest[:, 2 * tt * P:(2 * tt + 1) * P], identb[:, :], maskb[:, :], start=False, stop=True)
                    return last

                def scores(j):
                    h = j % FH
                    q, k = {"fox": (qf[:, h], kf[:, h // 2]), "mlstm": (qkm[:, h], qkm[:, MH + h]),
                            "moba": (qb[:, h], kb[:, h // 2])}[kind(j)]
                    row = h if kind(j) == "fox" else 4 + h
                    if j == 0:
                        pe.wait_ge(cat_ready, l + 1)
                    elif j == FH:
                        pe.wait_ge(qb_ready, l + 1)
                        pe.wait_ge(kb_ready, l + 1)
                    elif j == 2 * FH:
                        pe.wait_ge(kscaled, l + 1)
                    if j >= 1:
                        if kind(j - 1) == "mlstm":
                            pe.wait_ge(prod_done, MLS * l + mlstm_up_to(j - 1))
                        else:
                            pe.wait_ge(exp_done, SOFT * l + soft_up_to(j - 1))

                    def qk(tt, o, n, stop=False):
                        t.matmul(o, q[:, tt * P:(tt + 1) * P], k[:, 0:n], start=True, stop=stop)

                    def cum(tt, o, n, start=False):
                        t.matmul(o, bc(ident[:, row:row + 1], [P, P]), catT[:, 0:n], start=start, stop=False)

                    if kind(j) == "fox":
                        last = masked(ps[4], lambda tt, o, n: (qk(tt, o, n), cum(tt, o, n)))
                    elif kind(j) == "moba":
                        last = masked(ps[4], qk)
                    else:
                        for tt in range(TT):
                            qk(tt, ps[4][:, 0:P] if tt == 0 else ps[4][:, P:3 * P], (tt + 1) * P, True)
                        last = masked(ps[7], lambda tt, o, n: cum(tt, o, n, True))
                    last.then_inc(scored, 1)

                def attend(it):
                    if it < HEADS:
                        scores(it)
                    if 1 <= it <= HEADS:
                        j, b = it - 1, (it - 1) % 2
                        if kind(j) == "mlstm":
                            pe.wait_ge(prod_done, MLS * l + mlstm_up_to(j))
                        else:
                            pe.wait_ge(exp_done, SOFT * l + soft_up_to(j))
                        if j >= 1:
                            pe.wait_ge(pt_ready, HEADS * l + j)
                        for q in range(3):
                            last = t.transpose(ps[5][:, q * P:(q + 1) * P], Pm[:, b, q * P:(q + 1) * P], ident[:, :])
                        last.then_inc(p_tr, 1)
                    if it >= 2:
                        j, b = it - 2, it % 2
                        w, c = width(j), column(j)
                        pe.wait_ge(pt_ready, HEADS * l + j + 1)
                        if j == 0:
                            pe.wait_ge(read_act, 6 * l + ACT_READ[1])
                        elif j == FH:
                            pe.wait_ge(read_dve, 7 * l + DVE_READ[3])
                            pe.wait_ge(read_act, 6 * l + ACT_READ[3])
                        elif j == 2 * FH:
                            pe.wait_ge(read_dve, 7 * l + DVE_READ[6])
                            pe.wait_ge(read_act, 6 * l + ACT_READ[6])
                        if j >= 1:
                            pe.wait_ge(o_read, HEADS * l + j)
                        t.matmul(ps[6][:, 0:w], PT[:, b, 0:P], v[:, 0, c:c + w], start=True, stop=True)
                        t.matmul(ps[6][:, w:2 * w], PT[:, b, P:2 * P], v[:, 0, c:c + w], start=True, stop=False)
                        t.matmul(ps[6][:, w:2 * w], PT[:, b, 2 * P:3 * P], v[:, 1, c:c + w], start=False,
                                 stop=True).then_inc(pv_done, 1)

                def rope_blocks(o):
                    for c in range(2):
                        for tt in range(TT):
                            last = t.transpose(ps[7][:, c * SEQ + tt * P:c * SEQ + (tt + 1) * P],
                                               bqk[:, tt, o + c * P:o + (c + 1) * P], ident[:, :])
                    last.then_inc(rope_tr, 1)

                for what, n, part in mixer_order():
                    if what == "proj":
                        project(n, part)
                        if (n, part) == (0, 3):
                            pe.wait_ge(par_in, 16 * PAR_DMAS * (l + 1))
                            t.matmul(ps[7][:, 384:384 + CONV * 8], cwr[:, :], ident[0:CONV * 8, 0:CONV * 8],
                                     start=True, stop=True).then_inc(cw_tr, 1)
                    elif what == "att":
                        attend(n)
                    elif what == "cum":
                        pe.wait_ge(ls_ready, l + 1)
                        t.matmul(ps[7][:, 0:8], tri_incl[:, :], ls[:, 0, :], start=True, stop=True)
                        t.matmul(ps[7][:, 8:16], tri_incl[:, :], ls[:, 1, :], start=True, stop=False)
                        t.matmul(ps[7][:, 8:16], ones[:, :], ls[:, 0, :], start=False, stop=True).then_inc(cum_done, 1)
                    elif what == "cat":
                        pe.wait_ge(gpad_ready, l + 1)
                        for tt in range(TT):
                            last = t.transpose(ps[7][:, tt * P:(tt + 1) * P], gpad[:, tt, :], ident[:, :])
                        last.then_inc(cat_tr, 1)
                    elif what == "ropeq":
                        pe.wait_ge(roped, 2 * l + 2)
                        pe.wait_ge(cat_ready, l + 1)
                        rope_blocks(0)
                    elif what == "ropek":
                        pe.wait_ge(qb_ready, l + 1)
                        rope_blocks(2 * P)

                transpose_rows(y, y_ready, 2 * l + 1)
                pe.wait_ge(tr_dve, 6 * l + 4)
                pe.wait_ge(tr_act, 6 * l + 4)
                for c in (8, 9):
                    for part in range(4):
                        project(c, part)
                transpose_rows(x, x_done, 4 * l + 3)
                pe.wait_ge(tr_dve, 6 * l + 6)
                pe.wait_ge(tr_act, 6 * l + 6)
                for k in range(KT):
                    last = t.matmul(ps[0][0:NG + NE, 0:SEQ], wr[:, k, :], xT[:, k, :], start=(k == 0), stop=(k == KT - 1))
                last.then_inc(logits, 1)
                pe.wait_ge(lgT_ready, l + 1)
                pe.sem_inc(pe_held, 1)
                for tt in range(TT):
                    last = t.transpose(ps[1][:, tt * 64:tt * 64 + NG + NE], lgT[:, tt * P:(tt + 1) * P],
                                       ident[0:NG + NE, 0:NG + NE])
                last.then_inc(logits_tr, 1)
                pe.wait_ge(masks_ready, l + 1)
                t.matmul(ps[1][:, 0:NE], tri_strict[:, :], mall[:, 0, :], start=True, stop=True)
                t.matmul(ps[1][:, NE:2 * NE], tri_strict[:, :], mall[:, 1, :], start=True, stop=False)
                t.matmul(ps[1][:, NE:2 * NE], ones[:, :], mall[:, 0, :], start=False, stop=True)
                t.matmul(ps[1][0:NE, 128:256], mall[:, 0, :], ones[:, :], start=True, stop=False)
                t.matmul(ps[1][0:NE, 128:256], mall[:, 1, :], ones[:, :], start=False, stop=True).then_inc(ranks, 1)
                pe.wait_ge(novt_ready, l + 1)
                t.matmul(ps[2][:, 0:2 * NE + 1], novt[:, :], tri65[:, :], start=True, stop=True).then_inc(starts_ps, 1)
                pe.wait_ge(dst_ready, l + 1)
                for bank, col in ((2, dst), (3, wgt)):
                    for k in range(2):
                        for tt in range(TT):
                            last = t.matmul(ps[bank][:, k * SEQ + tt * P:k * SEQ + (tt + 1) * P], bc(col[:, k, tt, :], [P, P]),
                                            ident[:, :], start=True, stop=True)
                    last.then_inc(rows_ps, 1)

                pe.wait_ge(table_ready, l + 1)
                pe.sem_inc(pe_held, 1)
                pairs = pe.value_load(tabi[0:1, 40:41], min_val=NE // 2, max_val=(NE + EXTRA) // 2)
                done = pe.value_load(tabi[0:1, 41:42], min_val=0, max_val=DEPTH * (NE + EXTRA) // 2)
                pe.wait_ge(rows_dve, l + 1)
                pe.wait_ge(rows_act, l + 1)
                for b in range(4):
                    t.matmul(ps[b][:, :], zerob[:, :], bc(zerob[:, 0:1], [P, CH]), start=True, stop=False)

                def gather():
                    for k in range(KT):
                        for tt in range(TT):
                            last = t.matmul(ps[6 + k // 4][:, (k % 4) * P:(k % 4 + 1) * P], x[:, tt, k:D:KT], oneh[:, tt, :],
                                            start=(tt == 0), stop=(tt == TT - 1))
                        if k % 4 == 3:
                            last.then_inc(gathered, 1)

                def combine(last_pair=False):
                    for tt in range(TT):
                        for half in range(2):
                            last = t.matmul(ps[2 * half + tt][:, :], wt[:, tt * P:(tt + 1) * P], ym[:, half * CH:(half + 1) * CH],
                                            start=False, stop=last_pair)
                        if last_pair:
                            last.then_inc(acc_done, 1)
                    if not last_pair:
                        last.then_inc(combined, 1)

                pe.wait_ge(oneh_ready, done + l + 1)
                gather()
                with pe.Fori(0, pairs) as i:
                    n = pe.snap(done + i)
                    nl = pe.snap(n + l)
                    pe.wait_ge(xg_dve, nl + 1)
                    pe.wait_ge(xg_act, nl + 1)
                    pe.wait_ge(gate_in, n * 32 + 32)
                    for k in range(KT):
                        for q in range(2):
                            last = t.matmul(ps[4][64 * q:64 * q + 64, :], xg[:, k, 64 * q:64 * q + 64], slot(q)[:, k, :],
                                            start=(k == 0), stop=(k == KT - 1))
                    last.then_inc(gate_used, 1)
                    pe.wait_ge(y_dve, nl + 1)
                    pe.wait_ge(y_act, nl + 1)
                    pe.wait_ge(wt_ready, nl + 1)
                    combine()
                    pe.wait_ge(up_in, n * 32 + 32)
                    for k in range(KT):
                        for q in range(2):
                            last = t.matmul(ps[5][64 * q:64 * q + 64, :], xg[:, k, 64 * q:64 * q + 64], slot(2 + q)[:, k, :],
                                            start=(k == 0), stop=(k == KT - 1))
                    last.then_inc(up_used, 1)
                    pe.wait_ge(oneh_ready, nl + 2)
                    gather()
                    pe.wait_ge(h_ready, n + 1)
                    for f in range(FT):
                        last = t.transpose(ps[4][:, f * P:(f + 1) * P], hid[:, f:DE:FT], ident[:, :])
                    last.then_inc(h_tr, 1)
                    pe.wait_ge(hT_ready, n + 1)
                    pe.wait_ge(xg_dve, nl + 2)
                    pe.wait_ge(xg_act, nl + 2)
                    pe.wait_ge(down_in, n * 32 + 32)
                    for f in range(FT):
                        for half in range(2):
                            for q in range(2):
                                w = ring[:, 4 + q, :].rearrange("p (f n) -> p f n", f=FT)
                                last = t.matmul(ps[6 + half][64 * q:64 * q + 64, :], hT[:, f, 64 * q:64 * q + 64],
                                                w[:, f, half * CH:(half + 1) * CH], start=(f == 0), stop=(f == FT - 1))
                    last.then_inc(down_used, 1)
                end = pe.snap(done + pairs)
                pe.wait_ge(y_dve, end + l + 1)
                pe.wait_ge(y_act, end + l + 1)
                pe.wait_ge(wt_ready, end + l + 1)
                combine(True)


_INS = ['x', 'positions', 'w_in', 'b_fox_f', 'b_mlstm_i', 'b_mlstm_f', 'conv_w', 'g_fox', 'g_mlstm', 'g_moba',
        'w_out', 'ln1_g', 'ln1_b', 'w_grp', 'b_grp', 'w_exp_router', 'b_exp_router', 'w_gate', 'w_up', 'w_down',
        'ln2_g', 'ln2_b']


def kernel(**inputs):
    import numpy as _np
    import concourse.bacc as _bacc
    from concourse import mybir as _mybir
    from concourse.bass_utils import run_bass_kernel_spmd as _run

    nc = _bacc.Bacc("TRN2", target_bir_lowering=False, num_devices=1)
    arrays, args = {}, {}
    for name in _INS:
        a = _np.ascontiguousarray(inputs[name])
        arrays[f"in_{name}_dram"] = a
        args[name] = nc.dram_tensor(f"in_{name}_dram", a.shape, _mybir.dt.from_np(a.dtype), kind="ExternalInput").ap()
    out = nc.dram_tensor("out_0_dram", (1, SEQ, D), _mybir.dt.float32, kind="ExternalOutput").ap()
    build(nc, args, out)
    r = _run(nc, [arrays], core_ids=[0])
    return r.results[0]["out_0_dram"]
```

```python
from contextlib import ExitStack
import math

import concourse.bass as bass
from concourse import mybir

ALU = mybir.AluOpType
ACT = mybir.ActivationFunctionType
F32 = mybir.dt.float32
BF16 = mybir.dt.bfloat16
I32 = mybir.dt.int32
AXX = mybir.AxisListType.X

P = 128
SEQ, D, DEPTH = 256, 1024, 2
TT = SEQ // P
KT = D // P
FH, FD = 4, 64
MH, MD = 4, 128
CONV = 4
ROPE_HALF = 8
NG, EG, NE, DE = 4, 8, 32, 512
FT = DE // P
SLOTS = 64
EXTRA = 8
ALPHA = (2 * DEPTH) ** 0.25
EPS = 1e-5
BIG = 1e30
CH = 512
NCHUNK = 10
HEADS = 2 * FH + MH
SLOT_OF = [0, 1, 2, 3, 4, 5, 6, 7, 6, 7]
COLS = [[(0, 512)], [(512, 772), (2308, 2316)], [(2828, 3340)], [(3340, 3596)], [(772, 1284)],
        [(1284, 1796)], [(1796, 2308)], [(2316, 2828)]]
DVE_READ = [1, 2, 3, 4, 5, 6, 7, 7]
ACT_READ = [1, 2, 3, 4, 4, 4, 5, 6]
PAR_DMAS = 11


class Steps:

    def __init__(self, eng, sem, base):
        self.eng, self.sem, self.base, self.n = eng, sem, base, 0

    def __call__(self, ins):
        self.n += 1
        ins.then_inc(self.sem, 1)
        self.eng.wait_ge(self.sem, self.base + self.n)


def kind(j):
    return "fox" if j < FH else "moba" if j < 2 * FH else "mlstm"


def width(j):
    return MD if kind(j) == "mlstm" else FD


def column(j):
    if kind(j) == "fox":
        return j * FD
    if kind(j) == "mlstm":
        return FH * FD + (j - 2 * FH) * MD
    return FH * FD + MH * MD + (j - FH) * FD


def unit(r, part):
    return (3 * r + ("gate", "up", "down").index(part)) % 4


def soft_up_to(j):
    return min(j + 1, 2 * FH)


def mlstm_up_to(j):
    return max(j + 1 - 2 * FH, 0)


def mixer_order():
    between = {(2, 1): ["cum"], (2, 3): ["cat"], (3, 1): [0], (3, 3): [1], (4, 0): [2], (4, 1): ["ropeq", 3],
               (4, 2): ["ropek"], (4, 3): [4], (5, 0): [5], (5, 1): [6], (5, 2): [7], (6, 2): [8], (6, 3): [9],
               (7, 0): [10], (7, 1): [11], (7, 2): [12], (7, 3): [13]}
    taps = {4: (3,), 5: (2,), 6: (1,), 7: (0,)}
    for c in range(8):
        for part in range(4):
            yield "proj", c, part
            for e in between.get((c, part), ()):
                yield ("att", e, 0) if isinstance(e, int) else (e, 0, 0)
                for tap in taps.get(e, ()):
                    yield "conv", 0, tap
        if c == 5:
            for tap in range(CONV - 1, -1, -1):
                yield "conv", 1, tap


WARM_START, WARM_NORM, WARM_COPY, WARM_CHOOSE, WARM_SLOTS = 20, 24, 8, 8, 9
SOFT, MLS = soft_up_to(HEADS - 1), mlstm_up_to(HEADS - 1)
DVE_LAYER_STEPS = 86
DVE_PAIR_STEPS = 4
ACT_LAYER_STEPS = 1
POOL_LAYER_STEPS = 2


def build(nc, A, out):
    ctx = ExitStack()
    with ctx:
        def sb(name, shape, dt=F32):
            return ctx.enter_context(nc.sbuf_tensor(name, shape, dt))

        def sem(name):
            return ctx.enter_context(nc.semaphore(name))

        ring = sb("ring", [P, 8, KT * CH])
        x = sb("xres", [P, TT, D])
        bufa = sb("bufa", [P, 2048])
        bufb = sb("bufb", [P, 2048])
        bufc = sb("bufc", [P, 2048])
        bufd = sb("bufd", [P, 1024])
        bufe = sb("bufe", [P, 1024])
        lnp = sb("lnp", [P, 2, D])
        qf = sb("qf", [P, FH, SEQ])
        kf = sb("kf", [P, FH // 2, SEQ])
        qb = sb("qb", [P, FH, SEQ])
        kb = sb("kb", [P, FH // 2, SEQ])
        Pm = sb("Pm", [P, 2, 3 * P])
        Wm = sb("Wm", [P, 3 * P])
        catT = sb("catT", [P, SEQ])
        gpad = sb("gpad", [P, TT, P])
        ident = sb("ident", [P, P])
        identb = sb("identb", [P, P], BF16)
        maskb = sb("maskb", [P, P], BF16)
        tri_incl = sb("tri_incl", [P, P])
        tri_strict = sb("tri_strict", [P, P])
        alpha_i = sb("alpha_i", [P, P])
        iota_f = sb("iota_f", [P, P])
        desc = sb("desc", [P, NE])
        base_e = sb("base_e", [P, NE])
        tri65 = sb("tri65", [NE, 2 * NE + 1])
        iot8 = sb("iot8", [1, EXTRA * NE])
        pcol_i = sb("pcol_i", [P, 1], I32)
        pcol = sb("pcol", [P, 1])
        ones = sb("ones", [P, 1])
        gb = sb("gb", [P, 2, KT])
        pos_i = sb("pos_i", [P, TT], I32)
        pos_f = sb("pos_f", [P, TT])
        inv = sb("inv", [P, ROPE_HALF])
        ang = sb("ang", [P, TT, ROPE_HALF])
        kk = sb("kk", [P, TT, ROPE_HALF])
        ang_s = sb("ang_s", [P, TT, ROPE_HALF])
        ang_c = sb("ang_c", [P, TT, ROPE_HALF])
        cos = sb("cos", [P, TT, ROPE_HALF])
        sin = sb("sin", [P, TT, ROPE_HALF])
        cwr = sb("cwr", [CONV * 8, P])
        cw = sb("cw", [P, CONV * 8])
        bias12 = sb("bias12", [P, 12])
        rb36 = sb("rb36", [P, 36])
        gcol = sb("gcol", [P, KT])
        wr = sb("wr", [P, KT, NG + NE])
        junk = sb("junk", [P, 4, TT, FD])
        junk_m = bufc[:, 0:1024].rearrange("p (t n) -> p t n", t=TT)
        z12 = sb("z12", [P, TT, 12])
        az = sb("az", [P, TT, 8])
        mn = sb("mn", [P, TT, 8])
        ls = sb("ls", [P, TT, 8])
        bcum = sb("bcum", [P, TT, 4])
        nmx = sb("nmx", [P, 4, 2])
        stat = sb("stat", [P, 4, 2])
        rinv = sb("rinv", [P, 4, 2])
        em = sb("em", [P, 4, 2])
        mhalf = sb("mhalf", [P, TT])
        ms = sb("ms", [P, TT, HEADS])
        bns = sb("bns", [P, TT, 2, 6])
        mv = sb("mv", [P, TT, 2])
        rstd = sb("rstd", [P, TT])
        nmr = sb("nmr", [P, TT])
        lg = sb("lg", [P, TT, 36])
        r1 = sb("r1", [P, TT, 1])
        g4 = sb("g4", [P, TT, NG])
        e4 = sb("e4", [P, TT, NG])
        d4 = sb("d4", [P, TT, NG])
        s4 = sb("s4", [P, TT, 1])
        gmx = sb("gmx", [P, TT, 1])
        v12 = sb("v12", [P, 2, TT, 1])
        emk = sb("emk", [P, TT, NE])
        eq = sb("eq", [P, TT, NE])
        oh = sb("oh", [P, 2, TT, NE])
        mall = sb("mall", [P, TT, NE])
        dd = sb("dd", [P, TT, 1])
        ex = sb("ex", [P, TT, 1])
        wgt = sb("wgt", [P, 2, TT, 1])
        dst = sb("dst", [P, 2, TT, 1])
        novt = Wm[0:NE, 2 * P:3 * P]
        starts = sb("starts", [P, 2 * NE + 1])
        delta = sb("delta", [P, NE])
        dall = sb("dall", [P, TT, NE])
        dcur = sb("dcur", [P, 2, TT, 1])
        pcur = sb("pcur", [P, 1])
        tabf = sb("tabf", [1, 48])
        tabi = sb("tabi", [1, 48], I32)
        total = sb("total", [1, 1])

        xT = bufa[:, :].rearrange("p (k t) -> p k t", k=KT)
        y = lnp[:, :, :]
        v = bufb[:, :].rearrange("p (t n) -> p t n", t=TT)
        yT = bufb[:, :].rearrange("p (k t) -> p k t", k=KT)
        drow = bufb[:, 0:512].rearrange("p (k t) -> p k t", k=2)
        wrow = bufb[:, 512:1024].rearrange("p (k t) -> p k t", k=2)
        sil = bufb[:, 1024:1536]
        hid = bufb[:, 1536:2048]
        qkm = bufc[:, :].rearrange("p (c t) -> p c t", c=8)
        xg = bufc[:, 0:1024].rearrange("p (k s) -> p k s", k=KT)
        ym = bufc[:, 1024:2048]
        sg = bufd[:, :].rearrange("p (t n) -> p t n", t=TT)
        hT = bufd[:, 0:512].rearrange("p (k s) -> p k s", k=FT)
        oneh = bufd[:, 512:768].rearrange("p (t s) -> p t s", t=TT)
        wt = bufd[:, 768:1024]
        bqk = bufd[:, :].rearrange("p (t n) -> p t n", t=TT)
        PT = bufe[:, 0:768].rearrange("p (b n) -> p b n", b=2)
        rt = bufe[:, 768:1024].rearrange("p (i h d) -> p i h d", i=4, h=8)
        cmp8 = Wm[0:1, 0:EXTRA * NE].rearrange("p (b e) -> p b e", b=EXTRA)
        iota_i = bufc[:, 0:P].bitcast(I32)
        desc_i = bufc[:, P:P + NE].bitcast(I32)
        iot8_i = bufc[0:1, 512:512 + EXTRA * NE].bitcast(I32)
        wt_second = Pm[:, 0, 0:SEQ]

        ps = [ctx.enter_context(nc.psum_tensor(f"ps{i}", [P, 512], F32)) for i in range(8)]

        x_in, pos_in = sem("x_in"), sem("pos_in")
        chunk_in = [sem(f"chunk_in{c}") for c in range(NCHUNK)]
        expert_in = [sem(f"expert_in{u}") for u in range(4)]
        par_issued = sem("par_issued")
        par_in, ln_in = sem("par_in"), sem("ln_in")
        inv_ready, ident_ready = sem("inv_ready"), sem("ident_ready")
        consts_ready = sem("consts_ready")
        angles = sem("angles")
        trig = sem("trig")
        dve_step, act_step, pool_step = sem("dve_step"), sem("act_step"), sem("pool_step")
        dve_pair = sem("dve_pair")
        dve_setup = sem("dve_setup")
        pool_setup = sem("pool_setup")
        tr_bank = sem("tr_bank")
        tr_dve, tr_act = sem("tr_dve"), sem("tr_act")
        mix_half = sem("mix_half")
        proj = sem("proj")
        read_dve, read_act = sem("read_dve"), sem("read_act")
        cw_tr, cw_ready = sem("cw_tr"), sem("cw_ready")
        az_ready, ln_ready, ls_ready = sem("az_ready"), sem("ln_ready"), sem("ls_ready")
        cum_done, gpad_ready, cat_tr, cat_ready = sem("cum_done"), sem("gpad_ready"), sem("cat_tr"), sem("cat_ready")
        silu_done = sem("silu_done")
        roped, rope_tr, qb_ready, kb_ready = sem("roped"), sem("rope_tr"), sem("qb_ready"), sem("kb_ready")
        scored, maxed = sem("scored"), sem("maxed")
        exp_done, wexp_done, prod_done = sem("exp_done"), sem("wexp_done"), sem("prod_done")
        p_tr, pt_ready, pv_done, o_read = sem("p_tr"), sem("pt_ready"), sem("pv_done"), sem("o_read")
        y_gated, squared, y_ready = sem("y_gated"), sem("squared"), sem("y_ready")
        var_ready, rstd_ready = sem("var_ready"), sem("rstd_ready")
        stats_ready, normed, scaled = sem("stats_ready"), sem("normed"), sem("scaled")
        x_done = [sem(f"x_done{tt}") for tt in range(TT)]
        logits = sem("logits")
        gdiff, gexp, vdiff, vexp = sem("gdiff"), sem("gexp"), sem("vdiff"), sem("vexp")
        masks_ready, ranks, novt_ready, starts_ps = sem("masks_ready"), sem("ranks"), sem("novt_ready"), sem("starts_ps")
        dst_ready, rows_ps, rows_dve, rows_act = sem("dst_ready"), sem("rows_ps"), sem("rows_dve"), sem("rows_act")
        table_ready = sem("table_ready")
        oneh_ready, gathered, xg_dve, xg_act = sem("oneh_ready"), sem("gathered"), sem("xg_dve"), sem("xg_act")
        gate_used, up_used, down_used = sem("gate_used"), sem("up_used"), sem("down_used")
        combined, silued, h_ready, h_tr, hT_ready = sem("combined"), sem("silued"), sem("h_ready"), sem("h_tr"), sem("hT_ready")
        wt_ready, y_dve, y_act = sem("wt_ready"), sem("y_dve"), sem("y_act")
        acc_done = sem("acc_done")
        first_oneh = sem("first_oneh")
        first_gathered = sem("first_gathered")
        out_sem = sem("out_sem")
        dve_held, act_held, pe_held = sem("dve_held"), sem("act_held"), sem("pe_held")

        block = ctx.enter_context(nc.Block())

        def bc(ap, shape):
            return ap.to_broadcast(shape)

        def slot(s, n=CH):
            return ring[:, s, 0:KT * n].rearrange("p (k n) -> p k n", k=KT)

        @block.sync
        def _(sp):
            with nc.allow_non_contiguous_dma(reason="256 positions"):
                sp.dma_start(pos_i[:, :], A["positions"][0].rearrange("(t p) -> p t", p=P)).then_inc(pos_in, 16)
            sp.dma_start(x[:, :, :], A["x"][0].rearrange("(t p) d -> p t d", p=P)).then_inc(x_in, 16)

            def load_chunk(l, c):
                s = slot(SLOT_OF[c])
                if c >= 8:
                    src = A["w_out"][l].rearrange("(p k) n -> p k n", k=KT)[:, :, (c - 8) * CH:(c - 7) * CH]
                    sp.dma_start(s[:, :, :], src).then_inc(chunk_in[c], 16)
                    return
                at = 0
                for a, b in COLS[c]:
                    src = A["w_in"][l].rearrange("(p k) n -> p k n", k=KT)[:, :, a:b]
                    sp.dma_start(s[:, :, at:at + b - a], src).then_inc(chunk_in[c], 16)
                    at += b - a

            def load_pair(l, r, part, e):
                w = {"gate": "w_gate", "up": "w_up", "down": "w_down"}[part]
                for q in range(2):
                    rows = slice(e[q], e[q] + 1) if isinstance(e[q], int) else bass.ds(e[q], 1)
                    src = A[w][l].rearrange("e (p k) n -> e p (k n)", p=P)[rows]
                    sp.dma_start(ring[:, 2 * unit(r, part) + q, :],
                                 src.rearrange("a p n -> (a p) n")).then_inc(expert_in[unit(r, part)], 16)

            load_chunk(0, 0)
            load_chunk(0, 1)
            sp.wait_ge(par_issued, 1)
            done = 0
            for l in range(DEPTH):
                for c in range(0 if l else 2, 8):
                    if l > 0:
                        used, n = ((down_used, done_but_1), (gate_used, done), (up_used, done), (down_used, done))[c // 2]
                        sp.wait_ge(used, n)
                    load_chunk(l, c)
                for i, part in enumerate(("gate", "up", "down")):
                    sp.wait_ge(proj, NCHUNK * l + 2 * i + 2)
                    load_pair(l, 0, part, (0, 1))
                for c in (8, 9):
                    sp.wait_ge(proj, NCHUNK * l + c - 1)
                    load_chunk(l, c)
                sp.wait_ge(proj, NCHUNK * l + 10)
                load_pair(l, 1, "gate", (2, 3))
                sp.wait_ge(table_ready, l + 1)
                groups = sp.value_load(tabi[0:1, 40:41], min_val=NE // 8, max_val=(NE + EXTRA) // 8)

                def load_group(i0, loads):
                    e, at = None, None
                    for r, part in loads:
                        if at != r:
                            e = [sp.value_load(tabi[0:1, bass.ds(2 * i0 + 2 * r + q, 1)], min_val=0, max_val=NE - 1) for q in range(2)]
                            at = r
                        if part == "gate":
                            sp.wait_ge(down_used, done + i0 + (r - 1))
                        else:
                            sp.wait_ge({"up": gate_used, "down": up_used}[part], done + i0 + r)
                        load_pair(l, r % 4, part, e)

                rest = [(1, "up"), (1, "down")] + [(r, part) for r in (2, 3) for part in ("gate", "up", "down")]
                with sp.Fori(0, groups - 1) as i:
                    load_group(4 * i, rest + [(4, "gate"), (4, "up"), (4, "down"), (5, "gate")])
                last = sp.value_load(tabi[0:1, 43:44], min_val=NE // 2 - 4, max_val=(NE + EXTRA) // 2 - 4)
                load_group(last, rest)
                done_but_1, done = sp.snap(done + last + 3), sp.snap(done + last + 4)
            for tt in range(TT):
                sp.wait_ge(x_done[tt], 2 * DEPTH + 1)
                sp.dma_start(out[0].rearrange("(t p) d -> t p d", p=P)[tt], x[:, tt, :]).then_inc(out_sem, 16)
            sp.wait_ge(out_sem, 16 * TT)

        @block.gpsimd
        def _(pool):
            st = Steps(pool, pool_setup, 0)
            g = nc.gpsimd
            for j in range(ROPE_HALF):
                last = g.memset(inv[:, j:j + 1], 500000.0 ** (-j / ROPE_HALF))
            last.then_inc(inv_ready, 1)
            st(g.memset(ident[:, :], 0.0))
            st(g.affine_select(out=ident[:, :], in_=ident[:, :], compare_op=ALU.not_equal, fill=1.0,
                               base=0, pattern=[[-1, P]], channel_multiplier=1))
            g.tensor_copy(identb[:, :], ident[:, :]).then_inc(ident_ready, 1)
            g.memset(mhalf[:, :], -0.5).then_inc(normed, 1)
            g.memset(ones[:, :], 1.0).then_inc(normed, 1)
            g.memset(tri_incl[:, :], 1.0)
            g.memset(tri_strict[:, :], 1.0)
            g.memset(maskb[:, :], 0.0)
            g.memset(tri65[:, :], 1.0)
            g.memset(qf[:, :, :], 0.0)
            g.memset(qb[:, :, :], 0.0)
            g.memset(gpad[:, :, :], 0.0)
            g.memset(total[:, :], 0.0)
            g.iota(iota_i[:, :], pattern=[[1, P]], base=0, channel_multiplier=0)
            g.iota(desc_i[:, :], pattern=[[-1, NE]], base=NE, channel_multiplier=0)
            g.iota(iot8_i[:, :], pattern=[[1, EXTRA], [0, NE]], base=0, channel_multiplier=0)
            st(g.iota(pcol_i[:, :], pattern=[[0, 1]], base=0, channel_multiplier=1))
            g.tensor_copy(iota_f[:, :], iota_i[:, :])
            g.tensor_copy(desc[:, :], desc_i[:, :])
            g.tensor_copy(iot8[:, :], iot8_i[:, :])
            g.tensor_copy(pcol[:, :], pcol_i[:, :])
            g.affine_select(out=tri_incl[:, :], in_=tri_incl[:, :], compare_op=ALU.is_ge, fill=0.0,
                            base=0, pattern=[[1, P]], channel_multiplier=-1)
            g.affine_select(out=tri_strict[:, :], in_=tri_strict[:, :], compare_op=ALU.is_gt, fill=0.0,
                            base=0, pattern=[[1, P]], channel_multiplier=-1)
            g.affine_select(out=maskb[:, :], in_=maskb[:, :], compare_op=ALU.is_ge, fill=-BIG,
                            base=0, pattern=[[-1, P]], channel_multiplier=1)
            g.affine_select(out=tri65[:, 0:NE], in_=tri65[:, 0:NE], compare_op=ALU.is_gt, fill=0.0,
                            base=0, pattern=[[1, NE]], channel_multiplier=-1)
            st(g.affine_select(out=tri65[:, NE:2 * NE], in_=tri65[:, NE:2 * NE], compare_op=ALU.is_ge, fill=0.0,
                               base=0, pattern=[[1, NE]], channel_multiplier=-1))
            g.tensor_scalar(base_e[:, :], iota_f[:, 0:NE], float(SLOTS), None, ALU.mult)
            g.tensor_scalar(alpha_i[:, :], ident[:, :], ALPHA, None, ALU.mult).then_inc(consts_ready, 1)
            pool.wait_ge(trig, 2)
            with pool.Fori(0, DEPTH) as l:
                st = Steps(pool, pool_step, l * POOL_LAYER_STEPS)

                def shift(n):
                    pool.wait_ge(scaled, 4 * l + 2 * n + 1)
                    g.tensor_tensor(x[:, 0, :], x[:, 0, :], lnp[:, 1, :], ALU.add).then_inc(x_done[0], 1)

                shift(0)
                pool.wait_ge(read_dve, 7 * l + DVE_READ[2])
                pool.wait_ge(read_act, 6 * l + ACT_READ[2])
                for tt in range(TT):
                    u = bqk[:, tt, :].rearrange("p (h d) -> p h d", d=FD)
                    u1, u2 = u[:, :, 0:ROPE_HALF], u[:, :, ROPE_HALF:2 * ROPE_HALF]
                    c = bc(cos[:, tt:tt + 1, :], [P, 8, ROPE_HALF])
                    s = bc(sin[:, tt:tt + 1, :], [P, 8, ROPE_HALF])
                    g.tensor_tensor(rt[:, 0], u1, c, ALU.mult)
                    g.tensor_tensor(rt[:, 1], u2, s, ALU.mult)
                    g.tensor_tensor(rt[:, 2], u1, s, ALU.mult)
                    st(g.tensor_tensor(rt[:, 3], u2, c, ALU.mult))
                    g.tensor_tensor(u1, rt[:, 0], rt[:, 1], ALU.subtract)
                    g.tensor_tensor(u2, rt[:, 2], rt[:, 3], ALU.add).then_inc(roped, 1)
                    pool.wait_ge(roped, 2 * l + tt + 1)

                def powers(n, of, to):
                    pool.wait_ge(var_ready, 6 * l + n + 1)
                    g.tensor_tensor(to, of, bc(mhalf[:, 0:1], of.shape) if len(of.shape) == 2 else
                                    bc(mhalf[:, :].unsqueeze(2), of.shape), ALU.pow).then_inc(rstd_ready, 1)

                powers(0, ms[:, :, 0:2 * FH], ms[:, :, 0:2 * FH])
                powers(1, ms[:, :, 2 * FH:HEADS], ms[:, :, 2 * FH:HEADS])
                for q in range(2):
                    for tt in range(TT):
                        powers(2 + 2 * q + tt, mv[:, tt, 1:2], rstd[:, tt:tt + 1])
                    if q == 0:
                        shift(1)
                assert st.n == POOL_LAYER_STEPS, st.n
            pool.wait_ge(scaled, 4 * DEPTH + 1)
            g.tensor_tensor(x[:, 0, :], x[:, 0, :], lnp[:, 1, :], ALU.add).then_inc(x_done[0], 1)

        @block.scalar
        def _(act):
            a = nc.scalar

            def evac_tr(l, q):
                act.wait_ge(ln_in, 128 * l + 64 * q + 64)
                for b in (1, 3):
                    act.wait_ge(tr_bank, 12 * l + 8 * q + b + 1)
                    for k in (2 * b, 2 * b + 1):
                        last = a.activation(xT[:, k, :], ps[4 + b][:, (k % 2) * SEQ:(k % 2 + 1) * SEQ], ACT.Identity,
                                            bias=gb[:, 1, k:k + 1], scale=gb[:, 0, k:k + 1])
                    last.then_inc(tr_act, 1)

            act.wait_ge(angles, 1)
            a.activation(sin[:, :, :], ang_s[:, :, :], ACT.Sin).then_inc(trig, 1)
            a.activation(cos[:, :, :], ang_c[:, :, :], ACT.Sin).then_inc(trig, 1)
            with act.Fori(0, DEPTH) as l:
                st = Steps(act, act_step, l * ACT_LAYER_STEPS)

                evac_tr(l, 0)
                with nc.allow_non_contiguous_dma(reason="small parameters"):
                    act.dma_start(cwr[:, :], A["conv_w"][bass.ds(l, 1)].rearrange("a j (c p) -> (a j c) p", p=P)).then_inc(par_in, 16)
                    for i, n in enumerate(("b_fox_f", "b_mlstm_i", "b_mlstm_f")):
                        act.dma_start(bias12[:, 4 * i:4 * i + 4], A[n][bass.ds(l, 1)].to_broadcast([P, 4])).then_inc(par_in, 16)
                    for n, lo, hi in (("g_fox", 0, 32), ("g_mlstm", 32, 96), ("g_moba", 96, 128)):
                        act.dma_start(gcol[lo:hi, :], A[n][bass.ds(l, 1)].rearrange("a (p k) -> (a p) k", k=KT)).then_inc(par_in, 16)
                    act.dma_start(wr[:, :, 0:NG], A["w_grp"][bass.ds(l, 1)].rearrange("a (p k) g -> (a p) k g", k=KT)).then_inc(par_in, 16)
                    act.dma_start(wr[:, :, NG:NG + NE], A["w_exp_router"][bass.ds(l, 1)].rearrange("a (p k) g e -> (a p) k (g e)", k=KT)).then_inc(par_in, 16)
                    act.dma_start(rb36[:, 0:NG], A["b_grp"][bass.ds(l, 1)].to_broadcast([P, NG])).then_inc(par_in, 16)
                    act.dma_start(rb36[:, NG:36], A["b_exp_router"][bass.ds(l, 1)].rearrange("a g e -> a (g e)").to_broadcast([P, NE])).then_inc(par_in, 16)

                act.sem_inc(par_issued, 1)

                def chunk(c):
                    act.wait_ge(proj, NCHUNK * l + c + 1)

                def finished(c):
                    if c in (4, 5):
                        return
                    chunk(c)
                    if c == 0:
                        a.activation(kf[:, :, :].rearrange("p c t -> p (c t)"), ps[1][:, :], ACT.Copy).then_inc(read_act, 1)
                    elif c == 1:
                        a.activation(v[:, 1, 0:256], ps[3][:, 0:256], ACT.Copy)
                        a.activation(z12[:, 1, :], ps[3][:, 256:268], ACT.Copy).then_inc(read_act, 1)
                        act.wait_ge(az_ready, l + 1)
                        st(a.activation(ls[:, :, :], az[:, :, :], ACT.Exp))
                        a.activation(az[:, :, :], ls[:, :, :], ACT.Ln, bias=1.0).then_inc(ln_ready, 1)
                    elif c == 2:
                        a.activation(bqk[:, 1, :], ps[1][:, :], ACT.Copy).then_inc(read_act, 1)
                    elif c == 3:
                        a.activation(v[:, 1, 768:1024], ps[3][:, 0:256], ACT.Copy).then_inc(read_act, 1)
                    elif c == 6:
                        a.activation(v[:, 1, 256:768], ps[1][:, :], ACT.Copy).then_inc(read_act, 1)
                    elif c == 7:
                        a.activation(sg[:, 0, :], ps[2][:, :], ACT.Sigmoid)
                        a.activation(sg[:, 1, :], ps[3][:, :], ACT.Sigmoid).then_inc(read_act, 1)

                def attend(it):
                    if it < HEADS:
                        j, b = it, it % 2
                        act.wait_ge(maxed, HEADS * l + j + 1)
                        if kind(j) == "mlstm":
                            if mlstm_up_to(j) > 1:
                                act.wait_ge(prod_done, MLS * l + mlstm_up_to(j) - 1)
                            a.activation(Wm[:, 0:P], ps[7][:, 0:P], ACT.Exp, bias=nmx[:, j % 4, 0:1])
                            a.activation(em[:, j % 4, :], em[:, j % 4, :], ACT.Exp)
                            a.activation(Wm[:, P:3 * P], ps[7][:, P:3 * P], ACT.Exp, bias=nmx[:, j % 4, 1:2]).then_inc(wexp_done, 1)
                        else:
                            if j >= 2:
                                act.wait_ge(p_tr, HEADS * l + j - 1)
                            if j >= 4:
                                act.wait_ge(o_read, HEADS * l + j - 3)
                            a.activation(Pm[:, b, 0:P], ps[4][:, 0:P], ACT.Exp, bias=nmx[:, j % 4, 0:1],
                                         accum_out=stat[:, j % 4, 0:1])
                            a.activation(Pm[:, b, P:3 * P], ps[4][:, P:3 * P], ACT.Exp, bias=nmx[:, j % 4, 1:2],
                                         accum_out=stat[:, j % 4, 1:2]).then_inc(exp_done, 1)
                    if 1 <= it <= HEADS:
                        j = it - 1
                        act.wait_ge(p_tr, HEADS * l + j + 1)
                        if j >= 2:
                            act.wait_ge(pv_done, HEADS * l + j - 1)
                        a.activation(PT[:, j % 2, :], ps[5][:, 0:3 * P], ACT.Copy).then_inc(pt_ready, 1)
                    if it >= 3 and kind(it - 3) != "mlstm":
                        j = it - 3
                        act.wait_ge(o_read, HEADS * l + j + 1)
                        for tt in range(TT):
                            last = a.activation(junk[:, j % 4, tt, :], y[:, tt, column(j):column(j) + FD], ACT.Square,
                                                accum_out=ms[:, tt, j:j + 1])
                        last.then_inc(squared, 1)

                for what, n, part in mixer_order():
                    if what == "proj" and part == 3:
                        finished(n)
                    elif what == "conv" and part == 0:
                        act.wait_ge(read_dve, 7 * l + DVE_READ[4 + n])
                        u = qkm[:, MH * n:MH * (n + 1), :]
                        a.activation(u, u, ACT.Silu).then_inc(silu_done, 1)
                    elif what == "att":
                        attend(n)
                    elif what == "ropek":
                        act.wait_ge(rope_tr, 2 * l + 2)
                        a.activation(kb[:, :, :].rearrange("p c t -> p (c t)"), ps[7][:, :], ACT.Copy).then_inc(kb_ready, 1)

                for tt in range(TT):
                    act.wait_ge(y_gated, 2 * l + tt + 1)
                    for j in range(2 * FH, HEADS):
                        last = a.activation(junk_m[:, tt, (j - 2 * FH) * MD:(j - 2 * FH + 1) * MD], y[:, tt, column(j):column(j) + MD], ACT.Square,
                                            accum_out=ms[:, tt, j:j + 1])
                last.then_inc(squared, 1)
                for b in (1, 3):
                    act.wait_ge(tr_bank, 4 + 12 * l + b + 1)
                    a.activation(yT[:, 2 * b, :], ps[4 + b][:, 0:SEQ], ACT.Copy, scale=gcol[:, 2 * b:2 * b + 1])
                    a.activation(yT[:, 2 * b + 1, :], ps[4 + b][:, SEQ:2 * SEQ], ACT.Copy,
                                 scale=gcol[:, 2 * b + 1:2 * b + 2]).then_inc(tr_act, 1)
                act.wait_ge(tr_bank, 4 + 12 * l + 4)
                def load_ln(names):
                    for i, name in enumerate(names):
                        act.dma_start(lnp[:, i, :], A[name][bass.ds(l, 1)].to_broadcast([P, D])).then_inc(ln_in, 16)
                        act.dma_start(gb[:, i, :], A[name][bass.ds(l, 1)].rearrange("a (p k) -> (a p) k", k=KT)).then_inc(ln_in, 16)

                load_ln(("ln1_g", "ln1_b"))

                def normalise(q):
                    for tt in range(TT):
                        act.wait_ge(stats_ready, 4 * l + 2 * q + tt + 1)
                        for half in range(2):
                            last = a.activation(x[:, tt, half * CH:(half + 1) * CH], ps[2 * half + tt][:, :], ACT.Identity,
                                                bias=nmr[:, tt:tt + 1], scale=rstd[:, tt:tt + 1])
                        last.then_inc(normed, 1)

                normalise(0)
                evac_tr(l, 1)
                act.wait_ge(gdiff, l + 1)
                a.activation(e4[:, :, :], d4[:, :, :], ACT.Exp).then_inc(gexp, 1)
                for tt in range(TT):
                    act.wait_ge(x_done[tt], 2 * l + 2)
                load_ln(("ln2_g", "ln2_b"))
                act.wait_ge(vdiff, l + 1)
                a.activation(ex[:, :, :], dd[:, :, :], ACT.Exp).then_inc(vexp, 1)
                act.wait_ge(first_gathered, l + 1)
                a.activation(xg[:, 4:8, :].rearrange("p k s -> p (k s)"), ps[7][:, :], ACT.Copy).then_inc(xg_act, 1)
                act.wait_ge(rows_ps, 2 * l + 2)
                a.activation(wrow.rearrange("p k t -> p (k t)"), ps[5][:, :], ACT.Copy).then_inc(rows_act, 1)

                act.wait_ge(table_ready, l + 1)
                act.sem_inc(act_held, 1)
                pairs = act.value_load(tabi[0:1, 42:43], min_val=NE // 2, max_val=(NE + EXTRA) // 2)
                done = act.value_load(tabi[0:1, 41:42], min_val=0, max_val=DEPTH * (NE + EXTRA) // 2)
                with act.Fori(0, pairs) as i:
                    n = act.snap(done + i)
                    act.wait_ge(gate_used, n + 1)
                    a.activation(sil, ps[4][:, :], ACT.Silu).then_inc(silued, 1)
                    act.wait_ge(gathered, 2 * n + 2)
                    a.activation(xg[:, 4:8, :].rearrange("p k s -> p (k s)"), ps[7][:, :], ACT.Copy).then_inc(xg_act, 1)
                    act.wait_ge(down_used, n + 1)
                    a.activation(ym[:, CH:2 * CH], ps[7][:, :], ACT.Copy).then_inc(y_act, 1)
                normalise(1)
                assert st.n == ACT_LAYER_STEPS, st.n

        @block.vector
        def _(dve):
            d = nc.vector
            st = Steps(dve, dve_setup, 0)
            for i in range(2):
                d.memset(lnp[:, i, :], 1.0 - i).then_inc(ln_in, 16)
                d.memset(gb[:, i, :], 1.0 - i).then_inc(ln_in, 16)
            dve.wait_ge(pos_in, 16)
            dve.wait_ge(inv_ready, 1)
            st(d.tensor_copy(pos_f[:, :], pos_i[:, :]))
            st(d.tensor_tensor(ang[:, :, :], bc(pos_f[:, :].unsqueeze(2), [P, TT, ROPE_HALF]),
                               bc(inv[:, :].unsqueeze(1), [P, TT, ROPE_HALF]), ALU.mult))
            magic = 1.5 * 2.0 ** 23
            c1 = 6.28125
            c2 = float(int((2 * math.pi - c1) * 2 ** 20)) / 2 ** 20
            c3 = 2 * math.pi - c1 - c2
            st(d.tensor_scalar(kk[:, :, :], ang[:, :, :], 1 / (2 * math.pi), None, ALU.mult))
            st(d.tensor_scalar(kk[:, :, :], kk[:, :, :], magic, None, ALU.add))
            st(d.tensor_scalar(kk[:, :, :], kk[:, :, :], magic, None, ALU.subtract))
            for c in (c1, c2, c3):
                st(d.scalar_tensor_tensor(ang[:, :, :], kk[:, :, :], -c, ang[:, :, :], ALU.mult, ALU.add))
            pi = 3.1415925
            d.tensor_scalar(ang_s[:, :, :], ang[:, :, :], pi, -pi, ALU.min, ALU.max)
            st(d.tensor_scalar(ang_c[:, :, :], ang[:, :, :], math.pi / 2, None, ALU.add))
            st(d.tensor_scalar(kk[:, :, :], ang_c[:, :, :], math.pi, -2 * math.pi, ALU.is_gt, ALU.mult))
            st(d.tensor_tensor(ang_c[:, :, :], ang_c[:, :, :], kk[:, :, :], ALU.add))
            d.tensor_scalar(ang_c[:, :, :], ang_c[:, :, :], pi, -pi, ALU.min, ALU.max).then_inc(angles, 1)

            def evac_tr(l, q):
                dve.wait_ge(ln_in, 128 * l + 64 * q + 64)
                for b in (0, 2):
                    dve.wait_ge(tr_bank, 12 * l + 8 * q + b + 1)
                    for k in (2 * b, 2 * b + 1):
                        last = d.tensor_scalar(xT[:, k, :], ps[4 + b][:, (k % 2) * SEQ:(k % 2 + 1) * SEQ],
                                               gb[:, 0, k:k + 1], gb[:, 1, k:k + 1], ALU.mult, ALU.add)
                    last.then_inc(tr_dve, 1)
                dve.wait_ge(tr_bank, 12 * l + 8 * q + 4)
                for tt in range(TT):
                    d.tensor_tensor(x[:, tt, :], x[:, tt, :], lnp[:, 0, :], ALU.mult).then_inc(scaled, 1)
                dve.wait_ge(scaled, 4 * l + 2 * q + 2)
                d.tensor_tensor(x[:, 1, :], x[:, 1, :], lnp[:, 1, :], ALU.add).then_inc(x_done[1], 1)

            with dve.Fori(0, DEPTH) as l:
                st = Steps(dve, dve_step, l * DVE_LAYER_STEPS)
                evac_tr(l, 0)
                dve.wait_ge(consts_ready, 1)

                def chunk(c):
                    dve.wait_ge(proj, NCHUNK * l + c + 1)

                def conv(q, j):
                    back = CONV - 1 - j
                    if back == 0:
                        chunk(4 + q)
                    for c in range(MH):
                        u = ps[2 * q + c // 2][:, (c % 2) * SEQ:(c % 2 + 1) * SEQ]
                        w = cw[:, j * 8 + 4 * q + c:j * 8 + 4 * q + c + 1]
                        o = qkm[:, 4 * q + c, :]
                        if back == 0:
                            last = d.tensor_scalar(o, u, w, None, ALU.mult)
                        else:
                            last = d.scalar_tensor_tensor(o[:, back:], u[:, 0:SEQ - back], w, o[:, back:],
                                                          ALU.mult, ALU.add)
                    if j:
                        st(last)
                    else:
                        last.then_inc(read_dve, 1)

                def finished(c):
                    if c in (0, 1, 2, 3, 6):
                        chunk(c)
                    if c == 0:
                        u = ps[0][:, :].rearrange("p (c t) -> p c t", c=2)
                        d.tensor_scalar(qf[0:64, 0:FH:2, :], u[0:64], FD ** -0.5, None, ALU.mult)
                        d.tensor_scalar(qf[64:128, 1:FH:2, :], u[64:128], FD ** -0.5, None, ALU.mult).then_inc(read_dve, 1)
                    elif c == 1:
                        d.tensor_copy(v[:, 0, 0:256], ps[2][:, 0:256])
                        d.tensor_copy(z12[:, 0, :], ps[2][:, 256:268]).then_inc(read_dve, 1)
                        gates()
                    elif c == 2:
                        d.tensor_copy(bqk[:, 0, :], ps[0][:, :]).then_inc(read_dve, 1)
                    elif c == 3:
                        d.tensor_copy(v[:, 0, 768:1024], ps[2][:, 0:256]).then_inc(read_dve, 1)
                    elif c == 6:
                        d.tensor_copy(v[:, 0, 256:768], ps[0][:, :]).then_inc(read_dve, 1)

                def gates():
                    dve.wait_ge(read_dve, 7 * l + 2)
                    dve.wait_ge(read_act, 6 * l + 2)
                    dve.wait_ge(par_in, 16 * PAR_DMAS * (l + 1))
                    st(d.tensor_tensor(z12[:, :, :], z12[:, :, :], bc(bias12[:, :].unsqueeze(1), [P, TT, 12]), ALU.add))
                    for h, c in ((0, 0), (4, 8)):
                        d.tensor_scalar(mn[:, :, h:h + 4], z12[:, :, c:c + 4], 0.0, None, ALU.min)
                        last = d.tensor_scalar(az[:, :, h:h + 4], z12[:, :, c:c + 4], 0.0, None, ALU.max)
                    st(last)
                    d.tensor_tensor(az[:, :, :], mn[:, :, :], az[:, :, :], ALU.subtract).then_inc(az_ready, 1)
                    dve.wait_ge(cw_tr, l + 1)
                    d.tensor_copy(cw[:, :], ps[7][:, 384:384 + CONV * 8]).then_inc(cw_ready, 1)
                    dve.wait_ge(cw_ready, l + 1)
                    dve.wait_ge(ln_ready, l + 1)
                    d.tensor_tensor(ls[:, :, :], mn[:, :, :], az[:, :, :], ALU.subtract).then_inc(ls_ready, 1)

                def attend(it):
                    if it < HEADS:
                        j, b = it, it % 2
                        dve.wait_ge(scored, HEADS * l + j + 1)
                        s = ps[7 if kind(j) == "mlstm" else 4]
                        d.tensor_reduce(nmx[:, j % 4, 0:1], s[:, 0:P], AXX, ALU.max, negate=True)
                        last = d.tensor_reduce(nmx[:, j % 4, 1:2], s[:, P:3 * P], AXX, ALU.max, negate=True)
                        if kind(j) != "mlstm":
                            last.then_inc(maxed, 1)
                        else:
                            st(last)
                            st(d.tensor_scalar(nmx[:, j % 4, :], nmx[:, j % 4, :], 0.0, None, ALU.min))
                            d.tensor_tensor(em[:, j % 4, :], nmx[:, j % 4, :], bcum[:, :, j - 2 * FH], ALU.subtract).then_inc(maxed, 1)
                            dve.wait_ge(wexp_done, MLS * l + mlstm_up_to(j))
                            dve.wait_ge(p_tr, HEADS * l + j - 1)
                            d.scalar_tensor_tensor(Pm[:, b, 0:P], ps[4][:, 0:P], MD ** -0.5, Wm[:, 0:P], ALU.mult, ALU.mult,
                                                   accum_out=stat[:, j % 4, 0:1])
                            d.scalar_tensor_tensor(Pm[:, b, P:3 * P], ps[4][:, P:3 * P], MD ** -0.5, Wm[:, P:3 * P], ALU.mult,
                                                   ALU.mult, accum_out=stat[:, j % 4, 1:2]).then_inc(prod_done, 1)
                    if it >= 2:
                        j = it - 2
                        if kind(j) == "mlstm":
                            dve.wait_ge(prod_done, MLS * l + mlstm_up_to(j))
                            st(d.scalar_tensor_tensor(rinv[:, j % 4, :], stat[:, j % 4, :], -1.0, stat[:, j % 4, :], ALU.mult, ALU.max))
                            st(d.tensor_tensor(rinv[:, j % 4, :], rinv[:, j % 4, :], em[:, j % 4, :], ALU.max))
                            st(d.reciprocal(rinv[:, j % 4, :], rinv[:, j % 4, :]))
                        else:
                            dve.wait_ge(exp_done, SOFT * l + soft_up_to(j))
                            st(d.reciprocal(rinv[:, j % 4, :], stat[:, j % 4, :]))
                        dve.wait_ge(pv_done, HEADS * l + j + 1)
                        if j == 0:
                            dve.wait_ge(x_done[0], 2 * l + 1)
                            dve.wait_ge(x_done[1], 2 * l + 1)
                        w, c = width(j), column(j)
                        for tt in range(TT):
                            last = d.tensor_scalar(y[:, tt, c:c + w], ps[6][:, tt * w:(tt + 1) * w],
                                                   rinv[:, j % 4, tt:tt + 1], None, ALU.mult)
                        last.then_inc(o_read, 1)

                lo, mi, hi = FH * FD, FH * FD + MH * MD, D

                def mean_squares(h0, h1, w):
                    last = d.tensor_scalar(ms[:, :, h0:h1], ms[:, :, h0:h1], 1.0 / w, EPS, ALU.mult, ALU.add)
                    last.then_inc(var_ready, 1)

                def scale_heads(tt, a0, a1, w, h0):
                    u = y[:, tt, a0:a1].rearrange("p (h w) -> p h w", w=w)
                    return d.tensor_tensor(u, u, bc(ms[:, tt, h0:h0 + 4].unsqueeze(2), [P, 4, w]), ALU.mult)

                for what, n, part in mixer_order():
                    if what == "proj" and part == 3:
                        finished(n)
                    elif what == "conv":
                        conv(n, part)
                    elif what == "att":
                        attend(n)
                        if n == 11:
                            dve.wait_ge(squared, 9 * l + 8)
                            mean_squares(0, 2 * FH, FD)
                        elif n == 12:
                            dve.wait_ge(rstd_ready, 6 * l + 1)
                            for tt in range(TT):
                                scale_heads(tt, 0, lo, FD, 0)
                                scale_heads(tt, mi, hi, FD, FH)
                    elif what == "cum":
                        dve.wait_ge(cum_done, l + 1)
                        u = ps[7][:, 0:TT * 8].rearrange("p (t g) -> p t g", t=TT)
                        d.tensor_scalar(gpad[:, :, 0:4], u[:, :, 0:4], -1.0, None, ALU.mult)
                        d.tensor_copy(bcum[:, :, :], u[:, :, 4:8])
                        d.tensor_tensor(gpad[:, :, 4:8], z12[:, :, 4:8], u[:, :, 4:8], ALU.subtract).then_inc(gpad_ready, 1)
                    elif what == "cat":
                        dve.wait_ge(cat_tr, l + 1)
                        d.tensor_copy(catT[:, :], ps[7][:, 0:SEQ]).then_inc(cat_ready, 1)
                    elif what == "ropeq":
                        dve.wait_ge(rope_tr, 2 * l + 1)
                        u = ps[7][:, :].rearrange("p (c t) -> p c t", c=2)
                        d.tensor_scalar(qb[0:64, 0:FH:2, :], u[0:64], FD ** -0.5, None, ALU.mult)
                        d.tensor_scalar(qb[64:128, 1:FH:2, :], u[64:128], FD ** -0.5, None, ALU.mult).then_inc(qb_ready, 1)

                dve.wait_ge(read_act, 6 * l + ACT_READ[7])
                dve.wait_ge(o_read, HEADS * (l + 1))
                for tt in range(TT):
                    d.tensor_tensor(y[:, tt, lo:mi], y[:, tt, lo:mi], sg[:, tt, :], ALU.mult).then_inc(y_gated, 1)
                dve.wait_ge(squared, 9 * l + 9)
                mean_squares(2 * FH, HEADS, MD)
                dve.wait_ge(rstd_ready, 6 * l + 2)
                for tt in range(TT):
                    scale_heads(tt, lo, mi, MD, 2 * FH).then_inc(y_ready, 1)
                for b in (0, 2):
                    dve.wait_ge(tr_bank, 4 + 12 * l + b + 1)
                    d.tensor_scalar(yT[:, 2 * b, :], ps[4 + b][:, 0:SEQ], gcol[:, 2 * b:2 * b + 1], None, ALU.mult)
                    d.tensor_scalar(yT[:, 2 * b + 1, :], ps[4 + b][:, SEQ:2 * SEQ], gcol[:, 2 * b + 1:2 * b + 2],
                                    None, ALU.mult).then_inc(tr_dve, 1)

                def layer_norm(q, ready):
                    for half, tt in ((0, 0), (0, 1), (1, 0), (1, 1)):
                        ready(tt, half)
                        last = d.bn_stats(bns[:, tt, half, :], ps[2 * half + tt][:, :])
                        if half == 1:
                            st(last)
                            dve.sem_inc(dve_held, 1)
                            st(d.bn_aggr(mv[:, tt, :], bns[:, tt, :, :].rearrange("p a b -> p (a b)")))
                            d.tensor_scalar(mv[:, tt, 1:2], mv[:, tt, 1:2], EPS, None, ALU.add).then_inc(var_ready, 1)
                            dve.wait_ge(rstd_ready, 6 * l + 2 * q + tt + 3)
                            d.scalar_tensor_tensor(nmr[:, tt:tt + 1], mv[:, tt, 0:1], -1.0, rstd[:, tt:tt + 1],
                                                   ALU.mult, ALU.mult).then_inc(stats_ready, 1)

                def mixed(tt, half):
                    if tt == 0:
                        dve.wait_ge(mix_half, 2 * l + half + 1)
                    else:
                        dve.wait_ge(proj, NCHUNK * l + 9 + half)

                layer_norm(0, mixed)
                evac_tr(l, 1)

                dve.wait_ge(logits, l + 1)
                st(d.tensor_tensor(lg[:, :, :], ps[5][:, 0:128].rearrange("p (t n) -> p t n", t=TT)[:, :, 0:36],
                                   bc(rb36[:, :].unsqueeze(1), [P, TT, 36]), ALU.add))
                st(d.tensor_reduce(gmx[:, :, :], lg[:, :, 0:NG], AXX, ALU.max))
                d.tensor_tensor(d4[:, :, :], lg[:, :, 0:NG], bc(gmx[:, :, :], [P, TT, NG]), ALU.subtract).then_inc(gdiff, 1)
                st(d.tensor_tensor(g4[:, :, :], lg[:, :, 0:NG], bc(gmx[:, :, :], [P, TT, NG]), ALU.is_equal))
                st(d.tensor_tensor(g4[:, :, :], g4[:, :, :], bc(desc[:, 0:NG].unsqueeze(1), [P, TT, NG]), ALU.mult))
                st(d.tensor_reduce(r1[:, :, :], g4[:, :, :], AXX, ALU.max))
                st(d.tensor_tensor(g4[:, :, :], g4[:, :, :], bc(r1[:, :, :], [P, TT, NG]), ALU.is_equal))
                st(d.tensor_scalar(g4[:, :, :], g4[:, :, :], -1.0, BIG, ALU.add, ALU.mult))
                for tt in range(TT):
                    last = d.tensor_tensor(emk[:, tt, :].rearrange("p (g e) -> p g e", g=NG),
                                           lg[:, tt, NG:36].rearrange("p (g e) -> p g e", g=NG),
                                           bc(g4[:, tt, :].unsqueeze(2), [P, NG, EG]), ALU.add)
                st(last)
                for k in range(2):
                    st(d.tensor_reduce(v12[:, k], emk[:, :, :], AXX, ALU.max))
                    st(d.tensor_tensor(eq[:, :, :], emk[:, :, :], bc(v12[:, k], [P, TT, NE]), ALU.is_equal))
                    st(d.tensor_tensor(eq[:, :, :], eq[:, :, :], bc(desc[:, :].unsqueeze(1), [P, TT, NE]), ALU.mult))
                    st(d.tensor_reduce(r1[:, :, :], eq[:, :, :], AXX, ALU.max))
                    st(d.tensor_tensor(oh[:, k], bc(desc[:, :].unsqueeze(1), [P, TT, NE]), bc(r1[:, :, :], [P, TT, NE]), ALU.is_equal))
                    if k == 0:
                        st(d.scalar_tensor_tensor(emk[:, :, :], oh[:, 0], -3 * BIG, emk[:, :, :], ALU.mult, ALU.add))
                d.tensor_tensor(mall[:, :, :], oh[:, 0], oh[:, 1], ALU.add).then_inc(masks_ready, 1)
                d.tensor_tensor(dd[:, :, :], v12[:, 1], v12[:, 0], ALU.subtract).then_inc(vdiff, 1)
                dve.wait_ge(ranks, l + 1)
                cnt = ps[5][0:NE, 128:256]
                st(d.tensor_scalar(novt[:, :], cnt, float(SLOTS), None, ALU.is_gt))
                st(d.scalar_tensor_tensor(novt[:, :], cnt, 2.0 * SLOTS, novt[:, :], ALU.is_gt, ALU.add))
                d.scalar_tensor_tensor(novt[:, :], cnt, 3.0 * SLOTS, novt[:, :], ALU.is_gt, ALU.add).then_inc(novt_ready, 1)
                dve.wait_ge(gexp, l + 1)
                st(d.tensor_reduce(s4[:, :, :], e4[:, :, :], AXX, ALU.add))
                dve.wait_ge(vexp, l + 1)
                st(d.tensor_scalar(r1[:, :, :], ex[:, :, :], 1.0, None, ALU.add))
                st(d.tensor_tensor(s4[:, :, :], s4[:, :, :], r1[:, :, :], ALU.mult))
                st(d.reciprocal(wgt[:, 0], s4[:, :, :]))
                st(d.tensor_tensor(wgt[:, 1], wgt[:, 0], ex[:, :, :], ALU.mult))
                rank = ps[5][:, 0:TT * NE].rearrange("p (t e) -> p t e", t=TT)
                d.tensor_tensor(eq[:, :, :], rank, bc(base_e[:, :].unsqueeze(1), [P, TT, NE]), ALU.add)
                dve.wait_ge(starts_ps, l + 1)
                st(d.tensor_copy(starts[:, :], ps[6][:, 0:2 * NE + 1]))
                st(d.tensor_scalar(delta[:, :], starts[:, 0:NE], float(NE - 1), float(SLOTS), ALU.add, ALU.mult))
                st(d.tensor_tensor(delta[:, :], delta[:, :], base_e[:, :], ALU.subtract))
                st(d.scalar_tensor_tensor(dall[:, :, :], rank, float(SLOTS), bc(delta[:, :].unsqueeze(1), [P, TT, NE]),
                                          ALU.is_ge, ALU.mult))
                st(d.tensor_tensor(dall[:, :, :], dall[:, :, :], eq[:, :, :], ALU.add))
                st(d.tensor_tensor(eq[:, :, :], oh[:, 0], dall[:, :, :], ALU.mult))
                st(d.tensor_reduce(dst[:, 0], eq[:, :, :], AXX, ALU.add))
                st(d.tensor_tensor(eq[:, :, :], oh[:, 1], dall[:, :, :], ALU.mult))
                d.tensor_reduce(dst[:, 1], eq[:, :, :], AXX, ALU.add).then_inc(dst_ready, 1)
                dve.wait_ge(dst_ready, l + 1)

                def one_hots(steps, signal, made):
                    for tt in range(TT):
                        last = d.tensor_scalar(oneh[:, tt, :], iota_f[:, :], dcur[:, 0, tt, :], None, ALU.is_equal)
                    steps(last)
                    for tt in range(TT):
                        last = d.scalar_tensor_tensor(oneh[:, tt, :], iota_f[:, :], dcur[:, 1, tt, :], oneh[:, tt, :],
                                                      ALU.is_equal, ALU.add)
                    last.then_inc(signal, 1)
                    dve.wait_ge(signal, made)
                    steps(d.tensor_scalar(dcur[:, :, :, :], dcur[:, :, :, :], float(2 * SLOTS), None, ALU.subtract))

                d.tensor_copy(pcur[:, :], pcol[:, :])
                st(d.tensor_copy(dcur[:, :, :, :], dst[:, :, :, :]))
                one_hots(st, first_oneh, l + 1)
                st(d.tensor_tensor(cmp8[:, :, :], bc(starts[0:1, NE:2 * NE].unsqueeze(1), [1, EXTRA, NE]),
                                   iot8[:, :].rearrange("p (b e) -> p b e", b=EXTRA), ALU.is_le))
                st(d.tensor_reduce(tabf[:, NE:NE + EXTRA], cmp8[:, :, :], AXX, ALU.add))
                st(d.tensor_scalar(tabf[:, NE:NE + EXTRA], tabf[:, NE:NE + EXTRA], float(NE - 1), None, ALU.min))
                d.tensor_copy(tabf[:, 0:NE], iota_f[0:1, 0:NE])
                d.tensor_copy(tabf[:, 44:45], total[:, :])
                d.tensor_scalar(tabf[:, 41:42], total[:, :], 4.0, None, ALU.mult)
                st(d.tensor_scalar(tabf[:, 40:41], starts[0:1, 2 * NE:2 * NE + 1], 0.0, float(NE // 8), ALU.is_gt, ALU.add))
                d.tensor_scalar(tabf[:, 43:44], tabf[:, 40:41], 4.0, -4.0, ALU.mult, ALU.add)
                st(d.tensor_scalar(tabf[:, 42:43], tabf[:, 40:41], 4.0, None, ALU.mult))
                d.tensor_tensor(total[:, :], total[:, :], tabf[:, 40:41], ALU.add)
                d.tensor_copy(tabi[:, 0:45], tabf[:, 0:45]).then_inc(table_ready, 1)
                dve.wait_ge(rows_ps, 2 * l + 1)
                d.tensor_copy(drow.rearrange("p k t -> p (k t)"), ps[4][:, :]).then_inc(rows_dve, 1)

                def rows_in():
                    d.tensor_copy(xg[:, 0:4, :].rearrange("p k s -> p (k s)"), ps[6][:, :]).then_inc(xg_dve, 1)

                dve.wait_ge(first_gathered, l + 1)
                rows_in()

                dve.wait_ge(table_ready, l + 1)
                dve.sem_inc(dve_held, 1)
                pairs = dve.value_load(tabi[0:1, 42:43], min_val=NE // 2, max_val=(NE + EXTRA) // 2)
                done = dve.value_load(tabi[0:1, 41:42], min_val=0, max_val=DEPTH * (NE + EXTRA) // 2)

                d.memset(wt, 0.0).then_inc(wt_ready, 1)
                d.memset(ym[:, 0:CH], 0.0).then_inc(y_dve, 1)
                d.memset(ym[:, CH:2 * CH], 0.0).then_inc(y_act, 1)
                dve.wait_ge(rows_act, l + 1)
                dve.sem_inc(dve_held, 1)
                with dve.Fori(0, pairs) as i:
                    n = dve.snap(done + i)
                    sp_ = Steps(dve, dve_pair, n * DVE_PAIR_STEPS)
                    one_hots(sp_, oneh_ready, n + 1)
                    dve.wait_ge(combined, n + 1)
                    d.scalar_tensor_tensor(wt, drow[:, 0, :], pcur[:, :], wrow[:, 0, :], ALU.is_equal, ALU.mult)
                    sp_(d.scalar_tensor_tensor(wt_second, drow[:, 1, :], pcur[:, :], wrow[:, 1, :], ALU.is_equal, ALU.mult))
                    d.tensor_tensor(wt, wt, wt_second, ALU.add).then_inc(wt_ready, 1)
                    sp_(d.tensor_scalar(pcur[:, :], pcur[:, :], float(2 * SLOTS), None, ALU.add))
                    dve.wait_ge(up_used, n + 1)
                    dve.wait_ge(silued, n + 1)
                    d.tensor_tensor(hid, sil, ps[5][:, :], ALU.mult).then_inc(h_ready, 1)
                    dve.wait_ge(gathered, 2 * n + 1)
                    rows_in()
                    dve.wait_ge(h_tr, n + 1)
                    d.tensor_copy(hT.rearrange("p k s -> p (k s)"), ps[4][:, :]).then_inc(hT_ready, 1)
                    dve.wait_ge(down_used, n + 1)
                    d.tensor_copy(ym[:, 0:CH], ps[6][:, :]).then_inc(y_dve, 1)
                    assert sp_.n == DVE_PAIR_STEPS, sp_.n
                layer_norm(1, lambda tt, half: dve.wait_ge(acc_done, 2 * l + tt + 1))
                assert st.n == DVE_LAYER_STEPS, st.n

            dve.wait_ge(ln_in, 128 * DEPTH + 64)
            for tt in range(TT):
                dve.wait_ge(normed, 4 * DEPTH + tt + 1)
                d.tensor_tensor(x[:, tt, :], x[:, tt, :], lnp[:, 0, :], ALU.mult).then_inc(scaled, 1)
            dve.wait_ge(scaled, 4 * DEPTH + 2)
            d.tensor_tensor(x[:, 1, :], x[:, 1, :], lnp[:, 1, :], ALU.add).then_inc(x_done[1], 1)

        @block.tensor
        def _(pe):
            t = nc.tensor

            def keep_warm(bank, n, cols=CH, at=0):
                for _ in range(n):
                    t.matmul(ps[bank][:, at:at + cols], identb[:, :], bc(identb[:, 0:1], [P, cols]), start=True, stop=True)

            def transpose_rows(src, ready, n, idle=0):
                for tt in range(TT):
                    if tt == 1:
                        keep_warm(4, idle, P, P)
                    pe.wait_ge(ready, n + tt)
                    for k in range(KT):
                        last = t.transpose(ps[4 + k // 2][:, (k % 2) * SEQ + tt * P:(k % 2) * SEQ + (tt + 1) * P],
                                           src[:, tt, k:D:KT], ident[:, :])
                        if tt == TT - 1 and k % 2:
                            last.then_inc(tr_bank, 1)

            pe.wait_ge(ident_ready, 1)
            keep_warm(0, WARM_START)
            pe.wait_ge(x_in, 16)
            with pe.Fori(0, DEPTH) as l:
                def project(c, part):
                    if part == 0:
                        pe.wait_ge(chunk_in[c], 16 * (l + 1) * (len(COLS[c]) if c < 8 else 1))
                        if 2 <= c < 8:
                            pe.wait_ge(read_dve, 7 * l + DVE_READ[c - 2])
                            pe.wait_ge(read_act, 6 * l + ACT_READ[c - 2])
                    w = slot(SLOT_OF[c])
                    b0 = 2 * (c % 2)
                    if c in (0, 4, 5):
                        j = part
                        for k in range(KT):
                            last = t.matmul(ps[b0 + j // 2][:, (j % 2) * SEQ:(j % 2 + 1) * SEQ],
                                            w[:, k, j * P:(j + 1) * P], xT[:, k, :], start=(k == 0), stop=(k == KT - 1))
                    else:
                        n = sum(b - a for a, b in COLS[c]) if c < 8 else CH
                        src = xT if c < 8 else yT
                        tt = part // 2
                        for k in range((part % 2) * KT // 2, (part % 2 + 1) * KT // 2):
                            last = t.matmul(ps[b0 + tt][:, 0:n], src[:, k, tt * P:(tt + 1) * P], w[:, k, 0:n],
                                            start=(k == 0 and c < 8), stop=(k == KT - 1))
                    if part == 3:
                        last.then_inc(proj, 1)
                    elif part == 1 and c >= 8:
                        last.then_inc(mix_half, 1)

                transpose_rows(x, normed, 4 * l + 1)
                pe.wait_ge(consts_ready, 1)
                pe.wait_ge(tr_dve, 6 * l + 2)
                pe.wait_ge(tr_act, 6 * l + 2)
                def masked(dest, mm):
                    for tt in range(TT):
                        o = dest[:, 0:P] if tt == 0 else dest[:, P:3 * P]
                        mm(tt, o, (tt + 1) * P)
                        last = t.matmul(dest[:, 2 * tt * P:(2 * tt + 1) * P], identb[:, :], maskb[:, :], start=False, stop=True)
                    return last

                def scores(j):
                    h = j % FH
                    q, k = {"fox": (qf[:, h], kf[:, h // 2]), "mlstm": (qkm[:, h], qkm[:, MH + h]),
                            "moba": (qb[:, h], kb[:, h // 2])}[kind(j)]
                    row = h if kind(j) == "fox" else 4 + h
                    if j == 0:
                        pe.wait_ge(cat_ready, l + 1)
                    elif j == FH:
                        pe.wait_ge(qb_ready, l + 1)
                        pe.wait_ge(kb_ready, l + 1)
                    elif j == 2 * FH:
                        pe.wait_ge(silu_done, 2 * l + 2)
                    if j >= 1:
                        if kind(j - 1) == "mlstm":
                            pe.wait_ge(prod_done, MLS * l + mlstm_up_to(j - 1))
                        else:
                            pe.wait_ge(exp_done, SOFT * l + soft_up_to(j - 1))

                    def qk(tt, o, n, stop=False):
                        t.matmul(o, q[:, tt * P:(tt + 1) * P], k[:, 0:n], start=True, stop=stop)

                    def cum(tt, o, n, start=False):
                        t.matmul(o, bc(ident[:, row:row + 1], [P, P]), catT[:, 0:n], start=start, stop=False)

                    if kind(j) == "fox":
                        last = masked(ps[4], lambda tt, o, n: (qk(tt, o, n), cum(tt, o, n)))
                    elif kind(j) == "moba":
                        last = masked(ps[4], qk)
                    else:
                        for tt in range(TT):
                            qk(tt, ps[4][:, 0:P] if tt == 0 else ps[4][:, P:3 * P], (tt + 1) * P, True)
                        last = masked(ps[7], lambda tt, o, n: cum(tt, o, n, True))
                    last.then_inc(scored, 1)

                def attend(it):
                    if it < HEADS:
                        scores(it)
                    if 1 <= it <= HEADS:
                        j, b = it - 1, (it - 1) % 2
                        if kind(j) == "mlstm":
                            pe.wait_ge(prod_done, MLS * l + mlstm_up_to(j))
                        else:
                            pe.wait_ge(exp_done, SOFT * l + soft_up_to(j))
                        if j >= 1:
                            pe.wait_ge(pt_ready, HEADS * l + j)
                        for q in range(3):
                            last = t.transpose(ps[5][:, q * P:(q + 1) * P], Pm[:, b, q * P:(q + 1) * P], ident[:, :])
                        last.then_inc(p_tr, 1)
                    if it >= 2:
                        j, b = it - 2, it % 2
                        w, c = width(j), column(j)
                        pe.wait_ge(pt_ready, HEADS * l + j + 1)
                        if j == 0:
                            pe.wait_ge(read_act, 6 * l + ACT_READ[1])
                        elif j == FH:
                            pe.wait_ge(read_dve, 7 * l + DVE_READ[3])
                            pe.wait_ge(read_act, 6 * l + ACT_READ[3])
                        elif j == 2 * FH:
                            pe.wait_ge(read_dve, 7 * l + DVE_READ[6])
                            pe.wait_ge(read_act, 6 * l + ACT_READ[6])
                        if j >= 1:
                            pe.wait_ge(o_read, HEADS * l + j)
                        t.matmul(ps[6][:, 0:w], PT[:, b, 0:P], v[:, 0, c:c + w], start=True, stop=True)
                        t.matmul(ps[6][:, w:2 * w], PT[:, b, P:2 * P], v[:, 0, c:c + w], start=True, stop=False)
                        t.matmul(ps[6][:, w:2 * w], PT[:, b, 2 * P:3 * P], v[:, 1, c:c + w], start=False,
                                 stop=True).then_inc(pv_done, 1)

                def rope_blocks(o):
                    for c in range(2):
                        for tt in range(TT):
                            last = t.transpose(ps[7][:, c * SEQ + tt * P:c * SEQ + (tt + 1) * P],
                                               bqk[:, tt, o + c * P:o + (c + 1) * P], ident[:, :])
                    last.then_inc(rope_tr, 1)

                for what, n, part in mixer_order():
                    if what == "proj":
                        project(n, part)
                        if (n, part) == (1, 3):
                            pe.wait_ge(par_in, 16 * PAR_DMAS * (l + 1))
                            t.matmul(ps[7][:, 384:384 + CONV * 8], cwr[:, :], ident[0:CONV * 8, 0:CONV * 8],
                                     start=True, stop=True).then_inc(cw_tr, 1)
                    elif what == "att":
                        attend(n)
                    elif what == "cum":
                        pe.wait_ge(ls_ready, l + 1)
                        t.matmul(ps[7][:, 0:8], tri_incl[:, :], ls[:, 0, :], start=True, stop=True)
                        t.matmul(ps[7][:, 8:16], tri_incl[:, :], ls[:, 1, :], start=True, stop=False)
                        t.matmul(ps[7][:, 8:16], bc(ones[:, :], [P, P]), ls[:, 0, :], start=False, stop=True).then_inc(cum_done, 1)
                    elif what == "cat":
                        pe.wait_ge(gpad_ready, l + 1)
                        for tt in range(TT):
                            last = t.transpose(ps[7][:, tt * P:(tt + 1) * P], gpad[:, tt, :], ident[:, :])
                        last.then_inc(cat_tr, 1)
                    elif what == "ropeq":
                        pe.wait_ge(roped, 2 * l + 2)
                        pe.wait_ge(cat_ready, l + 1)
                        rope_blocks(0)
                    elif what == "ropek":
                        pe.wait_ge(qb_ready, l + 1)
                        rope_blocks(2 * P)

                def residual(tt, n):
                    pe.wait_ge(x_done[tt], 2 * l + n)
                    for half in range(2):
                        t.matmul(ps[2 * half + tt][:, :], alpha_i[:, :], x[:, tt, half * CH:(half + 1) * CH],
                                 start=True, stop=False)

                pe.wait_ge(read_dve, 7 * l + DVE_READ[7])
                pe.wait_ge(read_act, 6 * l + ACT_READ[7])
                residual(0, 1)
                residual(1, 1)
                transpose_rows(y, y_ready, 2 * l + 1)
                pe.wait_ge(tr_dve, 6 * l + 4)
                pe.wait_ge(tr_act, 6 * l + 4)
                for c in (8, 9):
                    for part in range(4):
                        project(c, part)
                transpose_rows(x, normed, 4 * l + 3, WARM_NORM)
                keep_warm(3, WARM_COPY)
                pe.wait_ge(tr_dve, 6 * l + 6)
                pe.wait_ge(tr_act, 6 * l + 6)
                for tt in range(TT):
                    for k in range(KT):
                        last = t.matmul(ps[5][:, tt * 64:tt * 64 + NG + NE], xT[:, k, tt * P:(tt + 1) * P], wr[:, k, :],
                                        start=(k == 0), stop=(k == KT - 1))
                last.then_inc(logits, 1)
                residual(0, 2)
                keep_warm(4, WARM_CHOOSE)
                pe.wait_ge(masks_ready, l + 1)
                t.matmul(ps[5][:, 0:NE], tri_strict[:, :], mall[:, 0, :], start=True, stop=True)
                t.matmul(ps[5][:, NE:2 * NE], tri_strict[:, :], mall[:, 1, :], start=True, stop=False)
                t.matmul(ps[5][:, NE:2 * NE], bc(ones[:, :], [P, P]), mall[:, 0, :], start=False, stop=True)
                t.matmul(ps[5][0:NE, 128:256], mall[:, 0, :], bc(ones[:, :], [P, P]), start=True, stop=False)
                t.matmul(ps[5][0:NE, 128:256], mall[:, 1, :], bc(ones[:, :], [P, P]), start=False, stop=True).then_inc(ranks, 1)
                pe.wait_ge(novt_ready, l + 1)
                t.matmul(ps[6][:, 0:2 * NE + 1], novt[:, :], tri65[:, :], start=True, stop=True).then_inc(starts_ps, 1)
                residual(1, 2)
                keep_warm(4, WARM_SLOTS)

                def gather(signal=False):
                    for k in range(KT):
                        for tt in range(TT):
                            last = t.matmul(ps[6 + k // 4][:, (k % 4) * P:(k % 4 + 1) * P], x[:, tt, k:D:KT], oneh[:, tt, :],
                                            start=(tt == 0), stop=(tt == TT - 1))
                        if signal and k % 4 == 3:
                            last.then_inc(gathered, 1)
                    return last

                pe.wait_ge(dst_ready, l + 1)
                for bank, col in ((4, dst), (5, wgt)):
                    for k in range(2):
                        for tt in range(TT):
                            last = t.matmul(ps[bank][:, k * SEQ + tt * P:k * SEQ + (tt + 1) * P], bc(col[:, k, tt, :], [P, P]),
                                            ident[:, :], start=True, stop=True)
                    last.then_inc(rows_ps, 1)
                pe.wait_ge(first_oneh, l + 1)
                gather().then_inc(first_gathered, 1)

                pe.wait_ge(table_ready, l + 1)
                pe.sem_inc(pe_held, 1)
                groups = pe.value_load(tabi[0:1, 40:41], min_val=NE // 8, max_val=(NE + EXTRA) // 8)
                groups_before = pe.value_load(tabi[0:1, 44:45], min_val=0, max_val=DEPTH * (NE + EXTRA) // 8)
                pe.wait_ge(rows_dve, l + 1)
                pe.wait_ge(rows_act, l + 1)
                pe.sem_inc(pe_held, 1)

                def combine(last_pair=False):
                    for tt in range(TT):
                        for half in range(2):
                            last = t.matmul(ps[2 * half + tt][:, :], wt[:, tt * P:(tt + 1) * P], ym[:, half * CH:(half + 1) * CH],
                                            start=False, stop=last_pair)
                        if last_pair:
                            last.then_inc(acc_done, 1)
                    if not last_pair:
                        last.then_inc(combined, 1)

                def arrived(gg, r, part):
                    load = 3 * r + ("gate", "up", "down").index(part)
                    pe.wait_ge(expert_in[unit(r, part)], gg * 96 + 32 * (load // 4 + 1))

                with pe.Fori(0, groups) as g:
                    gg = pe.snap(groups_before + g)
                    for r in range(4):
                        n = pe.snap(4 * gg + r)
                        nl = pe.snap(n + l)
                        pe.wait_ge(xg_dve, nl + 1)
                        pe.wait_ge(xg_act, nl + 1)
                        arrived(gg, r, "gate")
                        for k in range(KT):
                            for q in range(2):
                                last = t.matmul(ps[4][64 * q:64 * q + 64, :], xg[:, k, 64 * q:64 * q + 64], slot(2 * unit(r, "gate") + q)[:, k, :],
                                                start=(k == 0), stop=(k == KT - 1))
                        last.then_inc(gate_used, 1)
                        pe.wait_ge(y_dve, nl + 1)
                        pe.wait_ge(y_act, nl + 1)
                        pe.wait_ge(wt_ready, nl + 1)
                        combine()
                        arrived(gg, r, "up")
                        for k in range(KT):
                            for q in range(2):
                                last = t.matmul(ps[5][64 * q:64 * q + 64, :], xg[:, k, 64 * q:64 * q + 64], slot(2 * unit(r, "up") + q)[:, k, :],
                                                start=(k == 0), stop=(k == KT - 1))
                        last.then_inc(up_used, 1)
                        pe.wait_ge(oneh_ready, n + 1)
                        gather(signal=True)
                        pe.wait_ge(h_ready, n + 1)
                        for f in range(FT):
                            last = t.transpose(ps[4][:, f * P:(f + 1) * P], hid[:, f:DE:FT], ident[:, :])
                        last.then_inc(h_tr, 1)
                        pe.wait_ge(hT_ready, n + 1)
                        pe.wait_ge(xg_dve, nl + 2)
                        pe.wait_ge(xg_act, nl + 2)
                        arrived(gg, r, "down")
                        for f in range(FT):
                            for half in range(2):
                                for q in range(2):
                                    w = ring[:, 2 * unit(r, "down") + q, :].rearrange("p (f n) -> p f n", f=FT)
                                    last = t.matmul(ps[6 + half][64 * q:64 * q + 64, :], hT[:, f, 64 * q:64 * q + 64],
                                                    w[:, f, half * CH:(half + 1) * CH], start=(f == 0), stop=(f == FT - 1))
                        last.then_inc(down_used, 1)
                end = pe.snap(4 * groups_before + 4 * groups)
                pe.wait_ge(y_dve, end + l + 1)
                pe.wait_ge(y_act, end + l + 1)
                pe.wait_ge(wt_ready, end + l + 1)
                combine(True)


_INS = ['x', 'positions', 'w_in', 'b_fox_f', 'b_mlstm_i', 'b_mlstm_f', 'conv_w', 'g_fox', 'g_mlstm', 'g_moba',
        'w_out', 'ln1_g', 'ln1_b', 'w_grp', 'b_grp', 'w_exp_router', 'b_exp_router', 'w_gate', 'w_up', 'w_down',
        'ln2_g', 'ln2_b']


def kernel(**inputs):
    import numpy as _np
    import concourse.bacc as _bacc
    from concourse import mybir as _mybir
    from concourse.bass_utils import run_bass_kernel_spmd as _run

    nc = _bacc.Bacc("TRN2", target_bir_lowering=False, num_devices=1)
    arrays, args = {}, {}
    for name in _INS:
        a = _np.ascontiguousarray(inputs[name])
        arrays[f"in_{name}_dram"] = a
        args[name] = nc.dram_tensor(f"in_{name}_dram", a.shape, _mybir.dt.from_np(a.dtype), kind="ExternalInput").ap()
    out = nc.dram_tensor("out_0_dram", (1, SEQ, D), _mybir.dt.float32, kind="ExternalOutput").ap()
    build(nc, args, out)
    r = _run(nc, [arrays], core_ids=[0])
    return r.results[0]["out_0_dram"]
```
